# Optimizing a Trainium2 kernel written in Bass

```python
import jax, jax.numpy as jnp
from jax import lax
import numpy as np

D_MODEL = 1024
BATCH = 1
SEQ = 1024
DEPTH = 2

GRID_W = 64
CTX_LEN = 256
EPS = 1e-6
NEG_INF = -1e30

HEAD_DIM = 64
N_Q_HEADS = (D_MODEL // 2) // HEAD_DIM
N_KV_HEADS = N_Q_HEADS // 4
Q_GROUP = N_Q_HEADS // N_KV_HEADS
WINDOW = 128
BLOCK = 128
ROPE_BASE = 10000.0
ATT_WIDTH = N_Q_HEADS * HEAD_DIM
KV_WIDTH = N_KV_HEADS * HEAD_DIM
GM_WIDTH = D_MODEL // 2
GM_GROUPS = 8
GM_GROUP_DIM = GM_WIDTH // GM_GROUPS
CHUNK = 128
Q_END = ATT_WIDTH
KV_END = Q_END + 2 * KV_WIDTH
IN_WIDTH = KV_END + 2 * GM_WIDTH
MIX_WIDTH = ATT_WIDTH + GM_WIDTH
POOL_SIZES = (2, 4, 8, 16)
POOL_GROUPS = len(POOL_SIZES)
POOL_GROUP_DIM = D_MODEL // POOL_GROUPS
D_FF_DENSE = 256 * ((8 * D_MODEL // 3 + 255) // 256)
N_EXPERTS = 8
TOP_K = 2
D_FF_EXPERT = 7 * D_MODEL // 2
N_EVEN = (DEPTH + 1) // 2
N_ODD = DEPTH // 2

kernel_name = "hybrid_window_gmlp_pool_moe_dit"

def _rms_normalize(x):
    xf = x.astype(jnp.float32)
    y = xf * lax.rsqrt(jnp.mean(xf * xf, axis=-1, keepdims=True) + EPS)
    return y.astype(x.dtype)

def _modulate(x, shift, scale):
    return _rms_normalize(x) * (1 + scale) + shift

def _axial_rope_tables(n_tokens):
    rows = n_tokens // GRID_W
    row_pos = jnp.repeat(jnp.arange(rows, dtype=jnp.float32), GRID_W)
    col_pos = jnp.tile(jnp.arange(GRID_W, dtype=jnp.float32), rows)
    axis_dim = HEAD_DIM // 2
    inv_freq = ROPE_BASE ** (-jnp.arange(0, axis_dim, 2, dtype=jnp.float32) / axis_dim)
    ang = jnp.stack([row_pos[:, None] * inv_freq, col_pos[:, None] * inv_freq], axis=1)
    return jnp.cos(ang), jnp.sin(ang)

def _apply_axial_rope(t, cos, sin):
    shp = t.shape
    tr = t.reshape(shp[:-1] + (2, 2, HEAD_DIM // 4))
    t1, t2 = tr[..., 0, :], tr[..., 1, :]
    cs = cos[:, None].astype(t.dtype)
    sn = sin[:, None].astype(t.dtype)
    out = jnp.stack([t1 * cs - t2 * sn, t2 * cs + t1 * sn], axis=-2)
    return out.reshape(shp)

def _softmax_with_sink(scores, sink_l):
    m = jnp.maximum(jnp.max(scores, axis=-1, keepdims=True), sink_l)
    p = jnp.exp(scores - m)
    return p / (jnp.sum(p, axis=-1, keepdims=True) + jnp.exp(sink_l - m))

def _window_attention_with_context(q, k, v, kc, vc, sink):
    B, S = q.shape[0], q.shape[1]
    nb = S // BLOCK
    qb = q.reshape(B, nb, BLOCK, N_KV_HEADS, Q_GROUP, HEAD_DIM) * (HEAD_DIM ** -0.5)

    def band(t):
        tp = jnp.pad(t, ((0, 0), (BLOCK, BLOCK), (0, 0), (0, 0)))
        tp = tp.reshape(B, nb + 2, BLOCK, N_KV_HEADS, HEAD_DIM)
        return jnp.concatenate([tp[:, :-2], tp[:, 1:-1], tp[:, 2:]], axis=2)

    kb, vb = band(k), band(v)
    qpos = jnp.arange(nb)[:, None, None] * BLOCK + jnp.arange(BLOCK)[None, :, None]
    kpos = (jnp.arange(nb)[:, None, None] - 1) * BLOCK + jnp.arange(3 * BLOCK)[None, None, :]
    mask = (jnp.abs(kpos - qpos) <= WINDOW) & (kpos >= 0) & (kpos < S)
    s_loc = jnp.einsum('bnqhgd,bnkhd->bnhgqk', qb, kb).astype(jnp.float32)
    s_loc = jnp.where(mask[None, :, None, None], s_loc, NEG_INF)
    s_ctx = jnp.einsum('bnqhgd,bchd->bnhgqc', qb, kc).astype(jnp.float32)
    scores = jnp.concatenate([s_loc, s_ctx], axis=-1)
    sink_l = sink.astype(jnp.float32).reshape(1, 1, N_KV_HEADS, Q_GROUP, 1, 1)
    p = _softmax_with_sink(scores, sink_l).astype(v.dtype)
    out = (jnp.einsum('bnhgqk,bnkhd->bnqhgd', p[..., :3 * BLOCK], vb)
           + jnp.einsum('bnhgqc,bchd->bnqhgd', p[..., 3 * BLOCK:], vc))
    return out.reshape(B, S, ATT_WIDTH)

def _context_attention(qc, kc, vc, sink):
    B, L = qc.shape[0], qc.shape[1]
    qg = qc.reshape(B, L, N_KV_HEADS, Q_GROUP, HEAD_DIM) * (HEAD_DIM ** -0.5)
    s = jnp.einsum('blhgd,bchd->bhglc', qg, kc).astype(jnp.float32)
    sink_l = sink.astype(jnp.float32).reshape(1, N_KV_HEADS, Q_GROUP, 1, 1)
    p = _softmax_with_sink(s, sink_l).astype(vc.dtype)
    return jnp.einsum('bhglc,bchd->blhgd', p, vc).reshape(B, L, ATT_WIDTH)

def _spatial_gating(u, v, gain, w_s, b_s):
    B, S = u.shape[0], u.shape[1]
    v = _rms_normalize(v) * gain
    vg = v.reshape(B, S // CHUNK, CHUNK, GM_GROUPS, GM_GROUP_DIM)
    mixed = jnp.einsum('gts,bnsgd->bntgd', w_s, vg) + b_s.T[:, :, None]
    return u * mixed.reshape(B, S, GM_WIDTH)

def _attn_gmlp_mixer(hx, hc, cos, sin, w_in, sink, gm_gain, w_s, b_s, w_out, with_ctx_out):
    B, S = hx.shape[0], hx.shape[1]
    proj = hx @ w_in
    q = proj[..., :Q_END].reshape(B, S, N_Q_HEADS, HEAD_DIM)
    k = proj[..., Q_END:Q_END + KV_WIDTH].reshape(B, S, N_KV_HEADS, HEAD_DIM)
    v = proj[..., Q_END + KV_WIDTH:KV_END].reshape(B, S, N_KV_HEADS, HEAD_DIM)
    u_gm, v_gm = jnp.split(jax.nn.gelu(proj[..., KV_END:]), 2, axis=-1)
    q = _apply_axial_rope(q, cos, sin)
    k = _apply_axial_rope(k, cos, sin)
    L = hc.shape[1]
    kv_c = hc @ w_in[:, Q_END:KV_END]
    kc = kv_c[..., :KV_WIDTH].reshape(B, L, N_KV_HEADS, HEAD_DIM)
    vc = kv_c[..., KV_WIDTH:].reshape(B, L, N_KV_HEADS, HEAD_DIM)
    att = _window_attention_with_context(q, k, v, kc, vc, sink)
    gm = _spatial_gating(u_gm, v_gm, gm_gain, w_s, b_s)
    out_x = jnp.concatenate([att, gm], axis=-1) @ w_out
    if with_ctx_out:
        qc = (hc @ w_in[:, :Q_END]).reshape(B, L, N_Q_HEADS, HEAD_DIM)
        uc, vgc = jnp.split(jax.nn.gelu(hc @ w_in[:, KV_END:]), 2, axis=-1)
        att_c = _context_attention(qc, kc, vc, sink)
        gm_c = _spatial_gating(uc, vgc, gm_gain, w_s, b_s)
        return out_x, jnp.concatenate([att_c, gm_c], axis=-1) @ w_out
    return out_x, None

def _multiscale_pool(h, w_pool, scale):
    B, S, D = h.shape
    hg = h.reshape(B, S, POOL_GROUPS, POOL_GROUP_DIM)
    t = jnp.arange(S)
    outs = []
    for gi, w in enumerate(POOL_SIZES):
        seg = hg[:, :, gi].astype(jnp.float32)
        cs = jnp.pad(jnp.cumsum(seg, axis=1), ((0, 0), (1, 0), (0, 0)))
        lo = jnp.maximum(t - w // 2, 0)
        hi = jnp.minimum(t + (w - 1 - w // 2), S - 1) + 1
        mean = (cs[:, hi] - cs[:, lo]) / (hi - lo).astype(jnp.float32)[None, :, None]
        outs.append((mean - seg).astype(h.dtype))
    diff = jnp.stack(outs, axis=2)
    y = jnp.einsum('bsgc,gcd->bsgd', diff, w_pool).reshape(B, S, D)
    return y * scale

def _swiglu(h, w_gate, w_up, w_down):
    return (jax.nn.silu(h @ w_gate) * (h @ w_up)) @ w_down

def _moe_swiglu(h, w_router, w_gate, w_up, w_down):
    B, S, D = h.shape
    tok = h.reshape(-1, D)
    n = tok.shape[0]
    logits = (tok @ w_router).astype(jnp.float32)
    top_val, top_idx = lax.top_k(logits, TOP_K)
    weights = jax.nn.softmax(top_val, axis=-1)
    flat_e = top_idx.reshape(-1)
    order = jnp.argsort(flat_e)
    token_of = order // TOP_K
    xs = tok[token_of]
    group_sizes = jnp.bincount(flat_e, length=N_EXPERTS).astype(jnp.int32)
    g = lax.ragged_dot(xs, w_gate, group_sizes)
    u = lax.ragged_dot(xs, w_up, group_sizes)
    y = lax.ragged_dot(jax.nn.silu(g) * u, w_down, group_sizes)
    y = y * weights.reshape(-1)[order][:, None].astype(y.dtype)
    out = jax.ops.segment_sum(y, token_of, num_segments=n)
    return out.reshape(B, S, D)

def setup_inputs(seed: int = 0) -> dict:
    key = jax.random.key(seed)
    ks = jax.random.split(key, 24)
    D = D_MODEL
    f32 = jnp.float32
    nrm = lambda k, shp, s: jax.random.normal(k, shp, f32) * s
    return {
        "x": nrm(ks[0], (BATCH, SEQ, D), 1.0),
        "c": nrm(ks[1], (BATCH, D), 1.0),
        "ctx": nrm(ks[2], (BATCH, CTX_LEN, D), 1.0),
        "c_ctx": nrm(ks[3], (D,), 1.0),
        "w_ada": nrm(ks[4], (DEPTH, D, 6 * D), D ** -0.5),
        "b_ada": nrm(ks[5], (DEPTH, 6 * D), 0.02),
        "w_in": nrm(ks[6], (N_EVEN, D, IN_WIDTH), D ** -0.5),
        "attn_sink": nrm(ks[7], (N_EVEN, N_Q_HEADS), 1.0),
        "gm_gain": 1.0 + nrm(ks[8], (N_EVEN, GM_WIDTH), 0.1),
        "gm_w_s": nrm(ks[9], (N_EVEN, GM_GROUPS, CHUNK, CHUNK), CHUNK ** -0.5),
        "gm_b_s": 1.0 + nrm(ks[10], (N_EVEN, GM_GROUPS, CHUNK), 0.1),
        "w_out": nrm(ks[11], (N_EVEN, MIX_WIDTH, D), MIX_WIDTH ** -0.5),
        "ffn_w_gate": nrm(ks[12], (N_EVEN, D, D_FF_DENSE), D ** -0.5),
        "ffn_w_up": nrm(ks[13], (N_EVEN, D, D_FF_DENSE), D ** -0.5),
        "ffn_w_down": nrm(ks[14], (N_EVEN, D_FF_DENSE, D), D_FF_DENSE ** -0.5),
        "pool_w": nrm(ks[15], (N_ODD, POOL_GROUPS, POOL_GROUP_DIM, POOL_GROUP_DIM), POOL_GROUP_DIM ** -0.5),
        "pool_scale": 1.0 + nrm(ks[16], (N_ODD, D), 0.1),
        "router_w": nrm(ks[17], (N_ODD, D, N_EXPERTS), D ** -0.5),
        "moe_w_gate": nrm(ks[18], (N_ODD, N_EXPERTS, D, D_FF_EXPERT), D ** -0.5),
        "moe_w_up": nrm(ks[19], (N_ODD, N_EXPERTS, D, D_FF_EXPERT), D ** -0.5),
        "moe_w_down": nrm(ks[20], (N_ODD, N_EXPERTS, D_FF_EXPERT, D), D_FF_EXPERT ** -0.5),
        "final_gain": 1.0 + nrm(ks[21], (D,), 0.1),
    }

def reference(x, c, ctx, c_ctx, w_ada, b_ada, w_in, attn_sink, gm_gain, gm_w_s, gm_b_s, w_out,
              ffn_w_gate, ffn_w_up, ffn_w_down, pool_w, pool_scale, router_w,
              moe_w_gate, moe_w_up, moe_w_down, final_gain):
    S = x.shape[1]
    cos, sin = _axial_rope_tables(S)
    s_c = jax.nn.silu(c)
    s_cc = jax.nn.silu(c_ctx)
    for layer in range(DEPTH):
        even = layer % 2 == 0
        i = layer // 2
        advance_ctx = any(j % 2 == 0 for j in range(layer + 1, DEPTH))
        mx = jnp.split((s_c @ w_ada[layer] + b_ada[layer])[:, None, :], 6, axis=-1)
        if even or advance_ctx:
            mc = jnp.split(s_cc @ w_ada[layer] + b_ada[layer], 6)
        if even:
            hx = _modulate(x, mx[0], mx[1])
            hc = _modulate(ctx, mc[0], mc[1])
            yx, yc = _attn_gmlp_mixer(hx, hc, cos, sin, w_in[i], attn_sink[i], gm_gain[i],
                                      gm_w_s[i], gm_b_s[i], w_out[i], advance_ctx)
            x = x + mx[2] * yx
            x = x + mx[5] * _swiglu(_modulate(x, mx[3], mx[4]), ffn_w_gate[i], ffn_w_up[i], ffn_w_down[i])
            if advance_ctx:
                ctx = ctx + mc[2] * yc
                ctx = ctx + mc[5] * _swiglu(_modulate(ctx, mc[3], mc[4]),
                                            ffn_w_gate[i], ffn_w_up[i], ffn_w_down[i])
        else:
            x = x + mx[2] * _multiscale_pool(_modulate(x, mx[0], mx[1]), pool_w[i], pool_scale[i])
            x = x + mx[5] * _moe_swiglu(_modulate(x, mx[3], mx[4]), router_w[i],
                                        moe_w_gate[i], moe_w_up[i], moe_w_down[i])
            if advance_ctx:
                ctx = ctx + mc[2] * _multiscale_pool(_modulate(ctx, mc[0], mc[1]), pool_w[i], pool_scale[i])
                ctx = ctx + mc[5] * _moe_swiglu(_modulate(ctx, mc[3], mc[4]), router_w[i],
                                                moe_w_gate[i], moe_w_up[i], moe_w_down[i])
    return _rms_normalize(x) * final_gain


_drawn_inputs = setup_inputs


def setup_inputs(seed=0):
    import zlib

    import numpy as np

    out = dict(_drawn_inputs(seed))
    spreads = {}
    factors = {'attn_sink': 31.127}
    for name, (base, spread) in spreads.items():
        noise = np.random.default_rng([zlib.crc32(name.encode()), seed]).standard_normal(out[name].shape)
        drawn = base * np.exp(spread * noise) if base else spread * noise
        out[name] = __import__('jax').numpy.asarray(drawn.astype(out[name].dtype))
    for name, factor in factors.items():
        out[name] = (out[name] * factor).astype(out[name].dtype)
    return out
```

```python
from contextlib import ExitStack

import numpy as np

import concourse.bass as bass
from concourse import mybir

P = 128
D = 1024
SEQ = 1024
CTX_LEN = 256
DEPTH = 2
GRID_W = 64
EPS = 1e-6
NEG_INF = -1e30
HEAD = 64
Q_HEADS = D // 2 // HEAD
KV_WIDTH = Q_HEADS // 4 * HEAD
Q_END = Q_HEADS * HEAD
KV_END = Q_END + 2 * KV_WIDTH
GM_GROUPS = 8
WINDOW = 128
POOL_SIZES = (2, 4, 8, 16)
ROPE_BASE = 10000.0
FF_DENSE = 2816
FF_EXPERT = 3584
N_EXPERTS = 8
TOP_K = 2

KD = D // P
TX = SEQ // P
TC = CTX_LEN // P
CHUNK_FF = 256
FB = CHUNK_FF // P
TOKENS = 512
TILES_PASS = TOKENS // P
UNIT = 64
MAX_PASSES = N_EXPERTS + (TOP_K * SEQ - N_EXPERTS) // TOKENS
MAX_PASSES_PAD = 16
SLOT_TILES = MAX_PASSES * TILES_PASS


def constants():
    f = np.float32
    out = {"ident": np.eye(P, dtype=f), "ones": np.ones((P, P), f)}
    axis = HEAD // 2
    inv = (f(ROPE_BASE) ** (-np.arange(0, axis, 2, dtype=f) / f(axis))).astype(f)
    t = np.arange(SEQ)
    angle = np.stack([(t // GRID_W).astype(f)[:, None] * inv, (t % GRID_W).astype(f)[:, None] * inv], 1)
    cos, sin = np.cos(angle).astype(f), np.sin(angle).astype(f)
    out["cos"] = np.stack([cos, cos], 2).reshape(SEQ, HEAD)
    out["sin"] = np.stack([-sin, sin], 2).reshape(SEQ, HEAD)
    q, k = np.arange(P)[:, None], np.arange(-P, 2 * P)[None, :]
    out["mask"] = np.where(abs(k - q) <= WINDOW, 0.0, NEG_INF).astype(f)
    reach = max(POOL_SIZES) // 2
    full = np.zeros((len(POOL_SIZES), SEQ, SEQ), f)
    for g, w in enumerate(POOL_SIZES):
        for i in range(SEQ):
            lo, hi = max(i - w // 2, 0), min(i + (w - 1 - w // 2), SEQ - 1) + 1
            full[g, lo:hi, i] = f(1.0) / f(hi - lo)
            full[g, i, i] -= f(1.0)
    tile = [slice(i * P, (i + 1) * P) for i in range(TX)]
    out["band"] = np.stack([full[:, tile[i], tile[i]] for i in (0, 1, TX - 1)], 1)
    out["edge"] = np.stack([full[:, tile[0], P:P + reach], full[:, tile[1], P - reach:P]], 1)
    out["before"] = np.triu(np.ones((P, P), f), 1)
    out["count_up"] = np.arange(MAX_PASSES_PAD, dtype=f)
    out["unit_starts"] = (np.arange(TOKENS // UNIT) * UNIT).astype(f)
    out["tokens"] = (np.arange(TX)[None, :] * P + np.arange(P)[:, None]).astype(np.int32)
    return {name: np.ascontiguousarray(a) for name, a in out.items()}


def phase_semaphores(nc, ctx, phase):
    used = []

    def clear():
        nc.clear_and_free_semaphores(used)
        nc.all_engine_barrier(sem_only=True)

    def sem(name):
        used.append(nc.alloc_semaphore(f"{phase}_{name}"))
        return used[-1]

    ctx.callback(clear)
    return sem


def modulation_phase(nc, mod, dram, keep):
    F, R = mybir.dt.float32, mybir.dt.float32r
    ACT, ALU = mybir.ActivationFunctionType, mybir.AluOpType
    ctx = ExitStack()
    with ctx:
        def sb(n, s, d=F):
            return ctx.enter_context(nc.sbuf_tensor(f"mod_{n}", s, d))

        def ps(n, s):
            bank = ctx.enter_context(nc.psum_tensor(f"mod_{n}_ps", [P, 512], F))
            if len(s) == 3:
                return bank[:, 0:s[1] * s[2]].rearrange("p (a b) -> p a b", a=s[1])
            return bank[:, 0:s[1]]

        sem = phase_semaphores(nc, ctx, "mod")

        WBUF = 2
        w_sb = [sb(f"w{i}", [P, KD, 512]) for i in range(WBUF)]
        b_sb = [sb(f"b{i}", [P, 512]) for i in range(WBUF)]
        x_sb = sb("x", [P, TX + TC, D])
        c_col = sb("c", [P, 2, KD])
        c_silu = sb("c_silu", [P, 2, KD])
        lhs_x = sb("lhs_x", [P, KD, P])
        lhs_mixed = sb("lhs_mixed", [P, KD, P])
        wide = [sb(f"wide{i}", [P, 512]) for i in range(2)]
        square = sb("square", [P, D])
        sums = sb("sums", [P, TX + TC])
        mean = sb("mean", [P, TX + TC])
        root = sb("root", [P, TX + TC])
        rstd = sb("rstd", [P, TX + TC])
        x_full = sb("x_full", [P, 2, TOKENS])
        wide_ps = [ps(f"wide{i}", [P, 512]) for i in range(2)]
        col_ps = [ps(f"col{i}", [P, 4, 2]) for i in range(2)]
        turn_ps = [ps(f"turn{i}", [P, TOKENS]) for i in range(3)]

        small_ld, x_ld, row_st = sem("small_ld"), [sem(f"x_ld{i}") for i in range(3)], [sem(f"row_st{i}") for i in range(2)]
        w_ld = [sem(f"w_ld{i}") for i in range(WBUF)]
        silu, lhs, wide_mm, wide_out, col_mm, col_out = (
            sem(n) for n in ("silu", "lhs", "wide_mm", "wide_out", "col_mm", "col_out"))
        squared, rooted, dchain, normed = sem("squared"), sem("rooted"), sem("dchain"), sem("normed")
        turned, whole, rounded, split = sem("turned"), sem("whole"), sem("rounded"), sem("split")

        CHUNKS = [(layer, c) for layer in range(DEPTH) for c in range(6 * D // 512)]
        EARLY = 4
        GROUPS = [(0, 4, 0), (4, 4, 0), (TX, TC, 2)]

        def wants_columns(layer, c):
            vec = c // 2
            return vec != 2 and (layer == 0 or vec > 2)

        def column_targets(layer, c):
            vec, half = c // 2, (c % 2) * 4
            if layer == 0 and vec < 2:
                return [(float(vec == 1), 0, keep["attn_cols"][:, 1 - vec, half:half + 4]),
                        (float(vec == 1), 1, keep["attn_cols"][:, 3 - vec, half:half + 4])]
            cols = keep["ffn_cols"] if layer == 0 else keep["moe_cols"]
            slot = {3: 1, 4: 0, 5: 2}[vec]
            return [(float(vec == 4), 0, cols[:, slot, half:half + 4])]

        column_chunks = [n for n, ch in enumerate(CHUNKS) if wants_columns(*ch)]
        row_chunks = [n for n, (layer, c) in enumerate(CHUNKS) if layer == 1 and c < 6]
        block = ctx.enter_context(nc.Block())

        @block.sync
        def _(sp):
            sp.dma_start(c_col[:, 0, :], mod["c"].rearrange("a (k p) -> p (a k)", p=P)).then_inc(small_ld, 16)
            sp.dma_start(c_col[:, 1, :], mod["c_ctx"].rearrange("(k p) -> p k", p=P)).then_inc(small_ld, 16)
            sp.dma_start(keep["ident"][:, :], dram["ident"]).then_inc(small_ld, 16)
            for n, (layer, c) in enumerate(CHUNKS):
                if n >= WBUF:
                    sp.wait_ge(wide_out, n - WBUF + 1)
                s = slice(c * 512, (c + 1) * 512)
                sp.dma_start(w_sb[n % WBUF][:, :, :], mod["w_ada"][layer, :, s].rearrange("(k p) f -> p k f", p=P))\
                  .then_inc(w_ld[n % WBUF], 16)
                sp.dma_start(b_sb[n % WBUF][:, :], mod["b_ada"][layer, s].partition_broadcast(P)).then_inc(w_ld[n % WBUF], 16)

        @block.gpsimd
        def _(pool):
            x_tiles = mod["x"].rearrange("a (t p) d -> p (a t) d", p=P)
            pool.dma_start(x_sb[:, 0:4, :], x_tiles[:, 0:4, :]).then_inc(x_ld[0], 16)
            pool.dma_start(x_sb[:, 4:TX, :], x_tiles[:, 4:TX, :]).then_inc(x_ld[1], 16)
            pool.dma_start(x_sb[:, TX:TX + TC, :], mod["ctx"].rearrange("a (t p) d -> p (a t) d", p=P)).then_inc(x_ld[2], 16)
            for i, n in enumerate(row_chunks):
                pool.wait_ge(wide_out, n + 1)
                c = CHUNKS[n][1]
                pool.dma_start(dram["pool_mod"][c // 2:c // 2 + 1, (c % 2) * 512:(c % 2 + 1) * 512], wide[n % 2][0:1, :])\
                    .then_inc(row_st[n % 2], 16)
            for i in range(2):
                pool.wait_ge(row_st[i], 16 * len([n for n in row_chunks if n % 2 == i]))

        @block.tensor
        def _(pe):
            def products(n):
                layer, c = CHUNKS[n]
                pe.wait_ge(w_ld[n % WBUF], 32 * (n // WBUF + 1))
                if n == 0:
                    pe.wait_ge(lhs, 2)
                if n >= 2:
                    pe.wait_ge(wide_out, n - 1)
                stationary = lhs_mixed if layer == 0 and c < 4 else lhs_x
                for k in range(KD):
                    last = pe.matmul(wide_ps[n % 2][:, :], stationary[:, k, :], w_sb[n % WBUF][:, k, :],
                                     start=(k == 0), stop=(k == KD - 1))
                last.then_inc(wide_mm, 1)

            def columns(n):
                if n not in column_chunks:
                    return
                i = column_chunks.index(n)
                pe.wait_ge(wide_out, n + 1)
                if i >= 2:
                    pe.wait_ge(col_out, i - 1)
                for j in range(4):
                    last = pe.matmul(col_ps[i % 2][:, j, :], wide[n % 2][:, j * P:(j + 1) * P],
                                     keep["ident"][:, 0:65:64], start=True, stop=True)
                last.then_inc(col_mm, 1)

            def turn():
                i = 0
                for g, (first, tiles, _) in enumerate(GROUPS):
                    pe.wait_ge(normed, first + tiles)
                    for k in range(KD):
                        if i >= 3:
                            pe.wait_ge(whole, i - 2)
                        for t in range(tiles):
                            last = pe.transpose(turn_ps[i % 3][:, t * P:(t + 1) * P],
                                                x_sb[:, first + t, k * P:(k + 1) * P], keep["ident"][:, :])
                        last.then_inc(turned, 1)
                        i += 1

            pe.wait_ge(small_ld, 48)
            for n in range(len(CHUNKS)):
                products(n)
                if n >= 1:
                    columns(n - 1)
                if n == EARLY:
                    turn()
            columns(len(CHUNKS) - 1)

        @block.scalar
        def _(act):
            act.wait_ge(small_ld, 48)
            act.activation(c_silu[:, :, :], c_col[:, :, :], ACT.Silu).then_inc(silu, 1)
            for t in range(TX + TC):
                act.wait_ge(x_ld[min(t // 4, 2)], 16)
                if t:
                    act.wait_ge(squared, t)
                act.activation(square[:, :], x_sb[:, t, :], ACT.Square, accum_out=sums[:, t:t + 1]).then_inc(squared, 1)
            act.wait_ge(dchain, 1)
            act.activation(root[:, :], mean[:, :], ACT.Sqrt).then_inc(rooted, 1)
            act.wait_ge(dchain, 2)
            for t in range(TX + TC):
                act.activation(x_sb[:, t, :], x_sb[:, t, :], ACT.Copy, scale=rstd[:, t:t + 1]).then_inc(normed, 1)
            act.wait_ge(col_out, EARLY)
            i = 0
            for first, tiles, col in GROUPS:
                w = tiles * P
                for k in range(KD):
                    act.wait_ge(turned, i + 1)
                    if i >= 2:
                        act.wait_ge(split, i - 1)
                    act.activation(x_full[:, i % 2, 0:w], turn_ps[i % 3][:, 0:w], ACT.Identity,
                                   scale=keep["attn_cols"][:, col, k:k + 1], bias=keep["attn_cols"][:, col + 1, k:k + 1])\
                       .then_inc(whole, 1)
                    act.wait_ge(whole, i + 1)
                    act.activation(keep["x_hi"][:, k, first * P:first * P + w], x_full[:, i % 2, 0:w], ACT.Copy)\
                       .then_inc(rounded, 1)
                    i += 1

        @block.vector
        def _(dve):
            dve.wait_ge(silu, 1)
            dve.tensor_copy(lhs_x[:, :, :], c_silu[:, 0, :].unsqueeze(2).to_broadcast([P, KD, P])).then_inc(lhs, 1)
            dve.tensor_copy(lhs_mixed[:, :, 0:P // 2], c_silu[:, 0, :].unsqueeze(2).to_broadcast([P, KD, P // 2]))
            dve.tensor_copy(lhs_mixed[:, :, P // 2:P], c_silu[:, 1, :].unsqueeze(2).to_broadcast([P, KD, P // 2]))\
               .then_inc(lhs, 1)

            def sums_of(n):
                layer, c = CHUNKS[n]
                dve.wait_ge(wide_mm, n + 1)
                if n >= 2:
                    done = len([m for m in column_chunks if m <= n - 2])
                    if done:
                        dve.wait_ge(col_mm, done)
                    done = len([m for m in row_chunks if m <= n - 2 and m % 2 == n % 2])
                    if done:
                        dve.wait_ge(row_st[n % 2], 16 * done)
                target = keep["gate0"][:, (c % 2) * 512:(c % 2 + 1) * 512] if layer == 0 and c // 2 == 2 else wide[n % 2][:, :]
                dve.tensor_tensor(target, wide_ps[n % 2][:, :], b_sb[n % WBUF][:, :], ALU.add).then_inc(wide_out, 1)

            def columns_of(n):
                if n not in column_chunks:
                    return
                i = column_chunks.index(n)
                dve.wait_ge(col_mm, i + 1)
                targets = column_targets(*CHUNKS[n])
                for j, (added, source, target) in enumerate(targets):
                    last = dve.tensor_scalar(target, col_ps[i % 2][:, :, source], added, None, ALU.add)
                last.then_inc(col_out, 1)

            def chunk(n):
                sums_of(n)
                if n >= 1:
                    columns_of(n - 1)

            chunk(0)
            dve.wait_ge(squared, TX + TC)
            dve.tensor_scalar(mean[:, :], sums[:, :], 1.0 / D, EPS, ALU.mult, ALU.add).then_inc(dchain, 1)
            dve.wait_ge(rooted, 1)
            dve.reciprocal(rstd[:, :], root[:, :]).then_inc(dchain, 1)
            for n in range(1, EARLY + 1):
                chunk(n)
            i = 0
            for first, tiles, _ in GROUPS:
                for k in range(KD):
                    dve.wait_ge(rounded, i + 1)
                    here = slice(first * P, (first + tiles) * P)
                    dve.tensor_tensor(keep["x_lo"][:, k, here], x_full[:, i % 2, 0:tiles * P],
                                      keep["x_hi"][:, k, here].bitcast(F), ALU.subtract).then_inc(split, 1)
                    i += 1
            for n in range(EARLY + 1, len(CHUNKS)):
                chunk(n)
            columns_of(len(CHUNKS) - 1)


def projection_phase(nc, w_in, dram, keep):
    F, R = mybir.dt.float32, mybir.dt.float32r
    ACT, ALU = mybir.ActivationFunctionType, mybir.AluOpType
    ctx = ExitStack()
    with ctx:
        def sb(n, s, d=F):
            return ctx.enter_context(nc.sbuf_tensor(f"proj_{n}", s, d))

        def ps(n, s):
            bank = ctx.enter_context(nc.psum_tensor(f"proj_{n}_ps", [P, 512], F))
            if len(s) == 3:
                return bank[:, 0:s[1] * s[2]].rearrange("p (a b) -> p a b", a=s[1])
            return bank[:, 0:s[1]]

        sem = phase_semaphores(nc, ctx, "proj")

        W = 256
        raw = [sb(f"raw{i}", [P, KD, W]) for i in range(2)]
        w_hi = [sb(f"w_hi{i}", [P, KD, W], R) for i in range(2)]
        w_lo = [sb(f"w_lo{i}", [P, KD, W], R) for i in range(2)]
        cos = sb("cos", [P, TX, HEAD])
        sin = sb("sin", [P, TX, HEAD])
        with_cos = sb("with_cos", [P, W])
        with_sin = sb("with_sin", [P, W])
        roped = [sb(f"roped{i}", [P, W]) for i in range(2)]
        square = sb("square", [P, W])
        out_ps = [ps(f"out{i}", [P, W]) for i in range(4)]
        turn_ps = [ps(f"turn{i}", [P, 2, P]) for i in range(2)]

        tab_ld, raw_ld = sem("tab_ld"), [sem(f"raw_ld{i}") for i in range(2)]
        rounded, split, mm, turned, turned_out, ready, chain, squared = (
            sem(n) for n in ("rounded", "split", "mm", "turned", "turned_out", "ready", "chain", "squared"))
        left = {"dve": sem("left_dve"), "act": sem("left_act")}

        PIECES = ["q0", "q1", "kv", "u0", "u1", "v0", "v1"]
        UNITS = [(i, t) for i, piece in enumerate(PIECES) for t in range(TX + TC if piece == "kv" else TX)]
        who = ["act" if PIECES[i][0] in "uv" else "dve" for i, _ in UNITS]
        nth = [who[:u + 1].count(who[u]) for u in range(len(UNITS))]
        turns = [u for u, w in enumerate(who) if w == "dve"]
        last_unit = [max(u for u, (j, _) in enumerate(UNITS) if j == i) for i in range(len(PIECES))]
        block = ctx.enter_context(nc.Block())

        @block.sync
        def _(sp):
            sp.dma_start(cos[:, :, :], dram["cos"].rearrange("(t p) f -> p t f", p=P)).then_inc(tab_ld, 16)
            sp.dma_start(sin[:, :, :], dram["sin"].rearrange("(t p) f -> p t f", p=P)).then_inc(tab_ld, 16)
            rows = w_in.rearrange("a (k p) f -> p (a k) f", p=P)
            for i, piece in enumerate(PIECES):
                if i >= 2:
                    sp.wait_ge(split, i - 1)
                to, done = raw[i % 2], raw_ld[i % 2]
                if piece[0] == "q":
                    a = int(piece[1])
                    for side in range(2):
                        for j in range(2):
                            h = side * Q_HEADS // 2 + 2 * a + j
                            at = (2 * j + side) * HEAD
                            sp.dma_start(to[:, :, at:at + HEAD], rows[:, :, h * HEAD:(h + 1) * HEAD]).then_inc(done, 16)
                else:
                    at = {"kv": Q_END, "u0": KV_END, "u1": KV_END + W, "v0": KV_END + 2 * W, "v1": KV_END + 3 * W}[piece]
                    sp.dma_start(to[:, :, :], rows[:, :, at:at + W]).then_inc(done, 16)

        def loads(i):
            return 16 * sum(4 if PIECES[j][0] == "q" else 1 for j in range(i % 2, i + 1, 2))

        @block.tensor
        def _(pe):
            def turn(u):
                if who[u] == "act":
                    return
                i = turns.index(u)
                pe.wait_ge(ready, i + 1)
                if i >= 2:
                    pe.wait_ge(turned_out, i - 1)
                for j in range(2 if PIECES[UNITS[u][0]][0] == "q" else 1):
                    last = pe.transpose(turn_ps[i % 2][:, j, :], roped[i % 2][:, j * P:(j + 1) * P], keep["ident"][:, :])
                last.then_inc(turned, 1)

            for u, (i, t) in enumerate(UNITS):
                pe.wait_ge(split, i + 1)
                if u >= 4:
                    pe.wait_ge(left[who[u - 4]], nth[u - 4])
                bank = out_ps[u % 4]
                here = slice(t * P, (t + 1) * P)
                for k in range(KD):
                    wh, wl = w_hi[i % 2][:, k, :], w_lo[i % 2][:, k, :]
                    pe.matmul(bank[:, :], keep["x_hi"][:, k, here], wh, start=(k == 0), stop=False)
                    pe.matmul(bank[:, :], keep["x_hi"][:, k, here], wl, start=False, stop=False)
                    last = pe.matmul(bank[:, :], keep["x_lo"][:, k, here], wh, start=False, stop=(k == KD - 1))
                last.then_inc(mm, 1)
                if u >= 1:
                    turn(u - 1)
            turn(len(UNITS) - 1)

        @block.scalar
        def _(act):
            def round_piece(i):
                act.wait_ge(raw_ld[i % 2], loads(i))
                if i >= 2:
                    act.wait_ge(mm, last_unit[i - 2] + 1)
                act.activation(w_hi[i % 2][:, :, :], raw[i % 2][:, :, :], ACT.Copy).then_inc(rounded, 1)

            def copy_turned(u):
                i = turns.index(u)
                piece, t = PIECES[UNITS[u][0]], UNITS[u][1]
                act.wait_ge(turned, i + 1)
                if piece[0] == "q":
                    to = keep["q_t"][:, 2 * int(piece[1]):2 * int(piece[1]) + 2, t * P:(t + 1) * P]
                    act.activation(to, turn_ps[i % 2][:, :, :], ACT.Copy, scale=float(HEAD) ** -0.5).then_inc(turned_out, 1)
                else:
                    act.activation(keep["k_t"][:, t * P:(t + 1) * P], turn_ps[i % 2][:, 0, :], ACT.Copy).then_inc(turned_out, 1)

            round_piece(0)
            gelus = 0
            for u, (i, t) in enumerate(UNITS):
                if t == 1 and i + 1 < len(PIECES):
                    round_piece(i + 1)
                if u >= 2 and who[u - 2] == "dve":
                    copy_turned(u - 2)
                if who[u] == "act":
                    act.wait_ge(mm, u + 1)
                    half = int(PIECES[i][1])
                    to = (keep["u"] if PIECES[i][0] == "u" else keep["v_gm"])[:, t, half * W:(half + 1) * W]
                    act.activation(to, out_ps[u % 4][:, :], ACT.Gelu_apprx_tanh).then_inc(left["act"], 1)
                    if PIECES[i][0] == "v":
                        act.wait_ge(left["act"], nth[u])
                        if gelus:
                            act.wait_ge(squared, gelus)
                        gelus += 1
                        act.activation(square[:, :], to, ACT.Square, accum_out=keep["v_sums"][:, t, half:half + 1])\
                           .then_inc(squared, 1)

        @block.vector
        def _(dve):
            chain_n = [0]

            def link(ins):
                chain_n[0] += 1
                ins.then_inc(chain, 1)
                dve.wait_ge(chain, chain_n[0])

            def rest(i):
                dve.wait_ge(rounded, i + 1)
                dve.tensor_tensor(w_lo[i % 2][:, :, :], raw[i % 2][:, :, :], w_hi[i % 2][:, :, :].bitcast(F), ALU.subtract)\
                   .then_inc(split, 1)

            def rotate(u, t, heads, to):
                n = heads * HEAD
                bank = out_ps[u % 4]
                dve.tensor_tensor(with_cos[:, 0:n].rearrange("p (h f) -> p h f", h=heads),
                                  bank[:, 0:n].rearrange("p (h f) -> p h f", h=heads),
                                  cos[:, t:t + 1, :].to_broadcast([P, heads, HEAD]), ALU.mult)
                halves = "p (h a s f) -> p h a s f"
                for s in range(2):
                    o = with_sin[:, 0:n].rearrange(halves, h=heads, a=2, s=2)[:, :, :, s, :]
                    x = bank[:, 0:n].rearrange(halves, h=heads, a=2, s=2)[:, :, :, 1 - s, :]
                    y = sin[:, t:t + 1, :].rearrange("p o (a s f) -> p o a s f", a=2, s=2)[:, :, :, s, :]
                    last = dve.tensor_tensor(o, x, y.to_broadcast([P, heads, 2, HEAD // 4]), ALU.mult)
                link(last)
                return dve.tensor_tensor(to, with_cos[:, 0:n], with_sin[:, 0:n], ALU.add)

            rest(0)
            dve.wait_ge(tab_ld, 32)
            for u, (i, t) in enumerate(UNITS):
                if t == 1 and i + 1 < len(PIECES):
                    rest(i + 1)
                if who[u] != "dve":
                    continue
                n = turns.index(u)
                dve.wait_ge(mm, u + 1)
                if n:
                    dve.wait_ge(ready, n)
                if n >= 2:
                    dve.wait_ge(turned, n - 1)
                to = roped[n % 2]
                if PIECES[i] != "kv":
                    rotate(u, t, 4, to[:, :]).then_inc(ready, 1)
                    dve.wait_ge(ready, n + 1)
                    dve.sem_inc(left["dve"], 1)
                    continue
                if t < TX:
                    rotate(u, t, 2, to[:, 0:P]).then_inc(ready, 1)
                else:
                    dve.tensor_copy(to[:, 0:P], out_ps[u % 4][:, 0:P]).then_inc(ready, 1)
                dve.tensor_copy(keep["v"][:, t, :], out_ps[u % 4][:, P:2 * P]).then_inc(left["dve"], 1)

        @block.gpsimd
        def _(pool):
            pool.wait_ge(turned_out, len(turns))


def attention_phase(nc, sink, dram, keep):
    F = mybir.dt.float32
    ACT, ALU, AX = mybir.ActivationFunctionType, mybir.AluOpType, mybir.AxisListType
    ctx = ExitStack()
    with ctx:
        def sb(n, s, d=F):
            return ctx.enter_context(nc.sbuf_tensor(f"att_{n}", s, d))

        def ps(n, s):
            bank = ctx.enter_context(nc.psum_tensor(f"att_{n}_ps", [P, 512], F))
            if len(s) == 3:
                return bank[:, 0:s[1] * s[2]].rearrange("p (a b) -> p a b", a=s[1])
            return bank[:, 0:s[1]]

        sem = phase_semaphores(nc, ctx, "att")

        CTX = TC * P
        mask = sb("mask", [P, 3 * P])
        zeros = sb("zeros", [P, D])
        zeroed, cleared = sem("zeroed"), sem("cleared")
        sinks = sb("sinks", [P, Q_HEADS])
        top = sb("top", [P, Q_HEADS, 2])
        top1 = sb("top1", [P, Q_HEADS])
        minus = [sb(f"minus{i}", [P, Q_HEADS]) for i in range(2)]
        sink_less = sb("sink_less", [P, Q_HEADS])
        sink_exp = sb("sink_exp", [P, Q_HEADS])
        sums = [sb(f"sums{i}", [P, Q_HEADS, 2]) for i in range(2)]
        total = sb("total", [P, Q_HEADS])
        total2 = sb("total2", [P, Q_HEADS])
        inverse = sb("inverse", [P, Q_HEADS])
        masked = [sb(f"masked{i}", [P, 3 * P]) for i in range(2)]
        prob = [sb(f"prob{i}", [P, 3 * P + CTX]) for i in range(2)]
        prob_t = [sb(f"prob_t{i}", [P, 3 * P + CTX]) for i in range(2)]
        near_ps = [ps(f"near{i}", [P, 512]) for i in range(2)]
        far_ps = [ps(f"far{i}", [P, 512]) for i in range(2)]
        near_t, far_t = ps("near_t", [P, 512]), ps("far_t", [P, 512])
        out_ps = [ps(f"out{i}", [P, 512]) for i in range(2)]

        ld, scored, masked_ok, far_top, chain, minus_ok, near_exp, far_exp = (
            sem(n) for n in ("ld", "scored", "masked", "far_top", "chain", "minus", "near_exp", "far_exp"))
        near_turned, far_turned, near_copied, far_copied, valued, sink_ok, sink_done, written = (
            sem(n) for n in ("near_t", "far_t", "near_c", "far_c", "valued", "sink_ok", "sink_done", "written"))

        STEPS = [(n, h) for n in range(TX) for h in range(Q_HEADS)]

        def band(n):
            first, last = max(0, n - 1) * P, min(TX, n + 2) * P
            return first, last, first - (n - 1) * P

        def place(h):
            side = h // (Q_HEADS // 2)
            return slice(side * HEAD, (side + 1) * HEAD), h % (Q_HEADS // 2)

        block = ctx.enter_context(nc.Block())

        @block.sync
        def _(sp):
            sp.dma_start(mask[:, :], dram["mask"]).then_inc(ld, 16)
            sp.dma_start(sinks[:, :], sink[0, :].partition_broadcast(P)).then_inc(ld, 16)
            sp.wait_ge(zeroed, 1)
            sp.dma_start(dram["y"].rearrange("(c p) d -> p c d", p=P),
                         zeros[:, :].unsqueeze(1).to_broadcast([P, SLOT_TILES, D])).then_inc(cleared, 16)
            sp.wait_ge(cleared, 16)

        @block.gpsimd
        def _(pool):
            pool.memset(zeros[:, :], 0.0).then_inc(zeroed, 1)

        @block.tensor
        def _(pe):
            def score(s):
                n, h = STEPS[s]
                first, last, _ = band(n)
                rows, pair = place(h)
                if s >= 2:
                    pe.wait_ge(masked_ok, s - 1)
                    pe.wait_ge(far_exp, s - 1)
                q = keep["q_t"][rows, pair, n * P:(n + 1) * P]
                pe.matmul(near_ps[s % 2][:, 0:last - first], q, keep["k_t"][rows, first:last], start=True, stop=True)
                pe.matmul(far_ps[s % 2][:, 0:CTX], q, keep["k_t"][rows, TX * P:TX * P + CTX], start=True, stop=True)\
                  .then_inc(scored, 1)

            def turn(s):
                n, h = STEPS[s]
                first, last, _ = band(n)
                keys = last - first
                pe.wait_ge(near_exp, s + 1)
                if s:
                    pe.wait_ge(near_copied, s)
                for j in range(keys // P):
                    x = pe.transpose(near_t[:, j * P:(j + 1) * P], prob[s % 2][:, j * P:(j + 1) * P], keep["ident"][:, :])
                x.then_inc(near_turned, 1)
                pe.wait_ge(far_exp, s + 1)
                if s:
                    pe.wait_ge(far_copied, s)
                for j in range(TC):
                    x = pe.transpose(far_t[:, j * P:(j + 1) * P], prob[s % 2][:, (3 + j) * P:(4 + j) * P], keep["ident"][:, :])
                x.then_inc(far_turned, 1)

            def value(s):
                n, h = STEPS[s]
                first, last, _ = band(n)
                side = h // (Q_HEADS // 2)
                cols = slice(side * HEAD, (side + 1) * HEAD)
                if h == 0 and n >= 2:
                    pe.wait_ge(written, n - 1)
                pe.wait_ge(near_copied, s + 1)
                pe.wait_ge(far_copied, s + 1)
                tiles = [(j, first // P + j) for j in range((last - first) // P)] + [(3 + j, TX + j) for j in range(TC)]
                for m, (at, tile) in enumerate(tiles):
                    x = pe.matmul(out_ps[n % 2][:, h * HEAD:(h + 1) * HEAD], prob_t[s % 2][:, at * P:(at + 1) * P],
                                  keep["v"][:, tile, cols], start=(m == 0), stop=(m == len(tiles) - 1))
                x.then_inc(valued, 1)

            S = len(STEPS)
            for s in range(S + 2):
                if s < S:
                    score(s)
                if 1 <= s <= S:
                    turn(s - 1)
                if s >= 2:
                    value(s - 2)

        @block.vector
        def _(dve):
            chain_n = [0]

            def link(ins):
                chain_n[0] += 1
                ins.then_inc(chain, 1)
                dve.wait_ge(chain, chain_n[0])

            def maxima(s):
                n, h = STEPS[s]
                first, last, at = band(n)
                keys = last - first
                dve.wait_ge(scored, s + 1)
                if s >= 2:
                    dve.wait_ge(near_exp, s - 1)
                dve.tensor_tensor(masked[s % 2][:, 0:keys], near_ps[s % 2][:, 0:keys], mask[:, at:at + keys], ALU.add)\
                   .then_inc(masked_ok, 1)
                dve.reduce_max(top[:, h, 1:2], far_ps[s % 2][:, 0:CTX], AX.X)
                dve.wait_ge(masked_ok, s + 1)
                link(dve.reduce_max(top[:, h, 0:1], masked[s % 2][:, 0:keys], AX.X))
                link(dve.tensor_tensor(top1[:, h:h + 1], top[:, h, 0:1], top[:, h, 1:2], ALU.max))
                if h == 0 and n >= 2:
                    dve.wait_ge(sink_done, n - 1)
                dve.tensor_scalar(minus[n % 2][:, h:h + 1], top1[:, h:h + 1], sinks[:, h:h + 1], -1.0, ALU.max, ALU.mult)\
                   .then_inc(minus_ok, 1)

            def copy_near(s):
                n, h = STEPS[s]
                first, last, _ = band(n)
                dve.wait_ge(near_turned, s + 1)
                if s >= 2:
                    dve.wait_ge(valued, s - 1)
                dve.tensor_copy(prob_t[s % 2][:, 0:last - first], near_t[:, 0:last - first]).then_inc(near_copied, 1)

            def finish(n):
                b = n % 2
                dve.wait_ge(minus_ok, (n + 1) * Q_HEADS)
                dve.tensor_tensor(sink_less[:, :], sinks[:, :], minus[b][:, :], ALU.add).then_inc(sink_ok, 1)
                dve.wait_ge(far_exp, (n + 1) * Q_HEADS)
                link(dve.tensor_tensor(total[:, :], sums[b][:, :, 0], sums[b][:, :, 1], ALU.add))
                dve.wait_ge(sink_done, n + 1)
                link(dve.tensor_tensor(total2[:, :], total[:, :], sink_exp[:, :], ALU.add))
                link(dve.reciprocal(inverse[:, :], total2[:, :]))
                dve.wait_ge(valued, (n + 1) * Q_HEADS)
                dve.tensor_tensor(keep["att"][:, n, :].rearrange("p (h d) -> p h d", h=Q_HEADS),
                                  out_ps[b][:, :].rearrange("p (h d) -> p h d", h=Q_HEADS),
                                  inverse[:, :].unsqueeze(2).to_broadcast([P, Q_HEADS, HEAD]), ALU.mult).then_inc(written, 1)

            dve.wait_ge(ld, 32)
            S = len(STEPS)
            for s in range(S + 4):
                if s < S:
                    maxima(s)
                if 1 <= s <= S:
                    copy_near(s - 1)
                if s >= 4 and STEPS[s - 4][1] == Q_HEADS - 1:
                    finish(STEPS[s - 4][0])

        @block.scalar
        def _(act):
            def exps(s):
                n, h = STEPS[s]
                first, last, _ = band(n)
                keys = last - first
                act.wait_ge(minus_ok, s + 1)
                if s >= 2:
                    act.wait_ge(far_turned, s - 1)
                if h == 0 and n >= 2:
                    act.wait_ge(written, n - 1)
                act.activation(prob[s % 2][:, 0:keys], masked[s % 2][:, 0:keys], ACT.Exp, bias=minus[n % 2][:, h:h + 1],
                               accum_out=sums[n % 2][:, h, 0:1]).then_inc(near_exp, 1)
                act.activation(prob[s % 2][:, 3 * P:3 * P + CTX], far_ps[s % 2][:, 0:CTX], ACT.Exp,
                               bias=minus[n % 2][:, h:h + 1], accum_out=sums[n % 2][:, h, 1:2]).then_inc(far_exp, 1)

            def copy_far(s):
                act.wait_ge(far_turned, s + 1)
                if s >= 2:
                    act.wait_ge(valued, s - 1)
                act.activation(prob_t[s % 2][:, 3 * P:3 * P + CTX], far_t[:, 0:CTX], ACT.Copy).then_inc(far_copied, 1)

            S = len(STEPS)
            for s in range(S + 4):
                if s < S:
                    exps(s)
                if 1 <= s <= S:
                    copy_far(s - 1)
                if s >= 4 and STEPS[s - 4][1] == Q_HEADS - 1:
                    act.wait_ge(sink_ok, STEPS[s - 4][0] + 1)
                    act.activation(sink_exp[:, :], sink_less[:, :], ACT.Exp).then_inc(sink_done, 1)


def mixer_output_phase(nc, gm, dram, keep):
    F, R = mybir.dt.float32, mybir.dt.float32r
    ACT, ALU = mybir.ActivationFunctionType, mybir.AluOpType
    ctx = ExitStack()
    with ctx:
        def sb(n, s, d=F):
            return ctx.enter_context(nc.sbuf_tensor(f"mix_{n}", s, d))

        def ps(n, s):
            bank = ctx.enter_context(nc.psum_tensor(f"mix_{n}_ps", [P, 512], F))
            if len(s) == 3:
                return bank[:, 0:s[1] * s[2]].rearrange("p (a b) -> p a b", a=s[1])
            return bank[:, 0:s[1]]

        sem = phase_semaphores(nc, ctx, "mix")

        GM = D // 2
        w_s = sb("w_s", [P, GM_GROUPS, P])
        w_s_t = sb("w_s_t", [P, GM_GROUPS, P])
        bias = sb("bias", [P, GM_GROUPS])
        gain = sb("gain", [P, GM])
        mean, root, rstd = sb("mean", [P, TX]), sb("root", [P, TX]), sb("rstd", [P, TX])
        v_sum = sb("v_sum", [P, TX])
        biased = sb("biased", [P, GM])
        raw = [sb(f"raw{i}", [P, 2, D]) for i in range(2)]
        w_hi, w_lo = sb("w_hi", [P, KD, D], R), sb("w_lo", [P, KD, D], R)
        cat_hi = [sb(f"cat_hi{i}", [P, KD, P], R) for i in range(2)]
        cat_lo = [sb(f"cat_lo{i}", [P, KD, P], R) for i in range(2)]
        x_in = [sb(f"x_in{i}", [P, D]) for i in range(2)]
        gated = sb("gated", [P, D])
        x_new = [sb(f"x_new{i}", [P, D]) for i in range(2)]
        x_norm = [sb(f"x_norm{i}", [P, D]) for i in range(2)]
        square = sb("square", [P, D])
        ssum, smean, sroot, srstd = (sb(n, [P, TX]) for n in ("ssum", "smean", "sroot", "srstd"))
        gm_ps = ps("gm", [P, GM])
        turn_ps = [ps(f"turn{i}", [P, 4, P]) for i in range(2)]
        y_ps = [ps(f"y{i}", [P, 512]) for i in range(4)]

        ld, raw_ld, x_ld = sem("ld"), [sem(f"raw_ld{i}") for i in range(2)], [sem(f"x_ld{i}") for i in range(2)]
        w_turned, w_copied, rounded, split, chain, rooted, v_ok, mixed, gm_ok = (
            sem(n) for n in ("w_turned", "w_copied", "rounded", "split", "chain", "rooted", "v_ok", "mixed", "gm_ok"))
        turned, cat_rounded, cat_split, y_mm, y_read, x_ok, squared, s_mean, s_root, s_rstd, x_normed = (
            sem(n) for n in ("turned", "cat_rounded", "cat_split", "y_mm", "y_read", "x_ok", "squared", "s_mean", "s_root",
                             "s_rstd", "x_normed"))
        x_st = [sem(f"x_st{i}") for i in range(2)]
        mean_ok = sem("mean_ok")
        rstd_ok = sem("rstd_ok")
        block = ctx.enter_context(nc.Block())
        KB = 2
        BLOCKS = KD // KB
        x_tiles = gm["x"].rearrange("a (t p) d -> (a t) p d", p=P)

        @block.sync
        def _(sp):
            sp.dma_start(w_s[:, :, :], gm["w_s"].rearrange("a g t s -> t (a g) s")).then_inc(ld, 16)
            sp.dma_start(bias[:, :], gm["b_s"].rearrange("a g t -> t (a g)")).then_inc(ld, 16)
            sp.dma_start(gain[:, :], gm["gain"][0, :].partition_broadcast(P)).then_inc(ld, 16)
            rows = gm["w_out"].rearrange("a (k p) f -> p (a k) f", p=P)
            for b in range(BLOCKS):
                if b >= 2:
                    sp.wait_ge(split, b - 1)
                sp.dma_start(raw[b % 2][:, :, :], rows[:, b * KB:(b + 1) * KB, :]).then_inc(raw_ld[b % 2], 16)
            for t in range(TX):
                if t >= 2:
                    sp.wait_ge(x_ok, t - 1)
                sp.dma_start(x_in[t % 2][:, :], x_tiles[t]).then_inc(x_ld[t % 2], 16)

        @block.gpsimd
        def _(pool):
            for t in range(TX):
                pool.wait_ge(x_normed, t + 1)
                pool.dma_start(dram["x1"][t * P:(t + 1) * P, :], x_new[t % 2][:, :]).then_inc(x_st[t % 2], 16)
                pool.dma_start(dram["xn"][t * P:(t + 1) * P, :], x_norm[t % 2][:, :]).then_inc(x_st[t % 2], 16)
            for i in range(2):
                pool.wait_ge(x_st[i], 32 * (TX // 2))

        @block.tensor
        def _(pe):
            pe.wait_ge(ld, 48)
            for g in range(GM_GROUPS):
                x = pe.transpose(turn_ps[g // 4][:, g % 4, :], w_s[:, g, :], keep["ident"][:, :])
                if g % 4 == 3:
                    x.then_inc(w_turned, 1)
            pe.wait_ge(w_copied, 2)

            def gate(t):
                pe.wait_ge(v_ok, t + 1)
                if t:
                    pe.wait_ge(mixed, 2 * t)
                for g in range(GM_GROUPS):
                    x = pe.matmul(gm_ps[:, g * HEAD:(g + 1) * HEAD], w_s_t[:, g, :],
                                  keep["v_gm"][:, t, g * HEAD:(g + 1) * HEAD], start=True, stop=True)
                x.then_inc(mixed, 1)

            def turn(t):
                for half in range(2):
                    i = 2 * t + half
                    if half:
                        pe.wait_ge(gm_ok, t + 1)
                    if i >= 2:
                        pe.wait_ge(cat_split, i - 1)
                    source = keep["att"] if half == 0 else keep["u"]
                    for j in range(4):
                        x = pe.transpose(turn_ps[half][:, j, :], source[:, t, j * P:(j + 1) * P], keep["ident"][:, :])
                    x.then_inc(turned, 1)

            def project(t):
                pe.wait_ge(cat_split, 2 * t + 2)
                if t == 0:
                    pe.wait_ge(split, BLOCKS)
                if t >= 2:
                    pe.wait_ge(y_read, t - 1)
                for half in range(2):
                    bank = y_ps[2 * (t % 2) + half]
                    cols = slice(half * 512, (half + 1) * 512)
                    for k in range(KD):
                        pe.matmul(bank[:, :], cat_hi[t % 2][:, k, :], w_hi[:, k, cols], start=(k == 0), stop=False)
                        pe.matmul(bank[:, :], cat_hi[t % 2][:, k, :], w_lo[:, k, cols], start=False, stop=False)
                        x = pe.matmul(bank[:, :], cat_lo[t % 2][:, k, :], w_hi[:, k, cols], start=False, stop=(k == KD - 1))
                x.then_inc(y_mm, 1)

            gate(0)
            turn(0)
            for t in range(TX):
                if t + 1 < TX:
                    gate(t + 1)
                    turn(t + 1)
                project(t)

        @block.scalar
        def _(act):
            for i in range(2):
                act.wait_ge(w_turned, i + 1)
                act.activation(w_s_t[:, 4 * i:4 * i + 4, :], turn_ps[i][:, :, :], ACT.Copy).then_inc(w_copied, 1)
            act.wait_ge(mean_ok, 1)
            act.activation(root[:, :], mean[:, :], ACT.Sqrt).then_inc(rooted, 1)
            for b in range(BLOCKS):
                act.wait_ge(raw_ld[b % 2], 16 * (b // 2 + 1))
                act.activation(w_hi[:, b * KB:(b + 1) * KB, :], raw[b % 2][:, :, :], ACT.Copy).then_inc(rounded, 1)

            def round_cat(t):
                for half in range(2):
                    i = 2 * t + half
                    act.wait_ge(turned, i + 1)
                    if t >= 2 and half == 0:
                        act.wait_ge(y_mm, t - 1)
                    act.activation(cat_hi[t % 2][:, 4 * half:4 * half + 4, :], turn_ps[half][:, :, :], ACT.Copy)\
                       .then_inc(cat_rounded, 1)

            def norm(t):
                act.wait_ge(x_ok, t + 1)
                if t:
                    act.wait_ge(squared, t)
                act.activation(square[:, :], x_new[t % 2][:, :], ACT.Square, accum_out=ssum[:, t:t + 1]).then_inc(squared, 1)
                act.wait_ge(s_mean, t + 1)
                act.activation(sroot[:, t:t + 1], smean[:, t:t + 1], ACT.Sqrt).then_inc(s_root, 1)
                act.wait_ge(s_rstd, t + 1)
                if t >= 2:
                    act.wait_ge(x_st[t % 2], 32 * (t // 2))
                act.activation(x_norm[t % 2][:, :], x_new[t % 2][:, :], ACT.Copy, scale=srstd[:, t:t + 1]).then_inc(x_normed, 1)

            round_cat(0)
            for t in range(TX):
                if t + 1 < TX:
                    round_cat(t + 1)
                norm(t)

        @block.vector
        def _(dve):
            chain_n = [0]

            def link(ins):
                chain_n[0] += 1
                ins.then_inc(chain, 1)
                dve.wait_ge(chain, chain_n[0])

            link(dve.tensor_tensor(v_sum[:, :], keep["v_sums"][:, :, 0], keep["v_sums"][:, :, 1], ALU.add))
            dve.tensor_scalar(mean[:, :], v_sum[:, :], 1.0 / GM, EPS, ALU.mult, ALU.add).then_inc(mean_ok, 1)
            dve.wait_ge(rooted, 1)
            dve.reciprocal(rstd[:, :], root[:, :]).then_inc(rstd_ok, 1)
            dve.wait_ge(rstd_ok, 1)
            dve.wait_ge(ld, 48)

            def scale_v(t):
                dve.scalar_tensor_tensor(keep["v_gm"][:, t, :], keep["v_gm"][:, t, :], rstd[:, t:t + 1], gain[:, :],
                                         ALU.mult, ALU.mult).then_inc(v_ok, 1)

            def gate(t):
                dve.wait_ge(mixed, 2 * t + 1)
                if t:
                    dve.wait_ge(gm_ok, t)
                dve.tensor_tensor(biased[:, :].rearrange("p (g d) -> p g d", g=GM_GROUPS),
                                  gm_ps[:, :].rearrange("p (g d) -> p g d", g=GM_GROUPS),
                                  bias[:, :].unsqueeze(2).to_broadcast([P, GM_GROUPS, HEAD]), ALU.add).then_inc(mixed, 1)
                dve.wait_ge(mixed, 2 * t + 2)
                dve.tensor_tensor(keep["u"][:, t, :], biased[:, :], keep["u"][:, t, :], ALU.mult).then_inc(gm_ok, 1)

            def rest_cat(t):
                for half in range(2):
                    dve.wait_ge(cat_rounded, 2 * t + half + 1)
                    dve.tensor_tensor(cat_lo[t % 2][:, 4 * half:4 * half + 4, :], turn_ps[half][:, :, :],
                                      cat_hi[t % 2][:, 4 * half:4 * half + 4, :].bitcast(F), ALU.subtract).then_inc(cat_split, 1)

            def add(t):
                dve.wait_ge(y_mm, t + 1)
                if t:
                    dve.wait_ge(x_ok, t)
                for half in range(2):
                    x = dve.tensor_tensor(gated[:, half * 512:(half + 1) * 512], y_ps[2 * (t % 2) + half][:, :],
                                          keep["gate0"][:, half * 512:(half + 1) * 512], ALU.mult)
                x.then_inc(y_read, 1)
                dve.wait_ge(y_read, t + 1)
                dve.wait_ge(x_ld[t % 2], 16 * (t // 2 + 1))
                if t >= 2:
                    dve.wait_ge(x_st[t % 2], 32 * (t // 2))
                    dve.wait_ge(x_normed, t - 1)
                dve.tensor_tensor(x_new[t % 2][:, :], gated[:, :], x_in[t % 2][:, :], ALU.add).then_inc(x_ok, 1)

            def norm(t):
                dve.wait_ge(squared, t + 1)
                dve.tensor_scalar(smean[:, t:t + 1], ssum[:, t:t + 1], 1.0 / D, EPS, ALU.mult, ALU.add).then_inc(s_mean, 1)
                dve.wait_ge(s_root, t + 1)
                dve.reciprocal(srstd[:, t:t + 1], sroot[:, t:t + 1]).then_inc(s_rstd, 1)

            scale_v(0)
            gate(0)
            scale_v(1)
            for b in range(BLOCKS):
                dve.wait_ge(rounded, b + 1)
                dve.tensor_tensor(w_lo[:, b * KB:(b + 1) * KB, :], raw[b % 2][:, :, :],
                                  w_hi[:, b * KB:(b + 1) * KB, :].bitcast(F), ALU.subtract).then_inc(split, 1)
            rest_cat(0)
            for t in range(TX):
                if t + 1 < TX:
                    gate(t + 1)
                    if t + 2 < TX:
                        scale_v(t + 2)
                    rest_cat(t + 1)
                add(t)
                norm(t)


def pool_phase(nc, pool_w, pool_scale, dram):
    F = mybir.dt.float32
    ACT, ALU = mybir.ActivationFunctionType, mybir.AluOpType
    ctx = ExitStack()
    with ctx:
        def sb(n, s, d=F):
            return ctx.enter_context(nc.sbuf_tensor(f"pool_{n}", s, d))

        def ps(n, s):
            bank = ctx.enter_context(nc.psum_tensor(f"pool_{n}_ps", [P, 512], F))
            if len(s) == 3:
                return bank[:, 0:s[1] * s[2]].rearrange("p (a b) -> p a b", a=s[1])
            return bank[:, 0:s[1]]

        sem = phase_semaphores(nc, ctx, "pool")

        G = len(POOL_SIZES)
        GD = D // G
        REACH = max(POOL_SIZES) // 2
        band = sb("band", [P, G, 3, P])
        edge = sb("edge", [P, G, 2, REACH])
        weights = sb("weights", [P, G, GD // P, GD])
        shift, scale, gate, scales = (sb(n, [P, D]) for n in ("shift", "scale", "gate", "scales"))
        y_in = [sb(f"y_in{i}", [P, D]) for i in range(2)]
        x = sb("x", [P, TX, D])
        h = sb("h", [P, TX, D])
        scaled = sb("scaled", [P, D])
        square = sb("square", [P, D])
        diff = [sb(f"diff{i}", [P, KD, P]) for i in range(2)]
        gated = sb("gated", [P, D])
        x_norm = [sb(f"x_norm{i}", [P, D]) for i in range(2)]
        sums, mean, root, rstd = (sb(n, [P, 2 * TX]) for n in ("sums", "mean", "root", "rstd"))
        diff_ps = [ps(f"diff{i}", [P, 4, P]) for i in range(4)]
        y_ps = [ps(f"y{i}", [P, 512]) for i in range(4)]

        ld, x_ld, y_ld, x_st = sem("ld"), sem("x_ld"), [sem(f"y_ld{i}") for i in range(2)], [sem(f"x_st{i}") for i in range(2)]
        chain, x_sum, squared, rooted, ready, scaled_ok, h_ok = (
            sem(n) for n in ("chain", "x_sum", "squared", "rooted", "ready", "scaled_ok", "h_ok"))
        mean_ok, diffed, copied, y_mm, y_read, x_ok, normed = (
            sem(n) for n in ("mean_ok", "diffed", "copied", "y_mm", "y_read", "x_ok", "normed"))
        block = ctx.enter_context(nc.Block())

        @block.sync
        def _(sp):
            sp.dma_start(x[:, :, :], dram["x1"].rearrange("(t p) d -> p t d", p=P)).then_inc(x_ld, 16)
            for t in range(TX):
                if t >= 2:
                    sp.wait_ge(x_sum, t - 1)
                sp.dma_start(y_in[t % 2][:, :], dram["y_dense"][t * P:(t + 1) * P, :]).then_inc(y_ld[t % 2], 16)
                if t == 1:
                    for i, to in enumerate((shift, scale, gate)):
                        sp.dma_start(to[:, :], dram["pool_mod"][i, :].partition_broadcast(P)).then_inc(ld, 16)
                    sp.dma_start(scales[:, :], pool_scale[0, :].partition_broadcast(P)).then_inc(ld, 16)
                    sp.dma_start(band[:, :, :, :], dram["band"].rearrange("g e s t -> s g e t")).then_inc(ld, 16)
                    sp.dma_start(edge[:, :, :, :], dram["edge"].rearrange("g e s t -> s g e t")).then_inc(ld, 16)
                    sp.dma_start(weights[:, :, :, :], pool_w.rearrange("a g (c p) d -> p (a g) c d", p=P)).then_inc(ld, 16)

        @block.gpsimd
        def _(pool):
            for t in range(TX):
                pool.wait_ge(normed, t + 1)
                pool.dma_start(dram["x3"][t * P:(t + 1) * P, :], x[:, t, :]).then_inc(x_st[t % 2], 16)
                pool.dma_start(dram["xn"][t * P:(t + 1) * P, :], x_norm[t % 2][:, :]).then_inc(x_st[t % 2], 16)
            for i in range(2):
                pool.wait_ge(x_st[i], 32 * (TX // 2))

        @block.tensor
        def _(pe):
            def difference(t):
                pe.wait_ge(h_ok, min(t + 2, TX))
                if t >= 2:
                    pe.wait_ge(copied, 2 * (t - 1))
                which = 0 if t == 0 else 2 if t == TX - 1 else 1
                for half in range(2):
                    bank = diff_ps[2 * (t % 2) + half]
                    for j in range(4):
                        k = 4 * half + j
                        g = k * P // GD
                        cols = slice(k * P, (k + 1) * P)
                        last = t == TX - 1
                        m = pe.matmul(bank[:, j, :], h[:, t, cols], band[:, g, which, :], start=True, stop=False,
                                      skip_group_check=True)
                        if t:
                            m = pe.matmul(bank[:, j, 0:REACH], h[:, t - 1, cols], edge[:, g, 0, :], start=False, stop=last,
                                          skip_group_check=True)
                        if not last:
                            m = pe.matmul(bank[:, j, P - REACH:P], h[:, t + 1, cols], edge[:, g, 1, :], start=False, stop=True,
                                          skip_group_check=True)
                    m.then_inc(diffed, 1)

            def project(t):
                pe.wait_ge(copied, 2 * t + 2)
                if t >= 2:
                    pe.wait_ge(y_read, t - 1)
                for g in range(G):
                    bank = y_ps[2 * (t % 2) + g * GD // 512]
                    at = g * GD % 512
                    for c in range(GD // P):
                        m = pe.matmul(bank[:, at:at + GD], diff[t % 2][:, g * GD // P + c, :], weights[:, g, c, :],
                                      start=(c == 0), stop=(c == GD // P - 1))
                m.then_inc(y_mm, 1)

            pe.wait_ge(ld, 16 * 7)
            difference(0)
            for t in range(TX):
                if t + 1 < TX:
                    difference(t + 1)
                project(t)

        @block.scalar
        def _(act):
            def sum_squares(i, source):
                if i:
                    act.wait_ge(squared, i)
                act.activation(square[:, :], source, ACT.Square, accum_out=sums[:, i:i + 1]).then_inc(squared, 1)
                act.wait_ge(mean_ok, i + 1)
                act.activation(root[:, i:i + 1], mean[:, i:i + 1], ACT.Sqrt).then_inc(rooted, 1)

            def copy(t):
                for half in range(2):
                    act.wait_ge(diffed, 2 * t + half + 1)
                    if t >= 2:
                        act.wait_ge(y_mm, t - 1)
                    act.activation(diff[t % 2][:, 4 * half:4 * half + 4, :], diff_ps[2 * (t % 2) + half][:, :, :], ACT.Copy)\
                       .then_inc(copied, 1)

            for t in range(TX):
                act.wait_ge(x_sum, t + 1)
                sum_squares(t, x[:, t, :])
            copy(0)
            for t in range(TX):
                if t + 1 < TX:
                    copy(t + 1)
                act.wait_ge(x_ok, t + 1)
                sum_squares(TX + t, x[:, t, :])
                act.wait_ge(ready, TX + t + 1)
                if t >= 2:
                    act.wait_ge(x_st[t % 2], 32 * (t // 2))
                act.activation(x_norm[t % 2][:, :], x[:, t, :], ACT.Copy, scale=rstd[:, TX + t:TX + t + 1]).then_inc(normed, 1)

        @block.vector
        def _(dve):
            chain_n = [0]

            def link(ins):
                chain_n[0] += 1
                ins.then_inc(chain, 1)
                dve.wait_ge(chain, chain_n[0])

            def norm(i):
                dve.wait_ge(squared, i + 1)
                dve.tensor_scalar(mean[:, i:i + 1], sums[:, i:i + 1], 1.0 / D, EPS, ALU.mult, ALU.add).then_inc(mean_ok, 1)
                dve.wait_ge(rooted, i + 1)
                dve.reciprocal(rstd[:, i:i + 1], root[:, i:i + 1]).then_inc(ready, 1)
                dve.wait_ge(ready, i + 1)

            def residual(t):
                dve.wait_ge(y_ld[t % 2], 16 * (t // 2 + 1))
                dve.tensor_tensor(x[:, t, :], x[:, t, :], y_in[t % 2][:, :], ALU.add).then_inc(x_sum, 1)

            def modulate(t):
                norm(t)
                if t:
                    dve.wait_ge(h_ok, t)
                link(dve.scalar_tensor_tensor(scaled[:, :], x[:, t, :], rstd[:, t:t + 1], scale[:, :], ALU.mult, ALU.mult))
                dve.tensor_tensor(h[:, t, :], scaled[:, :], shift[:, :], ALU.add).then_inc(h_ok, 1)

            dve.wait_ge(x_ld, 16)
            residual(0)
            dve.wait_ge(ld, 16 * 7)
            link(dve.tensor_scalar(scale[:, :], scale[:, :], 1.0, None, ALU.add))
            for t in range(TX):
                if t + 1 < TX:
                    residual(t + 1)
                modulate(t)
            for t in range(TX):
                dve.wait_ge(y_mm, t + 1)
                if t:
                    dve.wait_ge(x_ok, t)
                for half in range(2):
                    cols = slice(half * 512, (half + 1) * 512)
                    m = dve.tensor_tensor(gated[:, cols], y_ps[2 * (t % 2) + half][:, :], scales[:, cols], ALU.mult)
                m.then_inc(y_read, 1)
                dve.wait_ge(y_read, t + 1)
                link(dve.tensor_tensor(gated[:, :], gated[:, :], gate[:, :], ALU.mult))
                dve.tensor_tensor(x[:, t, :], x[:, t, :], gated[:, :], ALU.add).then_inc(x_ok, 1)
                norm(TX + t)


def routing_phase(nc, router_w, dram, keep):
    F, I = mybir.dt.float32, mybir.dt.int32
    ACT, ALU, AX = mybir.ActivationFunctionType, mybir.AluOpType, mybir.AxisListType
    ctx = ExitStack()
    with ctx:
        def sb(n, s, d=F):
            return ctx.enter_context(nc.sbuf_tensor(f"route_{n}", s, d))

        def ps(n, s):
            bank = ctx.enter_context(nc.psum_tensor(f"route_{n}_ps", [P, 512], F))
            if len(s) == 3:
                return bank[:, 0:s[1] * s[2]].rearrange("p (a b) -> p a b", a=s[1])
            return bank[:, 0:s[1]]

        sem = phase_semaphores(nc, ctx, "route")

        E = N_EXPERTS
        router = sb("router", [P, KD, E])
        before = sb("before", [P, P])
        ones = sb("ones", [P, P])
        expert_of = sb("expert_of", [P, E])
        pass_of = sb("pass_of", [P, MAX_PASSES_PAD])
        tokens = sb("tokens", [P, TX], I)
        x = sb("x", [P, TX, D])
        h = [sb(f"h{i}", [P, TOKENS]) for i in range(2 * KD)]
        logits = sb("logits", [P, TX, E])
        best = sb("best", [P, TX, E])
        best_at = sb("best_at", [P, TX, E], mybir.dt.uint32)
        best_f = sb("best_f", [P, TX, E])
        chosen = [sb(f"chosen{i}", [P, TX, E]) for i in range(TOP_K)]
        either = sb("either", [P, TX, E])
        ranks = sb("ranks", [P, TX, E])
        totals = sb("totals", [P, TX, E])
        running = sb("running", [P, TX + 1, E])
        small = {n: sb(n, [P, E]) for n in ("over", "passes", "half")}
        ends = sb("ends", [P, E])
        starts = sb("starts", [P, E])
        slots = sb("slots", [P, TX, E])
        picked = sb("picked", [P, TX, E])
        slot_f = sb("slot_f", [P, TOP_K, TX])
        gap = sb("gap", [P, TX])
        gap_exp = sb("gap_exp", [P, TX])
        gap_1 = sb("gap_1", [P, TX])
        M = MAX_PASSES_PAD
        started, ended, here, part, counts = (sb(n, [P, M, E]) for n in ("started", "ended", "here", "part", "counts"))
        count, units, table_f = sb("count", [P, M]), sb("units", [P, M, TOKENS // UNIT]), sb("table_f", [P, 2, M])
        unit_of = sb("unit_of", [P, TOKENS // UNIT])
        zeros = sb("zeros", [P, SLOT_TILES], I)
        turn_ps = [ps(f"turn{i}", [P, TOKENS]) for i in range(3)]
        logit_ps = ps("logit", [P, TX, E])
        rank_ps = ps("rank", [P, TX * E])
        total_ps = ps("total", [P, TX * E])

        ld, x_ld, turned, h_ok, logit_mm, chain, exp_ok, either_ok, ranked, slots_ok, zeroed, cleared, scattered, listed = (
            sem(n) for n in ("ld", "x_ld", "turned", "h_ok", "logit_mm", "chain", "exp_ok", "either_ok", "ranked",
                             "slots_ok", "zeroed", "cleared", "scattered", "listed"))
        gap_ok = sem("gap_ok")
        block = ctx.enter_context(nc.Block())

        @block.sync
        def _(sp):
            sp.dma_start(x[:, :, :], dram["xn"].rearrange("(t p) d -> p t d", p=P)).then_inc(x_ld, 16)
            for to, name in ((before[:, :], "before"), (ones[:, :], "ones"), (tokens[:, :], "tokens")):
                sp.dma_start(to, dram[name]).then_inc(ld, 16)
            sp.dma_start(expert_of[:, :], dram["count_up"][0:E].partition_broadcast(P)).then_inc(ld, 16)
            sp.dma_start(pass_of[:, :], dram["count_up"][0:M].partition_broadcast(P)).then_inc(ld, 16)
            sp.dma_start(unit_of[:, :], dram["unit_starts"].partition_broadcast(P)).then_inc(ld, 16)
            sp.dma_start(router[:, :, :], router_w.rearrange("a (k p) e -> p (a k) e", p=P)).then_inc(ld, 16)
            sp.wait_ge(zeroed, 1)
            sp.dma_start(dram["slot_token"].rearrange("(p c) o -> p (c o)", p=P), zeros[:, :]).then_inc(cleared, 16)
            sp.wait_ge(scattered, 16 * TOP_K * TX)
            sp.dma_start(keep["token_of"][:, :], dram["slot_token"].rearrange("(c p) o -> p (c o)", p=P)).then_inc(listed, 16)
            sp.wait_ge(listed, 16)

        @block.gpsimd
        def _(pool):
            pool.memset(zeros[:, :], 0).then_inc(zeroed, 1)
            pool.wait_ge(ld, 16 * 7)
            pool.wait_ge(cleared, 16)
            pool.wait_ge(slots_ok, 1)
            for i in range(TOP_K):
                for t in range(TX):
                    pool.indirect_dma_start(dram["slot_token"], bass.IndirectOffsetOnAxis(ap=keep["slot"][:, i, t:t + 1], axis=0),
                                            tokens[:, t:t + 1], None).then_inc(scattered, 16)

        @block.tensor
        def _(pe):
            pe.wait_ge(x_ld, 16)
            for g in range(2):
                for k in range(KD):
                    i = g * KD + k
                    if i >= 3:
                        pe.wait_ge(h_ok, i - 2)
                    for t in range(4):
                        m = pe.transpose(turn_ps[i % 3][:, t * P:(t + 1) * P], x[:, 4 * g + t, k * P:(k + 1) * P],
                                         keep["ident"][:, :])
                    m.then_inc(turned, 1)
            pe.wait_ge(ld, 16 * 7)
            pe.wait_ge(h_ok, 2 * KD)
            for t in range(TX):
                for k in range(KD):
                    m = pe.matmul(logit_ps[:, t, :], h[t // 4 * KD + k][:, t % 4 * P:(t % 4 + 1) * P], router[:, k, :],
                                  start=(k == 0), stop=(k == KD - 1))
            m.then_inc(logit_mm, 1)
            pe.wait_ge(either_ok, 1)
            flat = either[:, :, :].rearrange("p t e -> p (t e)")
            pe.matmul(rank_ps[:, :], before[:, :], flat, start=True, stop=True)
            pe.matmul(total_ps[:, :], ones[:, :], flat, start=True, stop=True).then_inc(ranked, 1)

        @block.scalar
        def _(act):
            for i in range(2 * KD):
                k = i % KD
                act.wait_ge(turned, i + 1)
                act.activation(h[i][:, :], turn_ps[i % 3][:, :], ACT.Identity, scale=keep["moe_cols"][:, 0, k:k + 1],
                               bias=keep["moe_cols"][:, 1, k:k + 1]).then_inc(h_ok, 1)
            act.wait_ge(gap_ok, 1)
            act.activation(gap_exp[:, :], gap[:, :], ACT.Exp).then_inc(exp_ok, 1)

        @block.vector
        def _(dve):
            chain_n = [0]

            def link(ins):
                chain_n[0] += 1
                ins.then_inc(chain, 1)
                dve.wait_ge(chain, chain_n[0])

            def over_tiles(ap):
                return ap.unsqueeze(1).to_broadcast([P, TX, E])

            dve.wait_ge(logit_mm, 1)
            dve.wait_ge(ld, 16 * 7)
            link(dve.tensor_copy(logits[:, :, :], logit_ps[:, :, :]))
            for t in range(TX):
                m = dve.max(best[:, t, :], logits[:, t, :])
            link(m)
            for t in range(TX):
                m = dve.max_index(best_at[:, t, :], best[:, t, :], logits[:, t, :])
            link(m)
            link(dve.tensor_copy(best_f[:, :, :], best_at[:, :, :]))
            for i in range(TOP_K):
                m = dve.tensor_tensor(chosen[i][:, :, :], best_f[:, :, i:i + 1].to_broadcast([P, TX, E]),
                                      over_tiles(expert_of[:, :]), ALU.is_equal)
            link(m)
            dve.tensor_tensor(either[:, :, :], chosen[0][:, :, :], chosen[1][:, :, :], ALU.add).then_inc(either_ok, 1)
            dve.tensor_tensor(gap[:, :], best[:, :, 1], best[:, :, 0], ALU.subtract).then_inc(gap_ok, 1)
            dve.wait_ge(exp_ok, 1)
            link(dve.tensor_scalar(gap_1[:, :], gap_exp[:, :], 1.0, None, ALU.add))
            link(dve.reciprocal(keep["weight"][:, 0, :], gap_1[:, :]))
            dve.tensor_tensor(keep["weight"][:, 1, :], gap_exp[:, :], keep["weight"][:, 0, :], ALU.mult)
            dve.wait_ge(ranked, 1)
            dve.tensor_copy(totals[:, :, :].rearrange("p t e -> p (t e)"), total_ps[:, :])
            link(dve.memset(running[:, 0, :], 0.0))
            for t in range(TX):
                link(dve.tensor_tensor(running[:, t + 1, :], running[:, t, :], totals[:, t, :], ALU.add))
            link(dve.tensor_tensor(ranks[:, :, :].rearrange("p t e -> p (t e)"), rank_ps[:, :],
                                   running[:, 0:TX, :].rearrange("p t e -> p (t e)"), ALU.add))
            chose = running[:, TX, :]
            dve.tensor_scalar(small["over"][:, :], chose, float(TOKENS), None, ALU.is_gt)
            link(dve.tensor_scalar(small["half"][:, :], chose, 0.0, None, ALU.is_gt))
            link(dve.tensor_tensor(small["passes"][:, :], small["over"][:, :], small["half"][:, :], ALU.add))
            link(dve.tensor_copy(ends[:, 0:1], small["passes"][:, 0:1]))
            for e in range(1, E):
                link(dve.tensor_tensor(ends[:, e:e + 1], ends[:, e - 1:e], small["passes"][:, e:e + 1], ALU.add))
            link(dve.tensor_tensor(starts[:, :], ends[:, :], small["passes"][:, :], ALU.subtract))
            link(dve.scalar_tensor_tensor(slots[:, :, :], over_tiles(starts[:, :]), float(TOKENS), ranks[:, :, :],
                                          ALU.mult, ALU.add))
            for i in range(TOP_K):
                link(dve.tensor_tensor(picked[:, :, :], slots[:, :, :], chosen[i][:, :, :], ALU.mult))
                link(dve.reduce_sum(slot_f[:, i, :], picked[:, :, :], AX.X))
            dve.tensor_copy(keep["slot"][:, :, :], slot_f[:, :, :]).then_inc(slots_ok, 1)
            by_pass = pass_of[:, :].unsqueeze(2).to_broadcast([P, M, E])

            def by_expert(ap):
                return ap.unsqueeze(1).to_broadcast([P, M, E])

            dve.tensor_tensor(started[:, :, :], by_pass, by_expert(starts[:, :]), ALU.is_ge)
            dve.tensor_tensor(ended[:, :, :], by_pass, by_expert(ends[:, :]), ALU.is_lt)
            link(dve.tensor_tensor(part[:, :, :], by_expert(starts[:, :]), by_pass, ALU.subtract))
            dve.tensor_tensor(here[:, :, :], started[:, :, :], ended[:, :, :], ALU.mult)
            link(dve.scalar_tensor_tensor(counts[:, :, :], part[:, :, :], float(TOKENS), by_expert(chose), ALU.mult, ALU.add))
            link(dve.tensor_tensor(counts[:, :, :], counts[:, :, :], here[:, :, :], ALU.mult))
            dve.reduce_sum(count[:, :], counts[:, :, :], AX.X)
            link(dve.tensor_tensor(part[:, :, :], here[:, :, :], by_expert(expert_of[:, :]), ALU.mult))
            dve.reduce_sum(table_f[:, 0, :], part[:, :, :], AX.X)
            link(dve.tensor_tensor(units[:, :, :], count[:, :].unsqueeze(2).to_broadcast([P, M, TOKENS // UNIT]),
                                   unit_of[:, :].unsqueeze(1).to_broadcast([P, M, TOKENS // UNIT]), ALU.is_gt))
            link(dve.reduce_sum(table_f[:, 1, :], units[:, :, :], AX.X))
            link(dve.tensor_copy(table_f[:, 0, M - 1:M], ends[:, E - 1:E]))
            dve.tensor_copy(keep["table"][:, :, :], table_f[0:1, :, :])


def output_phase(nc, final_gain, dram, keep, out):
    F = mybir.dt.float32
    ACT, ALU = mybir.ActivationFunctionType, mybir.AluOpType
    ctx = ExitStack()
    with ctx:
        def sb(n, s, d=F):
            return ctx.enter_context(nc.sbuf_tensor(f"out_{n}", s, d))

        sem = phase_semaphores(nc, ctx, "out")

        gain = sb("gain", [P, D])
        x = sb("x", [P, TX, D])
        y = sb("y", [P, TX, TOP_K, D])
        square = sb("square", [P, D])
        result = [sb(f"result{i}", [P, D]) for i in range(2)]
        sums, mean, root, rstd = (sb(n, [P, TX]) for n in ("sums", "mean", "root", "rstd"))
        ld, y_ld, x_ok, squared, mean_ok, rooted, ready, done, chain = (
            sem(n) for n in ("ld", "y_ld", "x_ok", "squared", "mean_ok", "rooted", "ready", "done", "chain"))
        y_ld = [sem(f"y_ld{t}") for t in range(TX)]
        stored = [sem(f"stored{i}") for i in range(2)]
        block = ctx.enter_context(nc.Block())

        @block.sync
        def _(sp):
            sp.dma_start(gain[:, :], final_gain.partition_broadcast(P)).then_inc(ld, 16)
            sp.dma_start(x[:, :, :], dram["x3"].rearrange("(t p) d -> p t d", p=P)).then_inc(ld, 16)
            rows = out.rearrange("a (t p) d -> (a t) p d", p=P)
            for t in range(TX):
                sp.wait_ge(done, t + 1)
                sp.dma_start(rows[t], result[t % 2][:, :]).then_inc(stored[t % 2], 16)
            for i in range(2):
                sp.wait_ge(stored[i], 16 * (TX // 2))

        @block.gpsimd
        def _(pool):
            for t in range(TX):
                for i in range(TOP_K):
                    pool.indirect_dma_start(y[:, t, i, :], None, dram["y"],
                                            bass.IndirectOffsetOnAxis(ap=keep["slot"][:, i, t:t + 1], axis=0)).then_inc(y_ld[t], 16)

        @block.scalar
        def _(act):
            for t in range(TX):
                act.wait_ge(x_ok, t + 1)
                if t:
                    act.wait_ge(squared, t)
                act.activation(square[:, :], x[:, t, :], ACT.Square, accum_out=sums[:, t:t + 1]).then_inc(squared, 1)
                act.wait_ge(mean_ok, t + 1)
                act.activation(root[:, t:t + 1], mean[:, t:t + 1], ACT.Sqrt).then_inc(rooted, 1)

        @block.vector
        def _(dve):
            dve.wait_ge(ld, 32)

            def add(t):
                dve.wait_ge(y_ld[t], 16 * TOP_K)
                for i in range(TOP_K):
                    dve.scalar_tensor_tensor(x[:, t, :], y[:, t, i, :], keep["weight"][:, i, t:t + 1], x[:, t, :],
                                             ALU.mult, ALU.add).then_inc(chain if i == 0 else x_ok, 1)
                    if i == 0:
                        dve.wait_ge(chain, t + 1)

            def norm(t):
                dve.wait_ge(squared, t + 1)
                dve.tensor_scalar(mean[:, t:t + 1], sums[:, t:t + 1], 1.0 / D, EPS, ALU.mult, ALU.add).then_inc(mean_ok, 1)
                dve.wait_ge(rooted, t + 1)
                dve.reciprocal(rstd[:, t:t + 1], root[:, t:t + 1]).then_inc(ready, 1)
                dve.wait_ge(ready, t + 1)
                if t >= 2:
                    dve.wait_ge(stored[t % 2], 16 * (t // 2))
                dve.scalar_tensor_tensor(result[t % 2][:, :], x[:, t, :], rstd[:, t:t + 1], gain[:, :], ALU.mult, ALU.mult)\
                   .then_inc(done, 1)

            add(0)
            for t in range(TX):
                if t + 1 < TX:
                    add(t + 1)
                norm(t)


def expert_mlp_phase(nc, name, shape, weights, columns, ident, rows_of, y_rows, pad_rows, table):
    F, R = mybir.dt.float32, mybir.dt.float32r
    ACT, ALU = mybir.ActivationFunctionType, mybir.AluOpType
    passes, C = shape
    gate_w, up_w, down_w = weights
    ctx = ExitStack()
    with ctx:
        def sb(n, s, d=F):
            return ctx.enter_context(nc.sbuf_tensor(f"{name}_{n}", s, d))

        def ps(n):
            return ctx.enter_context(nc.psum_tensor(f"{name}_{n}", [P, TOKENS], F))

        sem = phase_semaphores(nc, ctx, name)

        raw_g = sb("raw_g", [P, KD, CHUNK_FF])
        raw_u = sb("raw_u", [P, KD, CHUNK_FF])
        raw_d = sb("raw_d", [P, FB, D])
        g_hi = [sb(f"g_hi{i}", [P, KD, CHUNK_FF], R) for i in range(2)]
        g_lo = [sb(f"g_lo{i}", [P, KD, CHUNK_FF], R) for i in range(2)]
        u_hi = [sb(f"u_hi{i}", [P, KD, CHUNK_FF], R) for i in range(2)]
        u_lo = [sb(f"u_lo{i}", [P, KD, CHUNK_FF], R) for i in range(2)]
        d_hi = [sb(f"d_hi{i}", [P, FB, D], R) for i in range(2)]
        d_lo = [sb(f"d_lo{i}", [P, FB, D], R) for i in range(2)]
        x_rows = sb("x_rows", [P, TILES_PASS, D])
        x_hi = sb("x_hi", [P, KD, TOKENS], R)
        x_lo = sb("x_lo", [P, KD, TOKENS], R)
        h_full = sb("h_full", [P, FB, TOKENS])
        x_full = h_full
        h_hi = [sb(f"h_hi{i}", [P, FB, TOKENS], R) for i in range(2)]
        h_lo = [sb(f"h_lo{i}", [P, FB, TOKENS], R) for i in range(2)]
        y_t = sb("y_t", [P, KD, TOKENS])
        y_out = sb("y_out", [P, D])
        g_ps = [ps(f"g{f}") for f in range(FB)]
        u_ps = [ps(f"u{f}") for f in range(FB)]
        y_ps = [ps(f"y{i}") for i in range(4)]
        x_ps = [g_ps[0], u_ps[0], g_ps[1], u_ps[1]]

        g_loaded, u_loaded, d_loaded, x_loaded, y_stored, all_stored = (
            sem(n) for n in ("g_ld", "u_ld", "d_ld", "x_ld", "y_st", "all_st"))
        g_rounded, u_rounded, d_rounded = (sem(n) for n in ("g_rnd", "u_rnd", "d_rnd"))
        g_split, u_split, d_split = (sem(n) for n in ("g_spl", "u_spl", "d_spl"))
        x_turned, x_rounded, x_whole, x_split = (sem(n) for n in ("x_t", "x_rnd", "x_wh", "x_spl"))
        g_done, u_done, silu_done, h_whole, h_rounded, h_split = (sem(n) for n in ("g_mm", "u_mm", "silu", "h_wh", "h_rnd", "h_spl"))
        y_done, y_added, y_turned, y_left, y_right = (sem(n) for n in ("y_mm", "y_add", "y_t2", "y_l", "y_r"))
        W0, U0, X0, H0, Y0, A0, T0, O0 = 1, 2 * FB, KD, FB, 2 * KD, 4, KD, TILES_PASS

        block = ctx.enter_context(nc.Block())

        def each_pass(eng, body):
            if table is None:
                for p in range(passes):
                    body(p, 0, None)
                return
            with eng.Fori(0, passes) as p:
                units = eng.value_load(table[0:1, 1, bass.ds(p, 1)], min_val=0, max_val=TOKENS // UNIT)
                with eng.If(units > 0):
                    expert = eng.value_load(table[0:1, 0, bass.ds(p, 1)], min_val=0, max_val=gate_w.shape[0] - 1)
                    body(p, expert, units)
                    eng.nop()

        def each_width(eng, units, body):
            if units is None:
                body(TOKENS)
                return
            for v in range(1, TOKENS // UNIT + 1):
                with eng.If(units == v):
                    body(v * UNIT)
            eng.nop()

        def chunk_pairs(eng, first, last, body):
            with eng.Fori(0, (last - first + 1) // 2) as i:
                body(2 * i + first, first % 2)
                body(2 * i + first + 1, (first + 1) % 2)

        @block.sync
        def _(sp):
            def one_pass(p, expert, _):
                def pick(w, lo_row, rows, lo_col, cols):
                    if table is None:
                        return w[0, bass.ds(lo_row, rows), bass.ds(lo_col, cols)]
                    return w[bass.ds(expert, 1), bass.ds(lo_row, rows), bass.ds(lo_col, cols)].rearrange("a r c -> (a r) c")

                with sp.Fori(0, C) as c:
                    n = p * C + c
                    sp.wait_ge(g_split, n + W0)
                    sp.dma_start(raw_g[:, :, :], pick(gate_w, 0, D, c * CHUNK_FF, CHUNK_FF)
                                 .rearrange("(k p) f -> p k f", p=P)).then_inc(g_loaded, 16)
                    sp.wait_ge(u_split, n + W0)
                    sp.dma_start(raw_u[:, :, :], pick(up_w, 0, D, c * CHUNK_FF, CHUNK_FF)
                                 .rearrange("(k p) f -> p k f", p=P)).then_inc(u_loaded, 16)
                    sp.wait_ge(d_split, n + W0)
                    sp.dma_start(raw_d[:, :, :], pick(down_w, c * CHUNK_FF, CHUNK_FF, 0, D)
                                 .rearrange("(b p) d -> p b d", p=P)).then_inc(d_loaded, 16)

            each_pass(sp, one_pass)

        @block.gpsimd
        def _(pool):
            pool.sem_inc(x_turned, X0)

            def one_pass(p, expert, _):
                pool.wait_ge(x_turned, p * KD + X0)
                for t in range(TILES_PASS):
                    rows_of(pool, p, t, x_rows[:, t, :]).then_inc(x_loaded, 16)

            each_pass(pool, one_pass)

        @block.tensor
        def _(pe):
            pe.sem_inc(u_done, U0)
            pe.sem_inc(y_done, Y0)

            def turn_rows(p, width):
                pe.wait_ge(x_loaded, (p + 1) * TILES_PASS * 16)
                pe.wait_ge(silu_done, p * C * FB + H0)
                pe.wait_ge(h_whole, p * C * FB + H0)
                for k in range(KD):
                    if k >= 4:
                        pe.wait_ge(x_whole, p * KD + k - 3)
                    for t in range(-(-width // P)):
                        last = pe.transpose(x_ps[k % 4][:, t * P:(t + 1) * P], x_rows[:, t, k * P:(k + 1) * P],
                                            ident[:, :])
                    last.then_inc(x_turned, 1)

            def hidden(p, c, par, width, first):
                n = p * C + c
                for f in range(FB):
                    for bank, w_hi, w_lo, split, freed, done in (
                            (g_ps[f], g_hi[par], g_lo[par], g_split, silu_done, g_done),
                            (u_ps[f], u_hi[par], u_lo[par], u_split, h_whole, u_done)):
                        if f == 0:
                            pe.wait_ge(split, n + W0 + 1)
                        if first:
                            if f == 0:
                                pe.wait_ge(x_split, p * KD + (5 if bank is g_ps[0] else 8) + 2)
                        pe.wait_ge(freed, n * FB + f - FB + 1 + H0)
                        for k in range(KD):
                            if first and f == 0 and bank is g_ps[0] and k >= 5:
                                pe.wait_ge(x_split, p * KD + k + 1 + 2)
                            wh, wl = (w[:, k, f * P:(f + 1) * P] for w in (w_hi, w_lo))
                            pe.matmul(bank[:, 0:width], wh, x_hi[:, k, 0:width], start=(k == 0), stop=False)
                            pe.matmul(bank[:, 0:width], wh, x_lo[:, k, 0:width], start=False, stop=False)
                            last = pe.matmul(bank[:, 0:width], wl, x_hi[:, k, 0:width], start=False, stop=(k == KD - 1))
                        last.then_inc(done, 1)

            def down(p, c, par, width):
                n = p * C + c
                pe.wait_ge(y_left, p * TILES_PASS + O0)
                pe.wait_ge(y_right, p * TILES_PASS + O0)
                pe.wait_ge(d_split, n + W0 + 1)
                pe.wait_ge(h_split, (n + 1) * FB + H0)
                for db in range(KD):
                    pe.wait_ge(y_added, n * KD + db - 3 + A0)
                    bank = y_ps[db % 4]
                    for f in range(FB):
                        wh, wl = (w[:, f, db * P:(db + 1) * P] for w in (d_hi[par], d_lo[par]))
                        pe.matmul(bank[:, 0:width], wh, h_hi[par][:, f, 0:width], start=(f == 0), stop=False)
                        pe.matmul(bank[:, 0:width], wh, h_lo[par][:, f, 0:width], start=False, stop=False)
                        last = pe.matmul(bank[:, 0:width], wl, h_hi[par][:, f, 0:width], start=False, stop=(f == FB - 1))
                    last.then_inc(y_done, 1)

            def turn_result(p, width):
                tiles = -(-width // P)
                pe.wait_ge(y_added, (p + 1) * C * KD + A0)
                for t in range(tiles):
                    if t >= 2:
                        pe.wait_ge(y_left, p * TILES_PASS + t - 1 + O0)
                        pe.wait_ge(y_right, p * TILES_PASS + t - 1 + O0)
                    for half in range(2):
                        bank = y_ps[(2 * t + half) % 4]
                        for j in range(4):
                            last = pe.transpose(bank[:, j * P:(j + 1) * P], y_t[:, 4 * half + j, t * P:(t + 1) * P],
                                                ident[:, :])
                        final = t == tiles - 1 and half == 1
                        last.then_inc(y_turned, KD - (2 * tiles - 1) if final else 1)

            def one_pass(p, expert, units):
                def at(width):
                    turn_rows(p, width)
                    hidden(p, 0, 0, width, True)

                    def step(c, par):
                        hidden(p, c, par, width, False)
                        down(p, c - 1, 1 - par, width)

                    odd_end = C % 2 == 0
                    chunk_pairs(pe, 1, C - 2 if odd_end else C - 1, step)
                    if odd_end:
                        step(C - 1, 1)
                    down(p, C - 1, (C - 1) % 2, width)
                    turn_result(p, width)

                each_width(pe, units, at)

            each_pass(pe, one_pass)

        @block.scalar
        def _(act):
            act.sem_inc(silu_done, H0)
            act.sem_inc(y_left, O0)
            act.sem_inc(y_stored, 16)

            def round_up(n, par, raw, hi, loaded, rounded, freed, count):
                act.wait_ge(freed, count)
                act.wait_ge(loaded, (n + 1) * 16)
                act.activation(hi[par][:, :, :], raw[:, :, :], ACT.Copy).then_inc(rounded, 1)

            def round_g(p, c, par):
                n = p * C + c
                round_up(n, par, raw_g, g_hi, g_loaded, g_rounded, u_done, (n - 1) * FB + U0)

            def round_u(p, c, par):
                n = p * C + c
                round_up(n, par, raw_u, u_hi, u_loaded, u_rounded, u_done, (n - 1) * FB + U0)

            def round_d(p, c, par):
                n = p * C + c
                round_up(n, par, raw_d, d_hi, d_loaded, d_rounded, y_done, (n - 1) * KD + Y0)

            def hidden(p, c, par, f, width):
                n = p * C + c
                act.wait_ge(g_done, n * FB + f + 1)
                act.wait_ge(h_split, n * FB + f - FB + 1 + H0)
                act.activation(h_full[:, f, 0:width], g_ps[f][:, 0:width], ACT.Silu).then_inc(silu_done, 1)
                act.wait_ge(h_whole, n * FB + f + 1 + H0)
                act.wait_ge(y_done, (n - 1) * KD + Y0)
                act.activation(h_hi[par][:, f, 0:width], h_full[:, f, 0:width], ACT.Copy).then_inc(h_rounded, 1)

            def one_pass(p, expert, units):
                def at(width):
                    act.wait_ge(u_done, p * C * FB + U0)
                    for k in range(KD):
                        act.wait_ge(x_turned, p * KD + k + 1 + X0)
                        act.wait_ge(x_split, p * KD + k - 1 + 2)
                        act.activation(x_full[:, k % 2, 0:width], x_ps[k % 4][:, 0:width], ACT.Identity,
                                       scale=columns[:, 0, k:k + 1], bias=columns[:, 1, k:k + 1]).then_inc(x_whole, 1)
                        act.wait_ge(x_whole, p * KD + k + 1)
                        act.activation(x_hi[:, k, 0:width], x_full[:, k % 2, 0:width], ACT.Copy).then_inc(x_rounded, 1)

                    def step(c, par):
                        round_g(p, c + 1, 1 - par)
                        hidden(p, c, par, 0, width)
                        round_u(p, c + 1, 1 - par)
                        hidden(p, c, par, 1, width)
                        round_d(p, c + 1, 1 - par)

                    round_g(p, 0, 0)
                    round_u(p, 0, 0)
                    round_d(p, 0, 0)
                    step(0, 0)
                    odd_end = C % 2 == 0
                    chunk_pairs(act, 1, C - 2, step) if odd_end else chunk_pairs(act, 1, C - 3, step)
                    if not odd_end:
                        step(C - 2, 1)
                    for f in range(FB):
                        hidden(p, C - 1, (C - 1) % 2, f, width)
                    tiles = -(-width // P)
                    for t in range(TILES_PASS):
                        if t < tiles:
                            act.wait_ge(y_turned, p * KD + 2 * t + 1 + T0)
                            act.wait_ge(y_stored, (p * TILES_PASS + t + 1) * 16)
                            act.activation(y_out[:, 0:D // 2], y_ps[2 * t % 4][:, :], ACT.Copy)\
                               .then_inc(y_left, TILES_PASS - tiles + 1 if t == tiles - 1 else 1)
                            act.wait_ge(y_left, p * TILES_PASS + t + 1 + O0)
                            act.wait_ge(y_right, p * TILES_PASS + t + 1 + O0)
                            act.dma_start(y_rows(p, t), y_out[:, :]).then_inc(y_stored, 16)
                        else:
                            act.dma_start(pad_rows(p, t), y_out[0:1, 0:16]).then_inc(y_stored, 16)

                each_width(act, units, at)

            each_pass(act, one_pass)
            ran = passes if table is None else act.value_load(table[0:1, 0, 15:16], min_val=1, max_val=passes)
            act.wait_ge(y_stored, (ran * TILES_PASS + 1) * 16)
            act.sem_inc(all_stored, 1)

        @block.vector
        def _(dve):
            if table is not None:
                dve.memset(y_t[:, :, :], 0.0).then_inc(y_added, A0)
                dve.wait_ge(y_added, A0)
            else:
                dve.sem_inc(y_added, A0)
            dve.sem_inc(g_split, W0)
            dve.sem_inc(u_split, W0)
            dve.sem_inc(d_split, W0)
            dve.sem_inc(h_whole, H0)
            dve.sem_inc(h_split, H0)
            dve.sem_inc(x_split, 2)
            dve.sem_inc(y_right, O0)
            dve.sem_inc(y_turned, T0)

            def rest(n, par, raw, hi, lo, rounded, split):
                dve.wait_ge(rounded, n + 1)
                dve.tensor_tensor(lo[par][:, :, :], raw[:, :, :], hi[par][:, :, :].bitcast(F), ALU.subtract).then_inc(split, 1)

            def rest_g(p, c, par):
                rest(p * C + c, par, raw_g, g_hi, g_lo, g_rounded, g_split)

            def rest_u(p, c, par):
                rest(p * C + c, par, raw_u, u_hi, u_lo, u_rounded, u_split)

            def rest_d(p, c, par):
                rest(p * C + c, par, raw_d, d_hi, d_lo, d_rounded, d_split)

            def hidden(p, c, par, f, width):
                n = p * C + c
                dve.wait_ge(silu_done, n * FB + f + 1 + H0)
                dve.wait_ge(u_done, n * FB + f + 1 + U0)
                dve.tensor_tensor(h_full[:, f, 0:width], h_full[:, f, 0:width], u_ps[f][:, 0:width], ALU.mult)\
                   .then_inc(h_whole, 1)
                dve.wait_ge(h_rounded, n * FB + f + 1)
                dve.tensor_tensor(h_lo[par][:, f, 0:width], h_full[:, f, 0:width], h_hi[par][:, f, 0:width].bitcast(F),
                                  ALU.subtract).then_inc(h_split, 1)

            def add(p, c, width, first):
                n = p * C + c
                for db in range(KD):
                    dve.wait_ge(y_done, n * KD + db + 1 + Y0)
                    gate = columns[:, 2, db:db + 1]
                    if first:
                        dve.tensor_scalar(y_t[:, db, 0:width], y_ps[db % 4][:, 0:width], gate, None, ALU.mult)\
                           .then_inc(y_added, 1)
                    else:
                        dve.wait_ge(y_added, (n - 1) * KD + db + 1 + A0)
                        dve.scalar_tensor_tensor(y_t[:, db, 0:width], y_ps[db % 4][:, 0:width], gate,
                                                 y_t[:, db, 0:width], ALU.mult, ALU.add).then_inc(y_added, 1)

            def one_pass(p, expert, units):
                def at(width):
                    dve.wait_ge(u_done, p * C * FB + U0)
                    for k in range(KD):
                        dve.wait_ge(x_rounded, p * KD + k + 1)
                        dve.tensor_tensor(x_lo[:, k, 0:width], x_full[:, k % 2, 0:width], x_hi[:, k, 0:width].bitcast(F),
                                          ALU.subtract).then_inc(x_split, 1)
                    rest_g(p, 0, 0)
                    rest_u(p, 0, 0)
                    rest_d(p, 0, 0)
                    dve.wait_ge(y_turned, p * KD + T0)

                    def step(c, par, first=False, second=False):
                        rest_g(p, c + 1, 1 - par)
                        hidden(p, c, par, 0, width)
                        rest_u(p, c + 1, 1 - par)
                        hidden(p, c, par, 1, width)
                        if not first:
                            add(p, c - 1, width, second)
                        rest_d(p, c + 1, 1 - par)

                    step(0, 0, first=True)
                    step(1, 1, second=True)
                    pairs = (C - 3) // 2
                    with dve.Fori(0, pairs) as i:
                        step(2 * i + 2, 0)
                        step(2 * i + 3, 1)
                    for c in range(2 + 2 * pairs, C - 1):
                        step(c, c % 2)
                    for f in range(FB):
                        hidden(p, C - 1, (C - 1) % 2, f, width)
                    add(p, C - 2, width, False)
                    add(p, C - 1, width, False)
                    tiles = -(-width // P)
                    for t in range(tiles):
                        dve.wait_ge(y_turned, p * KD + 2 * t + 2 + T0)
                        dve.wait_ge(y_stored, (p * TILES_PASS + t + 1) * 16)
                        dve.tensor_copy(y_out[:, D // 2:D], y_ps[(2 * t + 1) % 4][:, :])\
                           .then_inc(y_right, TILES_PASS - tiles + 1 if t == tiles - 1 else 1)

                each_width(dve, units, at)

            each_pass(dve, one_pass)


def backbone(nc, a, tables, out):
    F, R, I = mybir.dt.float32, mybir.dt.float32r, mybir.dt.int32
    dram = dict(tables)
    for name, shape, dtype in (("pool_mod", [3, D], F), ("x1", [SEQ, D], F), ("x3", [SEQ, D], F), ("xn", [SEQ, D], F),
                               ("y_dense", [SEQ, D], F), ("y", [SLOT_TILES * P, D], F), ("slot_token", [SLOT_TILES * P, 1], I)):
        dram[name] = nc.dram_tensor(f"scratch_{name}", shape, dtype).ap()
    outer = ExitStack()
    with outer:
        outer.enter_context(nc.allow_non_contiguous_dma(reason="small vectors and tables, one number to a partition"))

        def sb(stack, n, s, d=F):
            return stack.enter_context(nc.sbuf_tensor(n, s, d))

        keep = {
            "ident": sb(outer, "ident", [P, P]),
            "ffn_cols": sb(outer, "ffn_cols", [P, 3, KD]),
            "moe_cols": sb(outer, "moe_cols", [P, 3, KD]),
            "weight": sb(outer, "weight", [P, TOP_K, TX]),
            "slot": sb(outer, "slot", [P, TOP_K, TX], I),
            "token_of": sb(outer, "token_of", [P, SLOT_TILES], I),
            "token_now": sb(outer, "token_now", [P, TILES_PASS], I),
            "table": sb(outer, "table", [1, 2, MAX_PASSES_PAD], I),
        }
        picked = outer.enter_context(nc.semaphore("picked"))
        gathered = outer.enter_context(nc.semaphore("gathered"))

        right, right_short, left, tokens_side = ExitStack(), ExitStack(), ExitStack(), ExitStack()
        with left:
            keep["attn_cols"] = left.enter_context(nc.sbuf_tensor("attn_cols", [P, 4, KD], F))
            keep["gate0"] = left.enter_context(nc.sbuf_tensor("gate0", [P, D], F))
            with right:
                with tokens_side:
                    for name in ("x_hi", "x_lo"):
                        keep[name] = tokens_side.enter_context(nc.sbuf_tensor(name, [P, KD, SEQ + CTX_LEN], R))
                    modulation_phase(nc, a, dram, keep)
                    for name, shape in (("u", [P, TX, D // 2]), ("v_gm", [P, TX, D // 2]), ("v_sums", [P, TX, 2])):
                        keep[name] = right.enter_context(nc.sbuf_tensor(name, shape, F, side="right"))
                    for name, shape in (("q_t", [P, Q_HEADS // 2, SEQ]), ("k_t", [P, SEQ + CTX_LEN]),
                                        ("v", [P, TX + TC, KV_WIDTH])):
                        keep[name] = right_short.enter_context(nc.sbuf_tensor(name, shape, F, side="right"))
                    projection_phase(nc, a["w_in"], dram, keep)
                keep["att"] = left.enter_context(nc.sbuf_tensor("att", [P, TX, D // 2], F))
                with right_short:
                    attention_phase(nc, a["attn_sink"], dram, keep)
                mixer_output_phase(nc, {"x": a["x"], "w_s": a["gm_w_s"], "b_s": a["gm_b_s"], "gain": a["gm_gain"],
                                        "w_out": a["w_out"]}, dram, keep)

        def tile_rows(y):
            return lambda p, t: y[bass.ds((p * TILES_PASS + t) * P, P), :]

        def spare_numbers(y):
            return lambda p, t: y[bass.ds((p * TILES_PASS + t) * P, 1), 0:16]

        def token_tile(pool, p, t, to):
            return pool.dma_start(to, dram["xn"][(p * TILES_PASS + t) * P:(p * TILES_PASS + t + 1) * P, :])

        expert_mlp_phase(nc, "ffn", (SEQ // TOKENS, FF_DENSE // CHUNK_FF), (a["ffn_w_gate"], a["ffn_w_up"], a["ffn_w_down"]),
                         keep["ffn_cols"], keep["ident"], token_tile, tile_rows(dram["y_dense"]),
                         spare_numbers(dram["y_dense"]), None)
        pool_phase(nc, a["pool_w"], a["pool_scale"], dram)
        routing_phase(nc, a["router_w"], dram, keep)

        def slot_tile(pool, p, t, to):
            pool.tensor_copy(keep["token_now"][:, t:t + 1], keep["token_of"][:, bass.ds(p * TILES_PASS + t, 1)]).then_inc(picked, 1)
            pool.wait_ge(picked, p * TILES_PASS + t + 1)
            pool.sem_inc(gathered, 1)
            return pool.indirect_dma_start(to, None, dram["xn"], bass.IndirectOffsetOnAxis(ap=keep["token_now"][:, t:t + 1], axis=0))

        experts = tuple(w.rearrange("a e r c -> (a e) r c") for w in (a["moe_w_gate"], a["moe_w_up"], a["moe_w_down"]))
        expert_mlp_phase(nc, "moe", (MAX_PASSES, FF_EXPERT // CHUNK_FF), experts, keep["moe_cols"], keep["ident"], slot_tile,
                         tile_rows(dram["y"]), spare_numbers(dram["y"]), keep["table"])
        output_phase(nc, a["final_gain"], dram, keep, out)


_INS = ["x", "c", "ctx", "c_ctx", "w_ada", "b_ada", "w_in", "attn_sink", "gm_gain", "gm_w_s", "gm_b_s", "w_out",
        "ffn_w_gate", "ffn_w_up", "ffn_w_down", "pool_w", "pool_scale", "router_w",
        "moe_w_gate", "moe_w_up", "moe_w_down", "final_gain"]


def kernel(**inputs):
    import concourse.bacc as bacc
    from concourse.bass_utils import run_bass_kernel_spmd

    nc = bacc.Bacc("TRN2", target_bir_lowering=False, num_devices=1, dynamic_dma_scratch_size=8192)
    arrays, aps, tables = {}, {}, {}

    def declare(name, a):
        arrays[name] = a
        return nc.dram_tensor(name, a.shape, mybir.dt.from_np(a.dtype), kind="ExternalInput").ap()

    for name in _INS:
        aps[name] = declare(f"in_{name}", np.ascontiguousarray(inputs[name]))
    for name, table in constants().items():
        tables[name] = declare(f"table_{name}", table)
    out = nc.dram_tensor("out", [1, SEQ, D], mybir.dt.float32, kind="ExternalOutput").ap()
    backbone(nc, aps, tables, out)
    r = run_bass_kernel_spmd(nc, [arrays], core_ids=[0])
    return r.results[0]["out"]
```

```python
from contextlib import ExitStack

import numpy as np

import concourse.bass as bass
from concourse import mybir

P = 128
D = 1024
SEQ = 1024
CTX_LEN = 256
DEPTH = 2
GRID_W = 64
EPS = 1e-6
NEG_INF = -1e30
HEAD = 64
Q_HEADS = D // 2 // HEAD
KV_WIDTH = Q_HEADS // 4 * HEAD
Q_END = Q_HEADS * HEAD
KV_END = Q_END + 2 * KV_WIDTH
GM_GROUPS = 8
WINDOW = 128
POOL_SIZES = (2, 4, 8, 16)
ROPE_BASE = 10000.0
FF_DENSE = 2816
FF_EXPERT = 3584
N_EXPERTS = 8
TOP_K = 2

KD = D // P
TX = SEQ // P
TC = CTX_LEN // P
CHUNK_FF = 256
FB = CHUNK_FF // P
TOKENS = 512
TILES_PASS = TOKENS // P
ROUND = 32
WIDTHS = (128, 160) + tuple(range(256, TOKENS + 1, ROUND))
MAX_PASSES = N_EXPERTS + (TOP_K * SEQ - N_EXPERTS) // TOKENS
MAX_PASSES_PAD = 16
SLOT_TILES = MAX_PASSES * TILES_PASS
LISTED_TILES = SLOT_TILES + TILES_PASS


def constants():
    f = np.float32
    out = {"ident": np.eye(P, dtype=f), "ones": np.ones((P, P), f)}
    axis = HEAD // 2
    inv = (f(ROPE_BASE) ** (-np.arange(0, axis, 2, dtype=f) / f(axis))).astype(f)
    t = np.arange(SEQ)
    angle = np.stack([(t // GRID_W).astype(f)[:, None] * inv, (t % GRID_W).astype(f)[:, None] * inv], 1)
    cos, sin = np.cos(angle).astype(f), np.sin(angle).astype(f)
    out["cos"] = np.stack([cos, cos], 2).reshape(SEQ, HEAD)
    out["sin"] = np.stack([-sin, sin], 2).reshape(SEQ, HEAD)
    q, k = np.arange(P)[:, None], np.arange(-P, 2 * P)[None, :]
    out["mask"] = np.where(abs(k - q) <= WINDOW, 0.0, NEG_INF).astype(f)
    reach = max(POOL_SIZES) // 2
    full = np.zeros((len(POOL_SIZES), SEQ, SEQ), f)
    for g, w in enumerate(POOL_SIZES):
        for i in range(SEQ):
            lo, hi = max(i - w // 2, 0), min(i + (w - 1 - w // 2), SEQ - 1) + 1
            full[g, lo:hi, i] = f(1.0) / f(hi - lo)
            full[g, i, i] -= f(1.0)
    tile = [slice(i * P, (i + 1) * P) for i in range(TX)]
    out["band"] = np.stack([full[:, tile[i], tile[i]] for i in (0, 1, TX - 1)], 1)
    out["edge"] = np.stack([full[:, tile[0], P:P + reach], full[:, tile[1], P - reach:P]], 1)
    out["before"] = np.triu(np.ones((P, P), f), 1)
    out["count_up"] = np.arange(MAX_PASSES_PAD, dtype=f)
    out["width_starts"] = np.array((0,) + WIDTHS[:-1], f)
    out["half_starts"] = (np.arange(TOKENS // ROUND) * 2 * ROUND).astype(f)
    out["tokens"] = (np.arange(TX)[None, :] * P + np.arange(P)[:, None]).astype(np.int32)
    return {name: np.ascontiguousarray(a) for name, a in out.items()}


def phase_semaphores(nc, ctx, phase):
    used = []

    def clear():
        nc.clear_and_free_semaphores(used)
        nc.all_engine_barrier(sem_only=True)

    def sem(name):
        used.append(nc.alloc_semaphore(f"{phase}_{name}"))
        return used[-1]

    ctx.callback(clear)
    return sem


def modulation_phase(nc, mod, dram, keep):
    F, R = mybir.dt.float32, mybir.dt.float32r
    ACT, ALU = mybir.ActivationFunctionType, mybir.AluOpType
    ctx = ExitStack()
    with ctx:
        def sb(n, s, d=F):
            return ctx.enter_context(nc.sbuf_tensor(f"mod_{n}", s, d))

        def ps(n, s):
            bank = ctx.enter_context(nc.psum_tensor(f"mod_{n}_ps", [P, 512], F))
            if len(s) == 3:
                return bank[:, 0:s[1] * s[2]].rearrange("p (a b) -> p a b", a=s[1])
            return bank[:, 0:s[1]]

        sem = phase_semaphores(nc, ctx, "mod")

        WBUF = 2
        w_sb = [sb(f"w{i}", [P, KD, 512]) for i in range(WBUF)]
        b_sb = [sb(f"b{i}", [P, 512]) for i in range(WBUF)]
        x_sb = sb("x", [P, TX + TC, D])
        c_col = sb("c", [P, 2, KD])
        c_silu = sb("c_silu", [P, 2, KD])
        lhs_x = sb("lhs_x", [P, KD, P])
        lhs_mixed = sb("lhs_mixed", [P, KD, P])
        wide = [sb(f"wide{i}", [P, 512]) for i in range(2)]
        square = sb("square", [P, D])
        sums = sb("sums", [P, TX + TC])
        mean = sb("mean", [P, TX + TC])
        root = sb("root", [P, TX + TC])
        rstd = sb("rstd", [P, TX + TC])
        x_full = sb("x_full", [P, 2, TOKENS])
        wide_ps = [ps(f"wide{i}", [P, 512]) for i in range(2)]
        col_ps = [ps(f"col{i}", [P, 4, 2]) for i in range(2)]
        turn_ps = [ps(f"turn{i}", [P, TOKENS]) for i in range(3)]

        small_ld, x_ld, row_st = sem("small_ld"), [sem(f"x_ld{i}") for i in range(3)], [sem(f"row_st{i}") for i in range(2)]
        w_ld = [sem(f"w_ld{i}") for i in range(WBUF)]
        silu, lhs, wide_mm, wide_out, col_mm, col_out = (
            sem(n) for n in ("silu", "lhs", "wide_mm", "wide_out", "col_mm", "col_out"))
        squared, rooted, dchain, normed = sem("squared"), sem("rooted"), sem("dchain"), sem("normed")
        turned, whole, rounded, split = sem("turned"), sem("whole"), sem("rounded"), sem("split")

        CHUNKS = [(layer, c) for layer in range(DEPTH) for c in range(6 * D // 512)]
        EARLY = 4
        GROUPS = [(0, 4, 0), (4, 4, 0), (TX, TC, 2)]

        def wants_columns(layer, c):
            vec = c // 2
            return vec != 2 and (layer == 0 or vec > 2)

        def column_targets(layer, c):
            vec, half = c // 2, (c % 2) * 4
            if layer == 0 and vec < 2:
                return [(float(vec == 1), 0, keep["attn_cols"][:, 1 - vec, half:half + 4]),
                        (float(vec == 1), 1, keep["attn_cols"][:, 3 - vec, half:half + 4])]
            cols = keep["ffn_cols"] if layer == 0 else keep["moe_cols"]
            slot = {3: 1, 4: 0, 5: 2}[vec]
            return [(float(vec == 4), 0, cols[:, slot, half:half + 4])]

        column_chunks = [n for n, ch in enumerate(CHUNKS) if wants_columns(*ch)]
        row_chunks = [n for n, (layer, c) in enumerate(CHUNKS) if layer == 1 and c < 6]
        block = ctx.enter_context(nc.Block())

        @block.sync
        def _(sp):
            sp.dma_start(c_col[:, 0, :], mod["c"].rearrange("a (k p) -> p (a k)", p=P)).then_inc(small_ld, 16)
            sp.dma_start(c_col[:, 1, :], mod["c_ctx"].rearrange("(k p) -> p k", p=P)).then_inc(small_ld, 16)
            sp.dma_start(keep["ident"][:, :], dram["ident"]).then_inc(small_ld, 16)
            for n, (layer, c) in enumerate(CHUNKS):
                if n >= WBUF:
                    sp.wait_ge(wide_out, n - WBUF + 1)
                s = slice(c * 512, (c + 1) * 512)
                sp.dma_start(w_sb[n % WBUF][:, :, :], mod["w_ada"][layer, :, s].rearrange("(k p) f -> p k f", p=P))\
                  .then_inc(w_ld[n % WBUF], 16)
                sp.dma_start(b_sb[n % WBUF][:, :], mod["b_ada"][layer, s].partition_broadcast(P)).then_inc(w_ld[n % WBUF], 16)

        @block.gpsimd
        def _(pool):
            x_tiles = mod["x"].rearrange("a (t p) d -> p (a t) d", p=P)
            pool.dma_start(x_sb[:, 0:4, :], x_tiles[:, 0:4, :]).then_inc(x_ld[0], 16)
            pool.dma_start(x_sb[:, 4:TX, :], x_tiles[:, 4:TX, :]).then_inc(x_ld[1], 16)
            pool.dma_start(x_sb[:, TX:TX + TC, :], mod["ctx"].rearrange("a (t p) d -> p (a t) d", p=P)).then_inc(x_ld[2], 16)
            for i, n in enumerate(row_chunks):
                pool.wait_ge(wide_out, n + 1)
                c = CHUNKS[n][1]
                pool.dma_start(dram["pool_mod"][c // 2:c // 2 + 1, (c % 2) * 512:(c % 2 + 1) * 512], wide[n % 2][0:1, :])\
                    .then_inc(row_st[n % 2], 16)
            for i in range(2):
                pool.wait_ge(row_st[i], 16 * len([n for n in row_chunks if n % 2 == i]))

        @block.tensor
        def _(pe):
            def products(n):
                layer, c = CHUNKS[n]
                pe.wait_ge(w_ld[n % WBUF], 32 * (n // WBUF + 1))
                if n == 0:
                    pe.wait_ge(lhs, 2)
                if n >= 2:
                    pe.wait_ge(wide_out, n - 1)
                stationary = lhs_mixed if layer == 0 and c < 4 else lhs_x
                for k in range(KD):
                    last = pe.matmul(wide_ps[n % 2][:, :], stationary[:, k, :], w_sb[n % WBUF][:, k, :],
                                     start=(k == 0), stop=(k == KD - 1))
                last.then_inc(wide_mm, 1)

            def columns(n):
                if n not in column_chunks:
                    return
                i = column_chunks.index(n)
                pe.wait_ge(wide_out, n + 1)
                if i >= 2:
                    pe.wait_ge(col_out, i - 1)
                for j in range(4):
                    last = pe.matmul(col_ps[i % 2][:, j, :], wide[n % 2][:, j * P:(j + 1) * P],
                                     keep["ident"][:, 0:65:64], start=True, stop=True)
                last.then_inc(col_mm, 1)

            def turn():
                i = 0
                for g, (first, tiles, _) in enumerate(GROUPS):
                    pe.wait_ge(normed, first + tiles)
                    for k in range(KD):
                        if i >= 3:
                            pe.wait_ge(whole, i - 2)
                        for t in range(tiles):
                            last = pe.transpose(turn_ps[i % 3][:, t * P:(t + 1) * P],
                                                x_sb[:, first + t, k * P:(k + 1) * P], keep["ident"][:, :])
                        last.then_inc(turned, 1)
                        i += 1

            pe.wait_ge(small_ld, 48)
            for n in range(len(CHUNKS)):
                products(n)
                if n >= 1:
                    columns(n - 1)
                if n == EARLY:
                    turn()
            columns(len(CHUNKS) - 1)

        @block.scalar
        def _(act):
            act.wait_ge(small_ld, 48)
            act.activation(c_silu[:, :, :], c_col[:, :, :], ACT.Silu).then_inc(silu, 1)
            for t in range(TX + TC):
                act.wait_ge(x_ld[min(t // 4, 2)], 16)
                if t:
                    act.wait_ge(squared, t)
                act.activation(square[:, :], x_sb[:, t, :], ACT.Square, accum_out=sums[:, t:t + 1]).then_inc(squared, 1)
            act.wait_ge(dchain, 1)
            act.activation(root[:, :], mean[:, :], ACT.Sqrt).then_inc(rooted, 1)
            act.wait_ge(dchain, 2)
            for t in range(TX + TC):
                act.activation(x_sb[:, t, :], x_sb[:, t, :], ACT.Copy, scale=rstd[:, t:t + 1]).then_inc(normed, 1)
            act.wait_ge(col_out, EARLY)
            i = 0
            for first, tiles, col in GROUPS:
                w = tiles * P
                for k in range(KD):
                    act.wait_ge(turned, i + 1)
                    if i >= 2:
                        act.wait_ge(split, i - 1)
                    act.activation(x_full[:, i % 2, 0:w], turn_ps[i % 3][:, 0:w], ACT.Identity,
                                   scale=keep["attn_cols"][:, col, k:k + 1], bias=keep["attn_cols"][:, col + 1, k:k + 1])\
                       .then_inc(whole, 1)
                    act.wait_ge(whole, i + 1)
                    act.activation(keep["x_hi"][:, k, first * P:first * P + w], x_full[:, i % 2, 0:w], ACT.Copy)\
                       .then_inc(rounded, 1)
                    i += 1

        @block.vector
        def _(dve):
            dve.wait_ge(silu, 1)
            dve.tensor_copy(lhs_x[:, :, :], c_silu[:, 0, :].unsqueeze(2).to_broadcast([P, KD, P])).then_inc(lhs, 1)
            dve.tensor_copy(lhs_mixed[:, :, 0:P // 2], c_silu[:, 0, :].unsqueeze(2).to_broadcast([P, KD, P // 2]))
            dve.tensor_copy(lhs_mixed[:, :, P // 2:P], c_silu[:, 1, :].unsqueeze(2).to_broadcast([P, KD, P // 2]))\
               .then_inc(lhs, 1)

            def sums_of(n):
                layer, c = CHUNKS[n]
                dve.wait_ge(wide_mm, n + 1)
                if n >= 2:
                    done = len([m for m in column_chunks if m <= n - 2])
                    if done:
                        dve.wait_ge(col_mm, done)
                    done = len([m for m in row_chunks if m <= n - 2 and m % 2 == n % 2])
                    if done:
                        dve.wait_ge(row_st[n % 2], 16 * done)
                target = keep["gate0"][:, (c % 2) * 512:(c % 2 + 1) * 512] if layer == 0 and c // 2 == 2 else wide[n % 2][:, :]
                dve.tensor_tensor(target, wide_ps[n % 2][:, :], b_sb[n % WBUF][:, :], ALU.add).then_inc(wide_out, 1)

            def columns_of(n):
                if n not in column_chunks:
                    return
                i = column_chunks.index(n)
                dve.wait_ge(col_mm, i + 1)
                targets = column_targets(*CHUNKS[n])
                for j, (added, source, target) in enumerate(targets):
                    last = dve.tensor_scalar(target, col_ps[i % 2][:, :, source], added, None, ALU.add)
                last.then_inc(col_out, 1)

            def chunk(n):
                sums_of(n)
                if n >= 1:
                    columns_of(n - 1)

            chunk(0)
            dve.wait_ge(squared, TX + TC)
            dve.tensor_scalar(mean[:, :], sums[:, :], 1.0 / D, EPS, ALU.mult, ALU.add).then_inc(dchain, 1)
            dve.wait_ge(rooted, 1)
            dve.reciprocal(rstd[:, :], root[:, :]).then_inc(dchain, 1)
            for n in range(1, EARLY + 1):
                chunk(n)
            i = 0
            for first, tiles, _ in GROUPS:
                for k in range(KD):
                    dve.wait_ge(rounded, i + 1)
                    here = slice(first * P, (first + tiles) * P)
                    dve.tensor_tensor(keep["x_lo"][:, k, here], x_full[:, i % 2, 0:tiles * P],
                                      keep["x_hi"][:, k, here].bitcast(F), ALU.subtract).then_inc(split, 1)
                    i += 1
            for n in range(EARLY + 1, len(CHUNKS)):
                chunk(n)
            columns_of(len(CHUNKS) - 1)


def projection_phase(nc, w_in, dram, keep):
    F, R = mybir.dt.float32, mybir.dt.float32r
    ACT, ALU = mybir.ActivationFunctionType, mybir.AluOpType
    ctx = ExitStack()
    with ctx:
        def sb(n, s, d=F):
            return ctx.enter_context(nc.sbuf_tensor(f"proj_{n}", s, d))

        def ps(n, s):
            bank = ctx.enter_context(nc.psum_tensor(f"proj_{n}_ps", [P, 512], F))
            if len(s) == 3:
                return bank[:, 0:s[1] * s[2]].rearrange("p (a b) -> p a b", a=s[1])
            return bank[:, 0:s[1]]

        sem = phase_semaphores(nc, ctx, "proj")

        W = 256
        raw = [sb(f"raw{i}", [P, KD, W]) for i in range(2)]
        w_hi = [sb(f"w_hi{i}", [P, KD, W], R) for i in range(2)]
        w_lo = [sb(f"w_lo{i}", [P, KD, W], R) for i in range(2)]
        cos = sb("cos", [P, TX, HEAD])
        sin = sb("sin", [P, TX, HEAD])
        with_cos = sb("with_cos", [P, W])
        with_sin = sb("with_sin", [P, W])
        roped = [sb(f"roped{i}", [P, W]) for i in range(2)]
        square = sb("square", [P, W])
        out_ps = [ps(f"out{i}", [P, W]) for i in range(4)]
        turn_ps = [ps(f"turn{i}", [P, 2, P]) for i in range(2)]

        tab_ld, raw_ld = sem("tab_ld"), [sem(f"raw_ld{i}") for i in range(2)]
        rounded, split, mm, turned, turned_out, ready, chain, squared = (
            sem(n) for n in ("rounded", "split", "mm", "turned", "turned_out", "ready", "chain", "squared"))
        left = {"dve": sem("left_dve"), "act": sem("left_act")}

        PIECES = ["q0", "q1", "kv", "u0", "u1", "v0", "v1"]
        UNITS = [(i, t) for i, piece in enumerate(PIECES) for t in range(TX + TC if piece == "kv" else TX)]
        who = ["act" if PIECES[i][0] in "uv" else "dve" for i, _ in UNITS]
        nth = [who[:u + 1].count(who[u]) for u in range(len(UNITS))]
        turns = [u for u, w in enumerate(who) if w == "dve"]
        last_unit = [max(u for u, (j, _) in enumerate(UNITS) if j == i) for i in range(len(PIECES))]
        block = ctx.enter_context(nc.Block())

        @block.sync
        def _(sp):
            sp.dma_start(cos[:, :, :], dram["cos"].rearrange("(t p) f -> p t f", p=P)).then_inc(tab_ld, 16)
            sp.dma_start(sin[:, :, :], dram["sin"].rearrange("(t p) f -> p t f", p=P)).then_inc(tab_ld, 16)
            rows = w_in.rearrange("a (k p) f -> p (a k) f", p=P)
            for i, piece in enumerate(PIECES):
                if i >= 2:
                    sp.wait_ge(split, i - 1)
                to, done = raw[i % 2], raw_ld[i % 2]
                if piece[0] == "q":
                    a = int(piece[1])
                    for side in range(2):
                        for j in range(2):
                            h = side * Q_HEADS // 2 + 2 * a + j
                            at = (2 * j + side) * HEAD
                            sp.dma_start(to[:, :, at:at + HEAD], rows[:, :, h * HEAD:(h + 1) * HEAD]).then_inc(done, 16)
                else:
                    at = {"kv": Q_END, "u0": KV_END, "u1": KV_END + W, "v0": KV_END + 2 * W, "v1": KV_END + 3 * W}[piece]
                    sp.dma_start(to[:, :, :], rows[:, :, at:at + W]).then_inc(done, 16)

        def loads(i):
            return 16 * sum(4 if PIECES[j][0] == "q" else 1 for j in range(i % 2, i + 1, 2))

        @block.tensor
        def _(pe):
            def turn(u):
                if who[u] == "act":
                    return
                i = turns.index(u)
                pe.wait_ge(ready, i + 1)
                if i >= 2:
                    pe.wait_ge(turned_out, i - 1)
                for j in range(2 if PIECES[UNITS[u][0]][0] == "q" else 1):
                    last = pe.transpose(turn_ps[i % 2][:, j, :], roped[i % 2][:, j * P:(j + 1) * P], keep["ident"][:, :])
                last.then_inc(turned, 1)

            for u, (i, t) in enumerate(UNITS):
                pe.wait_ge(split, i + 1)
                if u >= 4:
                    pe.wait_ge(left[who[u - 4]], nth[u - 4])
                bank = out_ps[u % 4]
                here = slice(t * P, (t + 1) * P)
                for k in range(KD):
                    wh, wl = w_hi[i % 2][:, k, :], w_lo[i % 2][:, k, :]
                    pe.matmul(bank[:, :], keep["x_hi"][:, k, here], wh, start=(k == 0), stop=False)
                    pe.matmul(bank[:, :], keep["x_hi"][:, k, here], wl, start=False, stop=False)
                    last = pe.matmul(bank[:, :], keep["x_lo"][:, k, here], wh, start=False, stop=(k == KD - 1))
                last.then_inc(mm, 1)
                if u >= 1:
                    turn(u - 1)
            turn(len(UNITS) - 1)

        @block.scalar
        def _(act):
            def round_piece(i):
                act.wait_ge(raw_ld[i % 2], loads(i))
                if i >= 2:
                    act.wait_ge(mm, last_unit[i - 2] + 1)
                act.activation(w_hi[i % 2][:, :, :], raw[i % 2][:, :, :], ACT.Copy).then_inc(rounded, 1)

            def copy_turned(u):
                i = turns.index(u)
                piece, t = PIECES[UNITS[u][0]], UNITS[u][1]
                act.wait_ge(turned, i + 1)
                if piece[0] == "q":
                    to = keep["q_t"][:, 2 * int(piece[1]):2 * int(piece[1]) + 2, t * P:(t + 1) * P]
                    act.activation(to, turn_ps[i % 2][:, :, :], ACT.Copy, scale=float(HEAD) ** -0.5).then_inc(turned_out, 1)
                else:
                    act.activation(keep["k_t"][:, t * P:(t + 1) * P], turn_ps[i % 2][:, 0, :], ACT.Copy).then_inc(turned_out, 1)

            round_piece(0)
            gelus = 0
            for u, (i, t) in enumerate(UNITS):
                if t == 1 and i + 1 < len(PIECES):
                    round_piece(i + 1)
                if u >= 2 and who[u - 2] == "dve":
                    copy_turned(u - 2)
                if who[u] == "act":
                    act.wait_ge(mm, u + 1)
                    half = int(PIECES[i][1])
                    to = (keep["u"] if PIECES[i][0] == "u" else keep["v_gm"])[:, t, half * W:(half + 1) * W]
                    act.activation(to, out_ps[u % 4][:, :], ACT.Gelu_apprx_tanh).then_inc(left["act"], 1)
                    if PIECES[i][0] == "v":
                        act.wait_ge(left["act"], nth[u])
                        if gelus:
                            act.wait_ge(squared, gelus)
                        gelus += 1
                        act.activation(square[:, :], to, ACT.Square, accum_out=keep["v_sums"][:, t, half:half + 1])\
                           .then_inc(squared, 1)

        @block.vector
        def _(dve):
            chain_n = [0]

            def link(ins):
                chain_n[0] += 1
                ins.then_inc(chain, 1)
                dve.wait_ge(chain, chain_n[0])

            def rest(i):
                dve.wait_ge(rounded, i + 1)
                dve.tensor_tensor(w_lo[i % 2][:, :, :], raw[i % 2][:, :, :], w_hi[i % 2][:, :, :].bitcast(F), ALU.subtract)\
                   .then_inc(split, 1)

            def rotate(u, t, heads, to):
                n = heads * HEAD
                bank = out_ps[u % 4]
                dve.tensor_tensor(with_cos[:, 0:n].rearrange("p (h f) -> p h f", h=heads),
                                  bank[:, 0:n].rearrange("p (h f) -> p h f", h=heads),
                                  cos[:, t:t + 1, :].to_broadcast([P, heads, HEAD]), ALU.mult)
                halves = "p (h a s f) -> p h a s f"
                for s in range(2):
                    o = with_sin[:, 0:n].rearrange(halves, h=heads, a=2, s=2)[:, :, :, s, :]
                    x = bank[:, 0:n].rearrange(halves, h=heads, a=2, s=2)[:, :, :, 1 - s, :]
                    y = sin[:, t:t + 1, :].rearrange("p o (a s f) -> p o a s f", a=2, s=2)[:, :, :, s, :]
                    last = dve.tensor_tensor(o, x, y.to_broadcast([P, heads, 2, HEAD // 4]), ALU.mult)
                link(last)
                return dve.tensor_tensor(to, with_cos[:, 0:n], with_sin[:, 0:n], ALU.add)

            rest(0)
            dve.wait_ge(tab_ld, 32)
            for u, (i, t) in enumerate(UNITS):
                if t == 1 and i + 1 < len(PIECES):
                    rest(i + 1)
                if who[u] != "dve":
                    continue
                n = turns.index(u)
                dve.wait_ge(mm, u + 1)
                if n:
                    dve.wait_ge(ready, n)
                if n >= 2:
                    dve.wait_ge(turned, n - 1)
                to = roped[n % 2]
                if PIECES[i] != "kv":
                    rotate(u, t, 4, to[:, :]).then_inc(ready, 1)
                    dve.wait_ge(ready, n + 1)
                    dve.sem_inc(left["dve"], 1)
                    continue
                if t < TX:
                    rotate(u, t, 2, to[:, 0:P]).then_inc(ready, 1)
                else:
                    dve.tensor_copy(to[:, 0:P], out_ps[u % 4][:, 0:P]).then_inc(ready, 1)
                dve.tensor_copy(keep["v"][:, t, :], out_ps[u % 4][:, P:2 * P]).then_inc(left["dve"], 1)

        @block.gpsimd
        def _(pool):
            pool.wait_ge(turned_out, len(turns))


def attention_phase(nc, sink, dram, keep):
    F = mybir.dt.float32
    ACT, ALU, AX = mybir.ActivationFunctionType, mybir.AluOpType, mybir.AxisListType
    ctx = ExitStack()
    with ctx:
        def sb(n, s, d=F):
            return ctx.enter_context(nc.sbuf_tensor(f"att_{n}", s, d))

        def ps(n, s):
            bank = ctx.enter_context(nc.psum_tensor(f"att_{n}_ps", [P, 512], F))
            if len(s) == 3:
                return bank[:, 0:s[1] * s[2]].rearrange("p (a b) -> p a b", a=s[1])
            return bank[:, 0:s[1]]

        sem = phase_semaphores(nc, ctx, "att")

        CTX = TC * P
        mask = sb("mask", [P, 3 * P])
        zeros = sb("zeros", [P, D])
        zeroed, cleared = sem("zeroed"), sem("cleared")
        sinks = sb("sinks", [P, Q_HEADS])
        top = sb("top", [P, Q_HEADS, 2])
        top1 = sb("top1", [P, Q_HEADS])
        minus = [sb(f"minus{i}", [P, Q_HEADS]) for i in range(2)]
        sink_less = sb("sink_less", [P, Q_HEADS])
        sink_exp = sb("sink_exp", [P, Q_HEADS])
        sums = [sb(f"sums{i}", [P, Q_HEADS, 2]) for i in range(2)]
        total = sb("total", [P, Q_HEADS])
        total2 = sb("total2", [P, Q_HEADS])
        inverse = sb("inverse", [P, Q_HEADS])
        masked = [sb(f"masked{i}", [P, 3 * P]) for i in range(2)]
        prob = [sb(f"prob{i}", [P, 3 * P + CTX]) for i in range(2)]
        prob_t = [sb(f"prob_t{i}", [P, 3 * P + CTX]) for i in range(2)]
        near_ps = [ps(f"near{i}", [P, 512]) for i in range(2)]
        far_ps = [ps(f"far{i}", [P, 512]) for i in range(2)]
        near_t, far_t = ps("near_t", [P, 512]), ps("far_t", [P, 512])
        out_ps = [ps(f"out{i}", [P, 512]) for i in range(2)]

        ld, scored, masked_ok, far_top, chain, minus_ok, near_exp, far_exp = (
            sem(n) for n in ("ld", "scored", "masked", "far_top", "chain", "minus", "near_exp", "far_exp"))
        near_turned, far_turned, near_copied, far_copied, valued, sink_ok, sink_done, written = (
            sem(n) for n in ("near_t", "far_t", "near_c", "far_c", "valued", "sink_ok", "sink_done", "written"))

        STEPS = [(n, h) for n in range(TX) for h in range(Q_HEADS)]

        def band(n):
            first, last = max(0, n - 1) * P, min(TX, n + 2) * P
            return first, last, first - (n - 1) * P

        def place(h):
            side = h // (Q_HEADS // 2)
            return slice(side * HEAD, (side + 1) * HEAD), h % (Q_HEADS // 2)

        block = ctx.enter_context(nc.Block())

        @block.sync
        def _(sp):
            sp.dma_start(mask[:, :], dram["mask"]).then_inc(ld, 16)
            sp.dma_start(sinks[:, :], sink[0, :].partition_broadcast(P)).then_inc(ld, 16)
            sp.wait_ge(zeroed, 1)
            sp.dma_start(dram["y"].rearrange("(c p) d -> p c d", p=P),
                         zeros[:, :].unsqueeze(1).to_broadcast([P, SLOT_TILES, D])).then_inc(cleared, 16)
            sp.wait_ge(cleared, 16)

        @block.gpsimd
        def _(pool):
            pool.memset(zeros[:, :], 0.0).then_inc(zeroed, 1)

        @block.tensor
        def _(pe):
            def score(s):
                n, h = STEPS[s]
                first, last, _ = band(n)
                rows, pair = place(h)
                if s >= 2:
                    pe.wait_ge(masked_ok, s - 1)
                    pe.wait_ge(far_exp, s - 1)
                q = keep["q_t"][rows, pair, n * P:(n + 1) * P]
                pe.matmul(near_ps[s % 2][:, 0:last - first], q, keep["k_t"][rows, first:last], start=True, stop=True)
                pe.matmul(far_ps[s % 2][:, 0:CTX], q, keep["k_t"][rows, TX * P:TX * P + CTX], start=True, stop=True)\
                  .then_inc(scored, 1)

            def turn(s):
                n, h = STEPS[s]
                first, last, _ = band(n)
                keys = last - first
                pe.wait_ge(near_exp, s + 1)
                if s:
                    pe.wait_ge(near_copied, s)
                for j in range(keys // P):
                    x = pe.transpose(near_t[:, j * P:(j + 1) * P], prob[s % 2][:, j * P:(j + 1) * P], keep["ident"][:, :])
                x.then_inc(near_turned, 1)
                pe.wait_ge(far_exp, s + 1)
                if s:
                    pe.wait_ge(far_copied, s)
                for j in range(TC):
                    x = pe.transpose(far_t[:, j * P:(j + 1) * P], prob[s % 2][:, (3 + j) * P:(4 + j) * P], keep["ident"][:, :])
                x.then_inc(far_turned, 1)

            def value(s):
                n, h = STEPS[s]
                first, last, _ = band(n)
                side = h // (Q_HEADS // 2)
                cols = slice(side * HEAD, (side + 1) * HEAD)
                if h == 0 and n >= 2:
                    pe.wait_ge(written, n - 1)
                pe.wait_ge(near_copied, s + 1)
                pe.wait_ge(far_copied, s + 1)
                tiles = [(j, first // P + j) for j in range((last - first) // P)] + [(3 + j, TX + j) for j in range(TC)]
                for m, (at, tile) in enumerate(tiles):
                    x = pe.matmul(out_ps[n % 2][:, h * HEAD:(h + 1) * HEAD], prob_t[s % 2][:, at * P:(at + 1) * P],
                                  keep["v"][:, tile, cols], start=(m == 0), stop=(m == len(tiles) - 1))
                x.then_inc(valued, 1)

            S = len(STEPS)
            for s in range(S + 2):
                if s < S:
                    score(s)
                if 1 <= s <= S:
                    turn(s - 1)
                if s >= 2:
                    value(s - 2)

        @block.vector
        def _(dve):
            chain_n = [0]

            def link(ins):
                chain_n[0] += 1
                ins.then_inc(chain, 1)
                dve.wait_ge(chain, chain_n[0])

            def maxima(s):
                n, h = STEPS[s]
                first, last, at = band(n)
                keys = last - first
                dve.wait_ge(scored, s + 1)
                if s >= 2:
                    dve.wait_ge(near_exp, s - 1)
                dve.tensor_tensor(masked[s % 2][:, 0:keys], near_ps[s % 2][:, 0:keys], mask[:, at:at + keys], ALU.add)\
                   .then_inc(masked_ok, 1)
                dve.reduce_max(top[:, h, 1:2], far_ps[s % 2][:, 0:CTX], AX.X)
                dve.wait_ge(masked_ok, s + 1)
                link(dve.reduce_max(top[:, h, 0:1], masked[s % 2][:, 0:keys], AX.X))
                link(dve.tensor_tensor(top1[:, h:h + 1], top[:, h, 0:1], top[:, h, 1:2], ALU.max))
                if h == 0 and n >= 2:
                    dve.wait_ge(sink_done, n - 1)
                dve.tensor_scalar(minus[n % 2][:, h:h + 1], top1[:, h:h + 1], sinks[:, h:h + 1], -1.0, ALU.max, ALU.mult)\
                   .then_inc(minus_ok, 1)

            def copy_near(s):
                n, h = STEPS[s]
                first, last, _ = band(n)
                dve.wait_ge(near_turned, s + 1)
                if s >= 2:
                    dve.wait_ge(valued, s - 1)
                dve.tensor_copy(prob_t[s % 2][:, 0:last - first], near_t[:, 0:last - first]).then_inc(near_copied, 1)

            def finish(n):
                b = n % 2
                dve.wait_ge(minus_ok, (n + 1) * Q_HEADS)
                dve.tensor_tensor(sink_less[:, :], sinks[:, :], minus[b][:, :], ALU.add).then_inc(sink_ok, 1)
                dve.wait_ge(far_exp, (n + 1) * Q_HEADS)
                link(dve.tensor_tensor(total[:, :], sums[b][:, :, 0], sums[b][:, :, 1], ALU.add))
                dve.wait_ge(sink_done, n + 1)
                link(dve.tensor_tensor(total2[:, :], total[:, :], sink_exp[:, :], ALU.add))
                link(dve.reciprocal(inverse[:, :], total2[:, :]))
                dve.wait_ge(valued, (n + 1) * Q_HEADS)
                dve.tensor_tensor(keep["att"][:, n, :].rearrange("p (h d) -> p h d", h=Q_HEADS),
                                  out_ps[b][:, :].rearrange("p (h d) -> p h d", h=Q_HEADS),
                                  inverse[:, :].unsqueeze(2).to_broadcast([P, Q_HEADS, HEAD]), ALU.mult).then_inc(written, 1)

            dve.wait_ge(ld, 32)
            S = len(STEPS)
            for s in range(S + 4):
                if s < S:
                    maxima(s)
                if 1 <= s <= S:
                    copy_near(s - 1)
                if s >= 4 and STEPS[s - 4][1] == Q_HEADS - 1:
                    finish(STEPS[s - 4][0])

        @block.scalar
        def _(act):
            def exps(s):
                n, h = STEPS[s]
                first, last, _ = band(n)
                keys = last - first
                act.wait_ge(minus_ok, s + 1)
                if s >= 2:
                    act.wait_ge(far_turned, s - 1)
                if h == 0 and n >= 2:
                    act.wait_ge(written, n - 1)
                act.activation(prob[s % 2][:, 0:keys], masked[s % 2][:, 0:keys], ACT.Exp, bias=minus[n % 2][:, h:h + 1],
                               accum_out=sums[n % 2][:, h, 0:1]).then_inc(near_exp, 1)
                act.activation(prob[s % 2][:, 3 * P:3 * P + CTX], far_ps[s % 2][:, 0:CTX], ACT.Exp,
                               bias=minus[n % 2][:, h:h + 1], accum_out=sums[n % 2][:, h, 1:2]).then_inc(far_exp, 1)

            def copy_far(s):
                act.wait_ge(far_turned, s + 1)
                if s >= 2:
                    act.wait_ge(valued, s - 1)
                act.activation(prob_t[s % 2][:, 3 * P:3 * P + CTX], far_t[:, 0:CTX], ACT.Copy).then_inc(far_copied, 1)

            S = len(STEPS)
            for s in range(S + 4):
                if s < S:
                    exps(s)
                if 1 <= s <= S:
                    copy_far(s - 1)
                if s >= 4 and STEPS[s - 4][1] == Q_HEADS - 1:
                    act.wait_ge(sink_ok, STEPS[s - 4][0] + 1)
                    act.activation(sink_exp[:, :], sink_less[:, :], ACT.Exp).then_inc(sink_done, 1)


def mixer_output_phase(nc, gm, dram, keep):
    F, R = mybir.dt.float32, mybir.dt.float32r
    ACT, ALU = mybir.ActivationFunctionType, mybir.AluOpType
    ctx = ExitStack()
    with ctx:
        def sb(n, s, d=F):
            return ctx.enter_context(nc.sbuf_tensor(f"mix_{n}", s, d))

        def ps(n, s):
            bank = ctx.enter_context(nc.psum_tensor(f"mix_{n}_ps", [P, 512], F))
            if len(s) == 3:
                return bank[:, 0:s[1] * s[2]].rearrange("p (a b) -> p a b", a=s[1])
            return bank[:, 0:s[1]]

        sem = phase_semaphores(nc, ctx, "mix")

        GM = D // 2
        w_s = sb("w_s", [P, GM_GROUPS, P])
        w_s_t = sb("w_s_t", [P, GM_GROUPS, P])
        bias = sb("bias", [P, GM_GROUPS])
        gain = sb("gain", [P, GM])
        mean, root, rstd = sb("mean", [P, TX]), sb("root", [P, TX]), sb("rstd", [P, TX])
        v_sum = sb("v_sum", [P, TX])
        biased = sb("biased", [P, GM])
        raw = [sb(f"raw{i}", [P, 2, D]) for i in range(2)]
        w_hi, w_lo = sb("w_hi", [P, KD, D], R), sb("w_lo", [P, KD, D], R)
        cat_hi = [sb(f"cat_hi{i}", [P, KD, P], R) for i in range(2)]
        cat_lo = [sb(f"cat_lo{i}", [P, KD, P], R) for i in range(2)]
        x_in = [sb(f"x_in{i}", [P, D]) for i in range(2)]
        gated = sb("gated", [P, D])
        x_new = [sb(f"x_new{i}", [P, D]) for i in range(2)]
        x_norm = [sb(f"x_norm{i}", [P, D]) for i in range(2)]
        square = sb("square", [P, D])
        ssum, smean, sroot, srstd = (sb(n, [P, TX]) for n in ("ssum", "smean", "sroot", "srstd"))
        gm_ps = ps("gm", [P, GM])
        turn_ps = [ps(f"turn{i}", [P, 4, P]) for i in range(2)]
        y_ps = [ps(f"y{i}", [P, 512]) for i in range(4)]

        ld, raw_ld, x_ld = sem("ld"), [sem(f"raw_ld{i}") for i in range(2)], [sem(f"x_ld{i}") for i in range(2)]
        w_turned, w_copied, rounded, split, chain, rooted, v_ok, mixed, gm_ok = (
            sem(n) for n in ("w_turned", "w_copied", "rounded", "split", "chain", "rooted", "v_ok", "mixed", "gm_ok"))
        turned, cat_rounded, cat_split, y_mm, y_read, x_ok, squared, s_mean, s_root, s_rstd, x_normed = (
            sem(n) for n in ("turned", "cat_rounded", "cat_split", "y_mm", "y_read", "x_ok", "squared", "s_mean", "s_root",
                             "s_rstd", "x_normed"))
        x_st = [sem(f"x_st{i}") for i in range(2)]
        mean_ok = sem("mean_ok")
        rstd_ok = sem("rstd_ok")
        block = ctx.enter_context(nc.Block())
        KB = 2
        BLOCKS = KD // KB
        x_tiles = gm["x"].rearrange("a (t p) d -> (a t) p d", p=P)

        @block.sync
        def _(sp):
            sp.dma_start(w_s[:, :, :], gm["w_s"].rearrange("a g t s -> t (a g) s")).then_inc(ld, 16)
            sp.dma_start(bias[:, :], gm["b_s"].rearrange("a g t -> t (a g)")).then_inc(ld, 16)
            sp.dma_start(gain[:, :], gm["gain"][0, :].partition_broadcast(P)).then_inc(ld, 16)
            rows = gm["w_out"].rearrange("a (k p) f -> p (a k) f", p=P)
            for b in range(BLOCKS):
                if b >= 2:
                    sp.wait_ge(split, b - 1)
                sp.dma_start(raw[b % 2][:, :, :], rows[:, b * KB:(b + 1) * KB, :]).then_inc(raw_ld[b % 2], 16)
            for t in range(TX):
                if t >= 2:
                    sp.wait_ge(x_ok, t - 1)
                sp.dma_start(x_in[t % 2][:, :], x_tiles[t]).then_inc(x_ld[t % 2], 16)

        @block.gpsimd
        def _(pool):
            for t in range(TX):
                pool.wait_ge(x_normed, t + 1)
                pool.dma_start(dram["x1"][t * P:(t + 1) * P, :], x_new[t % 2][:, :]).then_inc(x_st[t % 2], 16)
                pool.dma_start(dram["xn"][t * P:(t + 1) * P, :], x_norm[t % 2][:, :]).then_inc(x_st[t % 2], 16)
            for i in range(2):
                pool.wait_ge(x_st[i], 32 * (TX // 2))

        @block.tensor
        def _(pe):
            pe.wait_ge(ld, 48)
            for g in range(GM_GROUPS):
                x = pe.transpose(turn_ps[g // 4][:, g % 4, :], w_s[:, g, :], keep["ident"][:, :])
                if g % 4 == 3:
                    x.then_inc(w_turned, 1)
            pe.wait_ge(w_copied, 2)

            def gate(t):
                pe.wait_ge(v_ok, t + 1)
                if t:
                    pe.wait_ge(mixed, 2 * t)
                for g in range(GM_GROUPS):
                    x = pe.matmul(gm_ps[:, g * HEAD:(g + 1) * HEAD], w_s_t[:, g, :],
                                  keep["v_gm"][:, t, g * HEAD:(g + 1) * HEAD], start=True, stop=True)
                x.then_inc(mixed, 1)

            def turn(t):
                for half in range(2):
                    i = 2 * t + half
                    if half:
                        pe.wait_ge(gm_ok, t + 1)
                    if i >= 2:
                        pe.wait_ge(cat_split, i - 1)
                    source = keep["att"] if half == 0 else keep["u"]
                    for j in range(4):
                        x = pe.transpose(turn_ps[half][:, j, :], source[:, t, j * P:(j + 1) * P], keep["ident"][:, :])
                    x.then_inc(turned, 1)

            def project(t):
                pe.wait_ge(cat_split, 2 * t + 2)
                if t == 0:
                    pe.wait_ge(split, BLOCKS)
                if t >= 2:
                    pe.wait_ge(y_read, t - 1)
                for half in range(2):
                    bank = y_ps[2 * (t % 2) + half]
                    cols = slice(half * 512, (half + 1) * 512)
                    for k in range(KD):
                        pe.matmul(bank[:, :], cat_hi[t % 2][:, k, :], w_hi[:, k, cols], start=(k == 0), stop=False)
                        pe.matmul(bank[:, :], cat_hi[t % 2][:, k, :], w_lo[:, k, cols], start=False, stop=False)
                        x = pe.matmul(bank[:, :], cat_lo[t % 2][:, k, :], w_hi[:, k, cols], start=False, stop=(k == KD - 1))
                x.then_inc(y_mm, 1)

            gate(0)
            turn(0)
            for t in range(TX):
                if t + 1 < TX:
                    gate(t + 1)
                    turn(t + 1)
                project(t)

        @block.scalar
        def _(act):
            for i in range(2):
                act.wait_ge(w_turned, i + 1)
                act.activation(w_s_t[:, 4 * i:4 * i + 4, :], turn_ps[i][:, :, :], ACT.Copy).then_inc(w_copied, 1)
            act.wait_ge(mean_ok, 1)
            act.activation(root[:, :], mean[:, :], ACT.Sqrt).then_inc(rooted, 1)
            for b in range(BLOCKS):
                act.wait_ge(raw_ld[b % 2], 16 * (b // 2 + 1))
                act.activation(w_hi[:, b * KB:(b + 1) * KB, :], raw[b % 2][:, :, :], ACT.Copy).then_inc(rounded, 1)

            def round_cat(t):
                for half in range(2):
                    i = 2 * t + half
                    act.wait_ge(turned, i + 1)
                    if t >= 2 and half == 0:
                        act.wait_ge(y_mm, t - 1)
                    act.activation(cat_hi[t % 2][:, 4 * half:4 * half + 4, :], turn_ps[half][:, :, :], ACT.Copy)\
                       .then_inc(cat_rounded, 1)

            def norm(t):
                act.wait_ge(x_ok, t + 1)
                if t:
                    act.wait_ge(squared, t)
                act.activation(square[:, :], x_new[t % 2][:, :], ACT.Square, accum_out=ssum[:, t:t + 1]).then_inc(squared, 1)
                act.wait_ge(s_mean, t + 1)
                act.activation(sroot[:, t:t + 1], smean[:, t:t + 1], ACT.Sqrt).then_inc(s_root, 1)
                act.wait_ge(s_rstd, t + 1)
                if t >= 2:
                    act.wait_ge(x_st[t % 2], 32 * (t // 2))
                act.activation(x_norm[t % 2][:, :], x_new[t % 2][:, :], ACT.Copy, scale=srstd[:, t:t + 1]).then_inc(x_normed, 1)

            round_cat(0)
            for t in range(TX):
                if t + 1 < TX:
                    round_cat(t + 1)
                norm(t)

        @block.vector
        def _(dve):
            chain_n = [0]

            def link(ins):
                chain_n[0] += 1
                ins.then_inc(chain, 1)
                dve.wait_ge(chain, chain_n[0])

            link(dve.tensor_tensor(v_sum[:, :], keep["v_sums"][:, :, 0], keep["v_sums"][:, :, 1], ALU.add))
            dve.tensor_scalar(mean[:, :], v_sum[:, :], 1.0 / GM, EPS, ALU.mult, ALU.add).then_inc(mean_ok, 1)
            dve.wait_ge(rooted, 1)
            dve.reciprocal(rstd[:, :], root[:, :]).then_inc(rstd_ok, 1)
            dve.wait_ge(rstd_ok, 1)
            dve.wait_ge(ld, 48)

            def scale_v(t):
                dve.scalar_tensor_tensor(keep["v_gm"][:, t, :], keep["v_gm"][:, t, :], rstd[:, t:t + 1], gain[:, :],
                                         ALU.mult, ALU.mult).then_inc(v_ok, 1)

            def gate(t):
                dve.wait_ge(mixed, 2 * t + 1)
                if t:
                    dve.wait_ge(gm_ok, t)
                dve.tensor_tensor(biased[:, :].rearrange("p (g d) -> p g d", g=GM_GROUPS),
                                  gm_ps[:, :].rearrange("p (g d) -> p g d", g=GM_GROUPS),
                                  bias[:, :].unsqueeze(2).to_broadcast([P, GM_GROUPS, HEAD]), ALU.add).then_inc(mixed, 1)
                dve.wait_ge(mixed, 2 * t + 2)
                dve.tensor_tensor(keep["u"][:, t, :], biased[:, :], keep["u"][:, t, :], ALU.mult).then_inc(gm_ok, 1)

            def rest_cat(t):
                for half in range(2):
                    dve.wait_ge(cat_rounded, 2 * t + half + 1)
                    dve.tensor_tensor(cat_lo[t % 2][:, 4 * half:4 * half + 4, :], turn_ps[half][:, :, :],
                                      cat_hi[t % 2][:, 4 * half:4 * half + 4, :].bitcast(F), ALU.subtract).then_inc(cat_split, 1)

            def add(t):
                dve.wait_ge(y_mm, t + 1)
                if t:
                    dve.wait_ge(x_ok, t)
                for half in range(2):
                    x = dve.tensor_tensor(gated[:, half * 512:(half + 1) * 512], y_ps[2 * (t % 2) + half][:, :],
                                          keep["gate0"][:, half * 512:(half + 1) * 512], ALU.mult)
                x.then_inc(y_read, 1)
                dve.wait_ge(y_read, t + 1)
                dve.wait_ge(x_ld[t % 2], 16 * (t // 2 + 1))
                if t >= 2:
                    dve.wait_ge(x_st[t % 2], 32 * (t // 2))
                    dve.wait_ge(x_normed, t - 1)
                dve.tensor_tensor(x_new[t % 2][:, :], gated[:, :], x_in[t % 2][:, :], ALU.add).then_inc(x_ok, 1)

            def norm(t):
                dve.wait_ge(squared, t + 1)
                dve.tensor_scalar(smean[:, t:t + 1], ssum[:, t:t + 1], 1.0 / D, EPS, ALU.mult, ALU.add).then_inc(s_mean, 1)
                dve.wait_ge(s_root, t + 1)
                dve.reciprocal(srstd[:, t:t + 1], sroot[:, t:t + 1]).then_inc(s_rstd, 1)

            scale_v(0)
            gate(0)
            scale_v(1)
            for b in range(BLOCKS):
                dve.wait_ge(rounded, b + 1)
                dve.tensor_tensor(w_lo[:, b * KB:(b + 1) * KB, :], raw[b % 2][:, :, :],
                                  w_hi[:, b * KB:(b + 1) * KB, :].bitcast(F), ALU.subtract).then_inc(split, 1)
            rest_cat(0)
            for t in range(TX):
                if t + 1 < TX:
                    gate(t + 1)
                    if t + 2 < TX:
                        scale_v(t + 2)
                    rest_cat(t + 1)
                add(t)
                norm(t)


def pool_phase(nc, pool_w, pool_scale, dram):
    F = mybir.dt.float32
    ACT, ALU = mybir.ActivationFunctionType, mybir.AluOpType
    ctx = ExitStack()
    with ctx:
        def sb(n, s, d=F):
            return ctx.enter_context(nc.sbuf_tensor(f"pool_{n}", s, d))

        def ps(n, s):
            bank = ctx.enter_context(nc.psum_tensor(f"pool_{n}_ps", [P, 512], F))
            if len(s) == 3:
                return bank[:, 0:s[1] * s[2]].rearrange("p (a b) -> p a b", a=s[1])
            return bank[:, 0:s[1]]

        sem = phase_semaphores(nc, ctx, "pool")

        G = len(POOL_SIZES)
        GD = D // G
        REACH = max(POOL_SIZES) // 2
        band = sb("band", [P, G, 3, P])
        edge = sb("edge", [P, G, 2, REACH])
        weights = sb("weights", [P, G, GD // P, GD])
        shift, scale, gate, scales = (sb(n, [P, D]) for n in ("shift", "scale", "gate", "scales"))
        y_in = [sb(f"y_in{i}", [P, D]) for i in range(2)]
        x = sb("x", [P, TX, D])
        h = sb("h", [P, TX, D])
        scaled = sb("scaled", [P, D])
        square = sb("square", [P, D])
        diff = [sb(f"diff{i}", [P, KD, P]) for i in range(2)]
        gated = sb("gated", [P, D])
        x_norm = [sb(f"x_norm{i}", [P, D]) for i in range(2)]
        sums, mean, root, rstd = (sb(n, [P, 2 * TX]) for n in ("sums", "mean", "root", "rstd"))
        diff_ps = [ps(f"diff{i}", [P, 4, P]) for i in range(4)]
        y_ps = [ps(f"y{i}", [P, 512]) for i in range(4)]

        ld, x_ld, y_ld, x_st = sem("ld"), sem("x_ld"), [sem(f"y_ld{i}") for i in range(2)], [sem(f"x_st{i}") for i in range(2)]
        chain, x_sum, squared, rooted, ready, scaled_ok, h_ok = (
            sem(n) for n in ("chain", "x_sum", "squared", "rooted", "ready", "scaled_ok", "h_ok"))
        mean_ok, diffed, copied, y_mm, y_read, x_ok, normed = (
            sem(n) for n in ("mean_ok", "diffed", "copied", "y_mm", "y_read", "x_ok", "normed"))
        block = ctx.enter_context(nc.Block())

        @block.sync
        def _(sp):
            sp.dma_start(x[:, :, :], dram["x1"].rearrange("(t p) d -> p t d", p=P)).then_inc(x_ld, 16)
            for t in range(TX):
                if t >= 2:
                    sp.wait_ge(x_sum, t - 1)
                sp.dma_start(y_in[t % 2][:, :], dram["y_dense"][t * P:(t + 1) * P, :]).then_inc(y_ld[t % 2], 16)
                if t == 1:
                    for i, to in enumerate((shift, scale, gate)):
                        sp.dma_start(to[:, :], dram["pool_mod"][i, :].partition_broadcast(P)).then_inc(ld, 16)
                    sp.dma_start(scales[:, :], pool_scale[0, :].partition_broadcast(P)).then_inc(ld, 16)
                    sp.dma_start(band[:, :, :, :], dram["band"].rearrange("g e s t -> s g e t")).then_inc(ld, 16)
                    sp.dma_start(edge[:, :, :, :], dram["edge"].rearrange("g e s t -> s g e t")).then_inc(ld, 16)
                    sp.dma_start(weights[:, :, :, :], pool_w.rearrange("a g (c p) d -> p (a g) c d", p=P)).then_inc(ld, 16)

        @block.gpsimd
        def _(pool):
            for t in range(TX):
                pool.wait_ge(normed, t + 1)
                pool.dma_start(dram["x3"][t * P:(t + 1) * P, :], x[:, t, :]).then_inc(x_st[t % 2], 16)
                pool.dma_start(dram["xn"][t * P:(t + 1) * P, :], x_norm[t % 2][:, :]).then_inc(x_st[t % 2], 16)
            for i in range(2):
                pool.wait_ge(x_st[i], 32 * (TX // 2))

        @block.tensor
        def _(pe):
            def difference(t):
                pe.wait_ge(h_ok, min(t + 2, TX))
                if t >= 2:
                    pe.wait_ge(copied, 2 * (t - 1))
                which = 0 if t == 0 else 2 if t == TX - 1 else 1
                for half in range(2):
                    bank = diff_ps[2 * (t % 2) + half]
                    for j in range(4):
                        k = 4 * half + j
                        g = k * P // GD
                        cols = slice(k * P, (k + 1) * P)
                        last = t == TX - 1
                        m = pe.matmul(bank[:, j, :], h[:, t, cols], band[:, g, which, :], start=True, stop=False,
                                      skip_group_check=True)
                        if t:
                            m = pe.matmul(bank[:, j, 0:REACH], h[:, t - 1, cols], edge[:, g, 0, :], start=False, stop=last,
                                          skip_group_check=True)
                        if not last:
                            m = pe.matmul(bank[:, j, P - REACH:P], h[:, t + 1, cols], edge[:, g, 1, :], start=False, stop=True,
                                          skip_group_check=True)
                    m.then_inc(diffed, 1)

            def project(t):
                pe.wait_ge(copied, 2 * t + 2)
                if t >= 2:
                    pe.wait_ge(y_read, t - 1)
                for g in range(G):
                    bank = y_ps[2 * (t % 2) + g * GD // 512]
                    at = g * GD % 512
                    for c in range(GD // P):
                        m = pe.matmul(bank[:, at:at + GD], diff[t % 2][:, g * GD // P + c, :], weights[:, g, c, :],
                                      start=(c == 0), stop=(c == GD // P - 1))
                m.then_inc(y_mm, 1)

            pe.wait_ge(ld, 16 * 7)
            difference(0)
            for t in range(TX):
                if t + 1 < TX:
                    difference(t + 1)
                project(t)

        @block.scalar
        def _(act):
            def sum_squares(i, source):
                if i:
                    act.wait_ge(squared, i)
                act.activation(square[:, :], source, ACT.Square, accum_out=sums[:, i:i + 1]).then_inc(squared, 1)
                act.wait_ge(mean_ok, i + 1)
                act.activation(root[:, i:i + 1], mean[:, i:i + 1], ACT.Sqrt).then_inc(rooted, 1)

            def copy(t):
                for half in range(2):
                    act.wait_ge(diffed, 2 * t + half + 1)
                    if t >= 2:
                        act.wait_ge(y_mm, t - 1)
                    act.activation(diff[t % 2][:, 4 * half:4 * half + 4, :], diff_ps[2 * (t % 2) + half][:, :, :], ACT.Copy)\
                       .then_inc(copied, 1)

            for t in range(TX):
                act.wait_ge(x_sum, t + 1)
                sum_squares(t, x[:, t, :])
            copy(0)
            for t in range(TX):
                if t + 1 < TX:
                    copy(t + 1)
                act.wait_ge(x_ok, t + 1)
                sum_squares(TX + t, x[:, t, :])
                act.wait_ge(ready, TX + t + 1)
                if t >= 2:
                    act.wait_ge(x_st[t % 2], 32 * (t // 2))
                act.activation(x_norm[t % 2][:, :], x[:, t, :], ACT.Copy, scale=rstd[:, TX + t:TX + t + 1]).then_inc(normed, 1)

        @block.vector
        def _(dve):
            chain_n = [0]

            def link(ins):
                chain_n[0] += 1
                ins.then_inc(chain, 1)
                dve.wait_ge(chain, chain_n[0])

            def norm(i):
                dve.wait_ge(squared, i + 1)
                dve.tensor_scalar(mean[:, i:i + 1], sums[:, i:i + 1], 1.0 / D, EPS, ALU.mult, ALU.add).then_inc(mean_ok, 1)
                dve.wait_ge(rooted, i + 1)
                dve.reciprocal(rstd[:, i:i + 1], root[:, i:i + 1]).then_inc(ready, 1)
                dve.wait_ge(ready, i + 1)

            def residual(t):
                dve.wait_ge(y_ld[t % 2], 16 * (t // 2 + 1))
                dve.tensor_tensor(x[:, t, :], x[:, t, :], y_in[t % 2][:, :], ALU.add).then_inc(x_sum, 1)

            def modulate(t):
                norm(t)
                if t:
                    dve.wait_ge(h_ok, t)
                link(dve.scalar_tensor_tensor(scaled[:, :], x[:, t, :], rstd[:, t:t + 1], scale[:, :], ALU.mult, ALU.mult))
                dve.tensor_tensor(h[:, t, :], scaled[:, :], shift[:, :], ALU.add).then_inc(h_ok, 1)

            dve.wait_ge(x_ld, 16)
            residual(0)
            dve.wait_ge(ld, 16 * 7)
            link(dve.tensor_scalar(scale[:, :], scale[:, :], 1.0, None, ALU.add))
            for t in range(TX):
                if t + 1 < TX:
                    residual(t + 1)
                modulate(t)
            for t in range(TX):
                dve.wait_ge(y_mm, t + 1)
                if t:
                    dve.wait_ge(x_ok, t)
                for half in range(2):
                    cols = slice(half * 512, (half + 1) * 512)
                    m = dve.tensor_tensor(gated[:, cols], y_ps[2 * (t % 2) + half][:, :], scales[:, cols], ALU.mult)
                m.then_inc(y_read, 1)
                dve.wait_ge(y_read, t + 1)
                link(dve.tensor_tensor(gated[:, :], gated[:, :], gate[:, :], ALU.mult))
                dve.tensor_tensor(x[:, t, :], x[:, t, :], gated[:, :], ALU.add).then_inc(x_ok, 1)
                norm(TX + t)


def routing_phase(nc, router_w, dram, keep):
    F, I = mybir.dt.float32, mybir.dt.int32
    ACT, ALU, AX = mybir.ActivationFunctionType, mybir.AluOpType, mybir.AxisListType
    ctx = ExitStack()
    with ctx:
        def sb(n, s, d=F):
            return ctx.enter_context(nc.sbuf_tensor(f"route_{n}", s, d))

        def ps(n, s):
            bank = ctx.enter_context(nc.psum_tensor(f"route_{n}_ps", [P, 512], F))
            if len(s) == 3:
                return bank[:, 0:s[1] * s[2]].rearrange("p (a b) -> p a b", a=s[1])
            return bank[:, 0:s[1]]

        sem = phase_semaphores(nc, ctx, "route")

        E = N_EXPERTS
        router = sb("router", [P, KD, E])
        before = sb("before", [P, P])
        ones = sb("ones", [P, P])
        expert_of = sb("expert_of", [P, E])
        pass_of = sb("pass_of", [P, MAX_PASSES_PAD])
        tokens = sb("tokens", [P, TX], I)
        x = sb("x", [P, TX, D])
        h = [sb(f"h{i}", [P, TOKENS]) for i in range(2 * KD)]
        logits = sb("logits", [P, TX, E])
        best = sb("best", [P, TX, E])
        best_at = sb("best_at", [P, TX, E], mybir.dt.uint32)
        best_f = sb("best_f", [P, TX, E])
        chosen = [sb(f"chosen{i}", [P, TX, E]) for i in range(TOP_K)]
        either = sb("either", [P, TX, E])
        ranks = sb("ranks", [P, TX, E])
        totals = sb("totals", [P, TX, E])
        running = sb("running", [P, TX + 1, E])
        small = {n: sb(n, [P, E]) for n in ("over", "passes", "any", "half", "room", "gap2")}
        ends = sb("ends", [P, E])
        starts = sb("starts", [P, E])
        slots = sb("slots", [P, TX, E])
        picked = sb("picked", [P, TX, E])
        slot_f = sb("slot_f", [P, TOP_K, TX])
        gap = sb("gap", [P, TX])
        gap_exp = sb("gap_exp", [P, TX])
        gap_1 = sb("gap_1", [P, TX])
        M = MAX_PASSES_PAD
        started, ended, here, part, counts = (sb(n, [P, M, E]) for n in ("started", "ended", "here", "part", "counts"))
        count, above, table_f = sb("count", [P, M]), sb("above", [P, M, len(WIDTHS)]), sb("table_f", [P, 2, M])
        width_of = sb("width_of", [P, len(WIDTHS)])
        half_of, halves = sb("half_of", [P, TOKENS // ROUND]), sb("halves", [P, E, TOKENS // ROUND])
        zeros = sb("zeros", [P, LISTED_TILES], I)
        turn_ps = [ps(f"turn{i}", [P, TOKENS]) for i in range(3)]
        logit_ps = ps("logit", [P, TX, E])
        rank_ps = ps("rank", [P, TX * E])
        total_ps = ps("total", [P, TX * E])

        ld, x_ld, turned, h_ok, logit_mm, chain, exp_ok, either_ok, ranked, slots_ok, zeroed, cleared, scattered, listed = (
            sem(n) for n in ("ld", "x_ld", "turned", "h_ok", "logit_mm", "chain", "exp_ok", "either_ok", "ranked",
                             "slots_ok", "zeroed", "cleared", "scattered", "listed"))
        gap_ok = sem("gap_ok")
        block = ctx.enter_context(nc.Block())

        @block.sync
        def _(sp):
            sp.dma_start(x[:, :, :], dram["xn"].rearrange("(t p) d -> p t d", p=P)).then_inc(x_ld, 16)
            for to, name in ((before[:, :], "before"), (ones[:, :], "ones"), (tokens[:, :], "tokens")):
                sp.dma_start(to, dram[name]).then_inc(ld, 16)
            sp.dma_start(expert_of[:, :], dram["count_up"][0:E].partition_broadcast(P)).then_inc(ld, 16)
            sp.dma_start(pass_of[:, :], dram["count_up"][0:M].partition_broadcast(P)).then_inc(ld, 16)
            sp.dma_start(width_of[:, :], dram["width_starts"].partition_broadcast(P)).then_inc(ld, 16)
            sp.dma_start(half_of[:, :], dram["half_starts"].partition_broadcast(P)).then_inc(ld, 16)
            sp.dma_start(router[:, :, :], router_w.rearrange("a (k p) e -> p (a k) e", p=P)).then_inc(ld, 16)
            sp.wait_ge(zeroed, 1)
            sp.dma_start(dram["slot_token"].rearrange("(p c) o -> p (c o)", p=P), zeros[:, :]).then_inc(cleared, 16)
            sp.wait_ge(scattered, 16 * TOP_K * TX)
            sp.dma_start(keep["token_of"][:, :], dram["slot_token"].rearrange("(c p) o -> p (c o)", p=P)).then_inc(listed, 16)
            sp.wait_ge(listed, 16)

        @block.gpsimd
        def _(pool):
            pool.memset(zeros[:, :], 0).then_inc(zeroed, 1)
            pool.wait_ge(ld, 16 * 8)
            pool.wait_ge(cleared, 16)
            pool.wait_ge(slots_ok, 1)
            for i in range(TOP_K):
                for t in range(TX):
                    pool.indirect_dma_start(dram["slot_token"], bass.IndirectOffsetOnAxis(ap=keep["slot"][:, i, t:t + 1], axis=0),
                                            tokens[:, t:t + 1], None).then_inc(scattered, 16)

        @block.tensor
        def _(pe):
            pe.wait_ge(x_ld, 16)
            for g in range(2):
                for k in range(KD):
                    i = g * KD + k
                    if i >= 3:
                        pe.wait_ge(h_ok, i - 2)
                    for t in range(4):
                        m = pe.transpose(turn_ps[i % 3][:, t * P:(t + 1) * P], x[:, 4 * g + t, k * P:(k + 1) * P],
                                         keep["ident"][:, :])
                    m.then_inc(turned, 1)
            pe.wait_ge(ld, 16 * 8)
            pe.wait_ge(h_ok, 2 * KD)
            for t in range(TX):
                for k in range(KD):
                    m = pe.matmul(logit_ps[:, t, :], h[t // 4 * KD + k][:, t % 4 * P:(t % 4 + 1) * P], router[:, k, :],
                                  start=(k == 0), stop=(k == KD - 1))
            m.then_inc(logit_mm, 1)
            pe.wait_ge(either_ok, 1)
            flat = either[:, :, :].rearrange("p t e -> p (t e)")
            pe.matmul(rank_ps[:, :], before[:, :], flat, start=True, stop=True)
            pe.matmul(total_ps[:, :], ones[:, :], flat, start=True, stop=True).then_inc(ranked, 1)

        @block.scalar
        def _(act):
            for i in range(2 * KD):
                k = i % KD
                act.wait_ge(turned, i + 1)
                act.activation(h[i][:, :], turn_ps[i % 3][:, :], ACT.Identity, scale=keep["moe_cols"][:, 0, k:k + 1],
                               bias=keep["moe_cols"][:, 1, k:k + 1]).then_inc(h_ok, 1)
            act.wait_ge(gap_ok, 1)
            act.activation(gap_exp[:, :], gap[:, :], ACT.Exp).then_inc(exp_ok, 1)

        @block.vector
        def _(dve):
            chain_n = [0]

            def link(ins):
                chain_n[0] += 1
                ins.then_inc(chain, 1)
                dve.wait_ge(chain, chain_n[0])

            def over_tiles(ap):
                return ap.unsqueeze(1).to_broadcast([P, TX, E])

            dve.wait_ge(logit_mm, 1)
            dve.wait_ge(ld, 16 * 8)
            link(dve.tensor_copy(logits[:, :, :], logit_ps[:, :, :]))
            for t in range(TX):
                m = dve.max(best[:, t, :], logits[:, t, :])
            link(m)
            for t in range(TX):
                m = dve.max_index(best_at[:, t, :], best[:, t, :], logits[:, t, :])
            link(m)
            link(dve.tensor_copy(best_f[:, :, :], best_at[:, :, :]))
            for i in range(TOP_K):
                m = dve.tensor_tensor(chosen[i][:, :, :], best_f[:, :, i:i + 1].to_broadcast([P, TX, E]),
                                      over_tiles(expert_of[:, :]), ALU.is_equal)
            link(m)
            dve.tensor_tensor(either[:, :, :], chosen[0][:, :, :], chosen[1][:, :, :], ALU.add).then_inc(either_ok, 1)
            dve.tensor_tensor(gap[:, :], best[:, :, 1], best[:, :, 0], ALU.subtract).then_inc(gap_ok, 1)
            dve.wait_ge(exp_ok, 1)
            link(dve.tensor_scalar(gap_1[:, :], gap_exp[:, :], 1.0, None, ALU.add))
            link(dve.reciprocal(keep["weight"][:, 0, :], gap_1[:, :]))
            dve.tensor_tensor(keep["weight"][:, 1, :], gap_exp[:, :], keep["weight"][:, 0, :], ALU.mult)
            dve.wait_ge(ranked, 1)
            dve.tensor_copy(totals[:, :, :].rearrange("p t e -> p (t e)"), total_ps[:, :])
            link(dve.memset(running[:, 0, :], 0.0))
            for t in range(TX):
                link(dve.tensor_tensor(running[:, t + 1, :], running[:, t, :], totals[:, t, :], ALU.add))
            link(dve.tensor_tensor(ranks[:, :, :].rearrange("p t e -> p (t e)"), rank_ps[:, :],
                                   running[:, 0:TX, :].rearrange("p t e -> p (t e)"), ALU.add))
            chose = running[:, TX, :]
            dve.tensor_scalar(small["over"][:, :], chose, float(TOKENS), None, ALU.is_gt)
            dve.tensor_tensor(halves[:, :, :], chose.unsqueeze(2).to_broadcast([P, E, TOKENS // ROUND]),
                              half_of[:, :].unsqueeze(1).to_broadcast([P, E, TOKENS // ROUND]), ALU.is_gt)
            link(dve.tensor_scalar(small["any"][:, :], chose, 0.0, None, ALU.is_gt))
            dve.reduce_sum(small["half"][:, :], halves[:, :, :], AX.X)
            link(dve.tensor_tensor(small["passes"][:, :], small["over"][:, :], small["any"][:, :], ALU.add))
            link(dve.tensor_scalar(small["gap2"][:, :], small["half"][:, :], float(-ROUND), float(TOKENS), ALU.mult, ALU.add))
            link(dve.tensor_tensor(small["gap2"][:, :], small["gap2"][:, :], small["over"][:, :], ALU.mult))
            link(dve.tensor_scalar(small["room"][:, :], small["gap2"][:, :], -1.0, float(TOKENS), ALU.mult, ALU.add))
            link(dve.tensor_copy(ends[:, 0:1], small["passes"][:, 0:1]))
            for e in range(1, E):
                link(dve.tensor_tensor(ends[:, e:e + 1], ends[:, e - 1:e], small["passes"][:, e:e + 1], ALU.add))
            link(dve.tensor_tensor(starts[:, :], ends[:, :], small["passes"][:, :], ALU.subtract))
            link(dve.tensor_tensor(picked[:, :, :], ranks[:, :, :], over_tiles(small["room"][:, :]), ALU.is_ge))
            link(dve.tensor_tensor(picked[:, :, :], picked[:, :, :], over_tiles(small["gap2"][:, :]), ALU.mult))
            link(dve.tensor_tensor(ranks[:, :, :], ranks[:, :, :], picked[:, :, :], ALU.add))
            link(dve.scalar_tensor_tensor(slots[:, :, :], over_tiles(starts[:, :]), float(TOKENS), ranks[:, :, :],
                                          ALU.mult, ALU.add))
            for i in range(TOP_K):
                link(dve.tensor_tensor(picked[:, :, :], slots[:, :, :], chosen[i][:, :, :], ALU.mult))
                link(dve.reduce_sum(slot_f[:, i, :], picked[:, :, :], AX.X))
            dve.tensor_copy(keep["slot"][:, :, :], slot_f[:, :, :]).then_inc(slots_ok, 1)
            by_pass = pass_of[:, :].unsqueeze(2).to_broadcast([P, M, E])

            def by_expert(ap):
                return ap.unsqueeze(1).to_broadcast([P, M, E])

            dve.tensor_tensor(started[:, :, :], by_pass, by_expert(starts[:, :]), ALU.is_ge)
            dve.tensor_tensor(ended[:, :, :], by_pass, by_expert(ends[:, :]), ALU.is_lt)
            link(dve.tensor_tensor(part[:, :, :], by_expert(starts[:, :]), by_pass, ALU.subtract))
            dve.tensor_tensor(here[:, :, :], started[:, :, :], ended[:, :, :], ALU.mult)
            link(dve.tensor_tensor(counts[:, :, :], part[:, :, :], by_expert(small["room"][:, :]), ALU.mult))
            link(dve.tensor_tensor(counts[:, :, :], counts[:, :, :], by_expert(chose), ALU.add))
            link(dve.tensor_tensor(counts[:, :, :], counts[:, :, :], by_expert(small["room"][:, :]), ALU.min))
            link(dve.tensor_tensor(counts[:, :, :], counts[:, :, :], here[:, :, :], ALU.mult))
            dve.reduce_sum(count[:, :], counts[:, :, :], AX.X)
            link(dve.tensor_tensor(part[:, :, :], here[:, :, :], by_expert(expert_of[:, :]), ALU.mult))
            dve.reduce_sum(table_f[:, 0, :], part[:, :, :], AX.X)
            link(dve.tensor_tensor(above[:, :, :], count[:, :].unsqueeze(2).to_broadcast([P, M, len(WIDTHS)]),
                                   width_of[:, :].unsqueeze(1).to_broadcast([P, M, len(WIDTHS)]), ALU.is_gt))
            link(dve.reduce_sum(table_f[:, 1, :], above[:, :, :], AX.X))
            link(dve.tensor_copy(table_f[:, 0, M - 1:M], ends[:, E - 1:E]))
            dve.tensor_copy(keep["table"][:, :, :], table_f[0:1, :, :])


def output_phase(nc, final_gain, dram, keep, out):
    F = mybir.dt.float32
    ACT, ALU = mybir.ActivationFunctionType, mybir.AluOpType
    ctx = ExitStack()
    with ctx:
        def sb(n, s, d=F):
            return ctx.enter_context(nc.sbuf_tensor(f"out_{n}", s, d))

        sem = phase_semaphores(nc, ctx, "out")

        gain = sb("gain", [P, D])
        x = sb("x", [P, TX, D])
        y = sb("y", [P, TX, TOP_K, D])
        square = sb("square", [P, D])
        result = [sb(f"result{i}", [P, D]) for i in range(2)]
        sums, mean, root, rstd = (sb(n, [P, TX]) for n in ("sums", "mean", "root", "rstd"))
        ld, y_ld, x_ok, squared, mean_ok, rooted, ready, done, chain = (
            sem(n) for n in ("ld", "y_ld", "x_ok", "squared", "mean_ok", "rooted", "ready", "done", "chain"))
        y_ld = [sem(f"y_ld{t}") for t in range(TX)]
        stored = [sem(f"stored{i}") for i in range(2)]
        block = ctx.enter_context(nc.Block())

        @block.sync
        def _(sp):
            sp.dma_start(gain[:, :], final_gain.partition_broadcast(P)).then_inc(ld, 16)
            sp.dma_start(x[:, :, :], dram["x3"].rearrange("(t p) d -> p t d", p=P)).then_inc(ld, 16)
            rows = out.rearrange("a (t p) d -> (a t) p d", p=P)
            for t in range(TX):
                sp.wait_ge(done, t + 1)
                sp.dma_start(rows[t], result[t % 2][:, :]).then_inc(stored[t % 2], 16)
            for i in range(2):
                sp.wait_ge(stored[i], 16 * (TX // 2))

        @block.gpsimd
        def _(pool):
            for t in range(TX):
                for i in range(TOP_K):
                    pool.indirect_dma_start(y[:, t, i, :], None, dram["y"],
                                            bass.IndirectOffsetOnAxis(ap=keep["slot"][:, i, t:t + 1], axis=0)).then_inc(y_ld[t], 16)

        @block.scalar
        def _(act):
            for t in range(TX):
                act.wait_ge(x_ok, t + 1)
                if t:
                    act.wait_ge(squared, t)
                act.activation(square[:, :], x[:, t, :], ACT.Square, accum_out=sums[:, t:t + 1]).then_inc(squared, 1)
                act.wait_ge(mean_ok, t + 1)
                act.activation(root[:, t:t + 1], mean[:, t:t + 1], ACT.Sqrt).then_inc(rooted, 1)

        @block.vector
        def _(dve):
            dve.wait_ge(ld, 32)

            def add(t):
                dve.wait_ge(y_ld[t], 16 * TOP_K)
                for i in range(TOP_K):
                    dve.scalar_tensor_tensor(x[:, t, :], y[:, t, i, :], keep["weight"][:, i, t:t + 1], x[:, t, :],
                                             ALU.mult, ALU.add).then_inc(chain if i == 0 else x_ok, 1)
                    if i == 0:
                        dve.wait_ge(chain, t + 1)

            def norm(t):
                dve.wait_ge(squared, t + 1)
                dve.tensor_scalar(mean[:, t:t + 1], sums[:, t:t + 1], 1.0 / D, EPS, ALU.mult, ALU.add).then_inc(mean_ok, 1)
                dve.wait_ge(rooted, t + 1)
                dve.reciprocal(rstd[:, t:t + 1], root[:, t:t + 1]).then_inc(ready, 1)
                dve.wait_ge(ready, t + 1)
                if t >= 2:
                    dve.wait_ge(stored[t % 2], 16 * (t // 2))
                dve.scalar_tensor_tensor(result[t % 2][:, :], x[:, t, :], rstd[:, t:t + 1], gain[:, :], ALU.mult, ALU.mult)\
                   .then_inc(done, 1)

            add(0)
            for t in range(TX):
                if t + 1 < TX:
                    add(t + 1)
                norm(t)


def expert_mlp_phase(nc, name, shape, weights, columns, ident, rows_of, y_rows, table):
    F, R = mybir.dt.float32, mybir.dt.float32r
    ACT, ALU, AX = mybir.ActivationFunctionType, mybir.AluOpType, mybir.AxisListType
    passes, C = shape
    gate_w, up_w, down_w = weights
    ctx = ExitStack()
    with ctx:
        def sb(n, s, d=F):
            return ctx.enter_context(nc.sbuf_tensor(f"{name}_{n}", s, d))

        def ps(n):
            return ctx.enter_context(nc.psum_tensor(f"{name}_{n}", [P, TOKENS], F))

        sem = phase_semaphores(nc, ctx, name)

        raw_g = sb("raw_g", [P, KD, CHUNK_FF])
        raw_u = sb("raw_u", [P, KD, CHUNK_FF])
        raw_d = sb("raw_d", [P, FB, D])
        g_hi = [sb(f"g_hi{i}", [P, KD, CHUNK_FF], R) for i in range(2)]
        g_lo = [sb(f"g_lo{i}", [P, KD, CHUNK_FF], R) for i in range(2)]
        u_hi = [sb(f"u_hi{i}", [P, KD, CHUNK_FF], R) for i in range(2)]
        u_lo = [sb(f"u_lo{i}", [P, KD, CHUNK_FF], R) for i in range(2)]
        d_hi = [sb(f"d_hi{i}", [P, FB, D], R) for i in range(2)]
        d_lo = [sb(f"d_lo{i}", [P, FB, D], R) for i in range(2)]
        x_rows = sb("x_rows", [P, TILES_PASS, D])
        x = sb("x", [P, KD, 2, TOKENS], R)
        h_full = sb("h_full", [P, FB, TOKENS])
        x_full = h_full
        h = [sb(f"h{i}", [P, FB, 2, TOKENS], R) for i in range(2)]
        y_t = sb("y_t", [P, KD, TOKENS])
        y_out = sb("y_out", [P, 2, D])
        g_ps = [ps(f"g{f}") for f in range(FB)]
        u_ps = [ps(f"u{f}") for f in range(FB)]
        y_ps = [ps(f"y{i}") for i in range(4)]
        x_ps = [g_ps[0], u_ps[0], g_ps[1], u_ps[1]]

        g_loaded, u_loaded, d_loaded, x_loaded, all_stored = (sem(n) for n in ("g_ld", "u_ld", "d_ld", "x_ld", "all_st"))
        y_stored = [sem(f"y_st{i}") for i in range(2)]
        g_rounded, u_rounded, d_rounded = (sem(n) for n in ("g_rnd", "u_rnd", "d_rnd"))
        g_split, u_split, d_split = (sem(n) for n in ("g_spl", "u_spl", "d_spl"))
        x_turned, x_rounded, x_whole, x_split = (sem(n) for n in ("x_t", "x_rnd", "x_wh", "x_spl"))
        g_done, u_done, silu_done, h_whole, h_rounded, h_split = (sem(n) for n in ("g_mm", "u_mm", "silu", "h_wh", "h_rnd", "h_spl"))
        halves_added, y_whole = sem("halves"), sem("y_wh")
        y_done, y_added, y_turned, y_left, y_right = (sem(n) for n in ("y_mm", "y_add", "y_t2", "y_l", "y_r"))
        W0, U0, X0, H0, Y0, A0, T0, O0 = 1, 2 * FB, KD, FB, 2 * KD, 4, KD, TILES_PASS

        block = ctx.enter_context(nc.Block())

        def each_pass(eng, body):
            if table is None:
                for p in range(passes):
                    body(p, None)
                return
            with eng.Fori(0, passes) as p:
                width_no = eng.value_load(table[0:1, 1, bass.ds(p, 1)], min_val=0, max_val=len(WIDTHS))
                with eng.If(width_no > 0):
                    body(p, width_no)
                    eng.nop()

        def each_width(eng, width_no, body):
            if width_no is None:
                body(TOKENS, False)
                return
            for v, width in enumerate(WIDTHS):
                with eng.If(width_no == v + 1):
                    body(width, 2 * width < TOKENS - 2 * ROUND)
            eng.nop()

        def has_next(p):
            return table is not None or p + 1 < passes

        def parity(p, c):
            return (c if table is not None else p * C + c) % 2

        def chunk_pairs(eng, p, first, last, body):
            pairs = (last - first + 1) // 2
            with eng.Fori(0, pairs) as i:
                body(2 * i + first, parity(p, first))
                body(2 * i + first + 1, parity(p, first + 1))
            for c in range(first + 2 * pairs, last + 1):
                body(c, parity(p, c))

        @block.sync
        def _(sp):
            def load(p, c, expert):
                def pick(w, lo_row, rows, lo_col, cols):
                    if table is None:
                        return w[0, bass.ds(lo_row, rows), bass.ds(lo_col, cols)]
                    return w[bass.ds(expert, 1), bass.ds(lo_row, rows), bass.ds(lo_col, cols)].rearrange("a r c -> (a r) c")

                n = p * C + c
                sp.wait_ge(g_split, n + W0)
                sp.dma_start(raw_g[:, :, :], pick(gate_w, 0, D, c * CHUNK_FF, CHUNK_FF)
                             .rearrange("(k p) f -> p k f", p=P)).then_inc(g_loaded, 16)
                sp.wait_ge(u_split, n + W0)
                sp.dma_start(raw_u[:, :, :], pick(up_w, 0, D, c * CHUNK_FF, CHUNK_FF)
                             .rearrange("(k p) f -> p k f", p=P)).then_inc(u_loaded, 16)
                sp.wait_ge(d_split, n + W0)
                sp.dma_start(raw_d[:, :, :], pick(down_w, c * CHUNK_FF, CHUNK_FF, 0, D)
                             .rearrange("(b p) d -> p b d", p=P)).then_inc(d_loaded, 16)

            def expert_of(p):
                if table is None:
                    return 0
                return sp.value_load(table[0:1, 0, bass.ds(p, 1)], min_val=0, max_val=gate_w.shape[0] - 1)

            def one_pass(p, _):
                expert = expert_of(p)
                with sp.Fori(1, C) as c:
                    load(p, c, expert)
                if has_next(p):
                    load(p + 1, 0, expert_of(p + 1))

            load(0, 0, expert_of(0))
            each_pass(sp, one_pass)

        @block.gpsimd
        def _(pool):
            pool.sem_inc(x_turned, X0)

            def rest_d(p, c, par):
                n = p * C + c
                pool.wait_ge(d_rounded, n + 1)
                pool.tensor_tensor(d_lo[par][:, :, :], raw_d[:, :, :], d_hi[par][:, :, :].bitcast(F), ALU.subtract)\
                    .then_inc(d_split, 1)

            def fetch(p):
                pool.wait_ge(x_turned, p * KD + X0)
                for t in range(TILES_PASS):
                    rows_of(pool, p, t, x_rows[:, t, :]).then_inc(x_loaded, 16)

            def one_pass(p, _):
                if has_next(p):
                    fetch(p + 1)
                chunk_pairs(pool, p, 1, C - 1, lambda c, par: rest_d(p, c, par))
                if has_next(p):
                    rest_d(p + 1, 0, parity(p + 1, 0))

            pool.sem_inc(d_split, W0)
            fetch(0)
            rest_d(0, 0, 0)
            each_pass(pool, one_pass)

        @block.tensor
        def _(pe):
            pe.sem_inc(u_done, U0)
            pe.sem_inc(y_done, Y0)

            def turn_rows(p, k):
                if k == 0:
                    pe.wait_ge(x_loaded, (p + 1) * TILES_PASS * 16)
                    pe.wait_ge(silu_done, p * C * FB + H0)
                    pe.wait_ge(h_whole, p * C * FB + H0)
                if k >= 4:
                    pe.wait_ge(x_whole, p * KD + k - 3)
                for t in range(TILES_PASS):
                    last = pe.transpose(x_ps[k % 4][:, t * P:(t + 1) * P], x_rows[:, t, k * P:(k + 1) * P],
                                        ident[:, :])
                last.then_inc(x_turned, 1)

            def product(bank, wh, wl, moving, width, narrow, start, stop):
                if narrow:
                    out = bank[:, 0:2 * width].rearrange("p (s w) -> p s w", s=2)
                    pe.matmul(out, wh, moving[:, :, 0:width], start=start, stop=False)
                    return pe.matmul(out, wl, moving[:, :, 0:width], start=False, stop=stop)
                pe.matmul(bank[:, 0:width], wh, moving[:, 0, 0:width], start=start, stop=False)
                pe.matmul(bank[:, 0:width], wh, moving[:, 1, 0:width], start=False, stop=False)
                return pe.matmul(bank[:, 0:width], wl, moving[:, 0, 0:width], start=False, stop=stop)

            def hidden(p, c, par, width, narrow):
                n = p * C + c
                if type(c) is int and c == 0:
                    pe.wait_ge(x_split, (p + 1) * KD + 2)
                for f in range(FB):
                    for bank, w_hi, w_lo, split, freed, done in (
                            (g_ps[f], g_hi[par], g_lo[par], g_split, silu_done, g_done),
                            (u_ps[f], u_hi[par], u_lo[par], u_split, h_whole, u_done)):
                        if f == 0:
                            pe.wait_ge(split, n + W0 + 1)
                        pe.wait_ge(freed, n * FB + f - FB + 1 + H0)
                        for k in range(KD):
                            wh, wl = (w[:, k, f * P:(f + 1) * P] for w in (w_hi, w_lo))
                            last = product(bank, wh, wl, x[:, k, :, :], width, narrow, k == 0, k == KD - 1)
                        last.then_inc(done, 1)

            def down(p, c, par, width, narrow, ready_next=False):
                n = p * C + c
                pe.wait_ge(y_left, p * TILES_PASS + O0)
                pe.wait_ge(y_right, p * TILES_PASS + O0)
                pe.wait_ge(d_split, n + W0 + 1)
                pe.wait_ge(h_split, (n + 1) * FB + H0)
                for db in range(KD):
                    if ready_next:
                        turn_rows(p + 1, db)
                    pe.wait_ge(y_added, n * KD + db - 3 + A0)
                    for f in range(FB):
                        wh, wl = (w[:, f, db * P:(db + 1) * P] for w in (d_hi[par], d_lo[par]))
                        last = product(y_ps[db % 4], wh, wl, h[par][:, f, :, :], width, narrow, f == 0, f == FB - 1)
                    last.then_inc(y_done, 1)

            def turn_result(p, width):
                tiles = -(-width // P)
                pe.wait_ge(y_whole, p + 1)
                for t in range(tiles):
                    if t >= 2:
                        pe.wait_ge(y_left, p * TILES_PASS + t - 1 + O0)
                        pe.wait_ge(y_right, p * TILES_PASS + t - 1 + O0)
                    for half in range(2):
                        bank = y_ps[(2 * t + half) % 4]
                        for j in range(4):
                            last = pe.transpose(bank[:, j * P:(j + 1) * P], y_t[:, 4 * half + j, t * P:(t + 1) * P],
                                                ident[:, :])
                        final = t == tiles - 1 and half == 1
                        last.then_inc(y_turned, KD - (2 * tiles - 1) if final else 1)

            def one_pass(p, width_no):
                def at(width, narrow):
                    hidden(p, 0, parity(p, 0), width, narrow)

                    def step(c, par):
                        hidden(p, c, par, width, narrow)
                        down(p, c - 1, 1 - par, width, narrow)

                    chunk_pairs(pe, p, 1, C - 1, step)
                    down(p, C - 1, parity(p, C - 1), width, narrow, has_next(p))
                    turn_result(p, width)

                each_width(pe, width_no, at)

            for k in range(KD):
                turn_rows(0, k)
            each_pass(pe, one_pass)

        @block.scalar
        def _(act):
            act.sem_inc(silu_done, H0)
            act.sem_inc(y_left, O0)
            for i in range(2):
                act.sem_inc(y_stored[i], 16)

            def round_up(n, par, raw, hi, loaded, rounded, freed, count):
                act.wait_ge(freed, count)
                act.wait_ge(loaded, (n + 1) * 16)
                act.activation(hi[par][:, :, :], raw[:, :, :], ACT.Copy).then_inc(rounded, 1)

            def round_g(p, c, par):
                n = p * C + c
                round_up(n, par, raw_g, g_hi, g_loaded, g_rounded, u_done, (n - 1) * FB + U0)

            def round_u(p, c, par):
                n = p * C + c
                round_up(n, par, raw_u, u_hi, u_loaded, u_rounded, u_done, (n - 1) * FB + U0)

            def round_d(p, c, par):
                n = p * C + c
                round_up(n, par, raw_d, d_hi, d_loaded, d_rounded, y_done, (n - 1) * KD + Y0)

            def silu(p, c, f, width, narrow):
                n = p * C + c
                if narrow:
                    act.wait_ge(halves_added, 2 * (n * FB + f) + 1)
                    gate = h_full[:, f, 0:width]
                else:
                    act.wait_ge(g_done, n * FB + f + 1)
                    act.wait_ge(h_split, n * FB + f - FB + 1 + H0)
                    gate = g_ps[f][:, 0:width]
                act.activation(h_full[:, f, 0:width], gate, ACT.Silu).then_inc(silu_done, 1)

            def round_hidden(p, c, par, f, width):
                n = p * C + c
                act.wait_ge(h_whole, n * FB + f + 1 + H0)
                act.wait_ge(y_done, (n - 1) * KD + Y0)
                act.activation(h[par][:, f, 0, 0:width], h_full[:, f, 0:width], ACT.Copy).then_inc(h_rounded, 1)

            def ready_tokens(p):
                act.wait_ge(u_done, p * C * FB + U0)
                act.wait_ge(h_split, p * C * FB + H0)
                for k in range(KD):
                    act.wait_ge(x_turned, p * KD + k + 1 + X0)
                    act.wait_ge(x_split, p * KD + k - 1 + 2)
                    act.activation(x_full[:, k % 2, :], x_ps[k % 4][:, :], ACT.Identity,
                                   scale=columns[:, 0, k:k + 1], bias=columns[:, 1, k:k + 1]).then_inc(x_whole, 1)
                    act.wait_ge(x_whole, p * KD + k + 1)
                    act.activation(x[:, k, 0, :], x_full[:, k % 2, :], ACT.Copy).then_inc(x_rounded, 1)

            def one_pass(p, width_no):
                def at(width, narrow):
                    def step(c, par, round_next=True):
                        if round_next:
                            round_g(p, c + 1, 1 - par)
                        silu(p, c, 0, width, narrow)
                        if round_next:
                            round_u(p, c + 1, 1 - par)
                        round_hidden(p, c, par, 0, width)
                        silu(p, c, 1, width, narrow)
                        round_hidden(p, c, par, 1, width)
                        if round_next:
                            round_d(p, c + 1, 1 - par)

                    chunk_pairs(act, p, 0, C - 2, step)
                    step(C - 1, parity(p, C - 1), has_next(p))
                    if has_next(p):
                        ready_tokens(p + 1)
                    tiles = -(-width // P)
                    for t in range(TILES_PASS):
                        if t < tiles:
                            act.wait_ge(y_turned, p * KD + 2 * t + 1 + T0)
                            act.wait_ge(y_stored[t % 2], (p * (TILES_PASS // 2) + t // 2 + 1) * 16)
                            act.activation(y_out[:, t % 2, 0:D // 2], y_ps[2 * t % 4][:, :], ACT.Copy)\
                               .then_inc(y_left, TILES_PASS - tiles + 1 if t == tiles - 1 else 1)
                            act.wait_ge(y_left, p * TILES_PASS + t + 1 + O0)
                            act.wait_ge(y_right, p * TILES_PASS + t + 1 + O0)
                            act.dma_start(y_rows(p, t), y_out[:, t % 2, :]).then_inc(y_stored[t % 2], 16)
                        else:
                            act.wait_ge(y_stored[t % 2], (p * (TILES_PASS // 2) + t // 2 + 1) * 16)
                            act.sem_inc(y_stored[t % 2], 16)

                each_width(act, width_no, at)

            round_g(0, 0, 0)
            round_u(0, 0, 0)
            round_d(0, 0, 0)
            ready_tokens(0)

            each_pass(act, one_pass)
            ran = passes if table is None else act.value_load(table[0:1, 0, 15:16], min_val=1, max_val=passes)
            for i in range(2):
                act.wait_ge(y_stored[i], (ran * (TILES_PASS // 2) + 1) * 16)
            act.sem_inc(all_stored, 1)

        @block.vector
        def _(dve):
            if table is not None:
                dve.memset(y_t[:, :, :], 0.0).then_inc(y_added, A0)
                dve.wait_ge(y_added, A0)
            else:
                dve.sem_inc(y_added, A0)
            dve.sem_inc(g_split, W0)
            dve.sem_inc(u_split, W0)
            dve.sem_inc(h_whole, H0)
            dve.sem_inc(h_split, H0)
            dve.sem_inc(x_split, 2)
            dve.sem_inc(y_right, O0)
            dve.sem_inc(y_turned, T0)

            def rest(n, par, raw, hi, lo, rounded, split):
                dve.wait_ge(rounded, n + 1)
                dve.tensor_tensor(lo[par][:, :, :], raw[:, :, :], hi[par][:, :, :].bitcast(F), ALU.subtract).then_inc(split, 1)

            def rest_g(p, c, par):
                rest(p * C + c, par, raw_g, g_hi, g_lo, g_rounded, g_split)

            def rest_u(p, c, par):
                rest(p * C + c, par, raw_u, u_hi, u_lo, u_rounded, u_split)

            def add_halves(to, bank, width):
                dve.reduce_sum(to, bank[:, 0:2 * width].rearrange("p (s w) -> p w s", s=2), AX.X).then_inc(halves_added, 1)

            def add_both(p, c, f, width):
                n = p * C + c
                dve.wait_ge(g_done, n * FB + f + 1)
                dve.wait_ge(h_split, n * FB + f - FB + 1 + H0)
                add_halves(h_full[:, f, 0:width], g_ps[f], width)
                dve.wait_ge(u_done, n * FB + f + 1 + U0)
                add_halves(h_full[:, f, TOKENS // 2:TOKENS // 2 + width], u_ps[f], width)

            def whole(p, c, f, width, narrow):
                n = p * C + c
                up = u_ps[f][:, 0:width]
                if narrow:
                    up = h_full[:, f, TOKENS // 2:TOKENS // 2 + width]
                    dve.wait_ge(halves_added, 2 * (n * FB + f) + 2)
                dve.wait_ge(silu_done, n * FB + f + 1 + H0)
                dve.wait_ge(u_done, n * FB + f + 1 + U0)
                dve.tensor_tensor(h_full[:, f, 0:width], h_full[:, f, 0:width], up, ALU.mult)\
                   .then_inc(h_whole, 1)

            def rest_hidden(p, c, par, f, width):
                n = p * C + c
                dve.wait_ge(h_rounded, n * FB + f + 1)
                dve.tensor_tensor(h[par][:, f, 1, 0:width], h_full[:, f, 0:width], h[par][:, f, 0, 0:width].bitcast(F),
                                  ALU.subtract).then_inc(h_split, 1)

            def add(p, c, db, cols, first=False):
                n = p * C + c
                dve.wait_ge(y_done, n * KD + db + 1 + Y0)
                gate = columns[:, 2, db:db + 1]
                if first:
                    dve.tensor_scalar(y_t[:, db, 0:cols], y_ps[db % 4][:, 0:cols], gate, None, ALU.mult)\
                       .then_inc(y_added, 1)
                else:
                    dve.wait_ge(y_added, (n - 1) * KD + db + 1 + A0)
                    dve.scalar_tensor_tensor(y_t[:, db, 0:cols], y_ps[db % 4][:, 0:cols], gate,
                                             y_t[:, db, 0:cols], ALU.mult, ALU.add).then_inc(y_added, 1)

            def split_tokens(p, k):
                dve.wait_ge(x_rounded, p * KD + k + 1)
                dve.tensor_tensor(x[:, k, 1, :], x_full[:, k % 2, :], x[:, k, 0, :].bitcast(F),
                                  ALU.subtract).then_inc(x_split, 1)

            def one_pass(p, width_no):
                def at(width, narrow):
                    cols = 2 * width if narrow else width
                    if not narrow and table is not None:
                        dve.sem_inc(halves_added, 2 * C * FB)

                    def step(c, par, share=2, rest_next=True):
                        if narrow:
                            add_both(p, c, 0, width)
                        if rest_next:
                            rest_g(p, c + 1, 1 - par)
                        whole(p, c, 0, width, narrow)
                        if rest_next:
                            rest_u(p, c + 1, 1 - par)
                        rest_hidden(p, c, par, 0, width)
                        if narrow:
                            add_both(p, c, 1, width)
                        whole(p, c, 1, width, narrow)
                        if share == 1:
                            dve.wait_ge(y_turned, p * KD + T0)
                        if share:
                            for db in range(2):
                                add(p, c - 1, db, cols, share == 1)
                        rest_hidden(p, c, par, 1, width)
                        if share:
                            for db in range(2, KD):
                                add(p, c - 1, db, cols, share == 1)

                    step(0, parity(p, 0), 0)
                    step(1, parity(p, 1), 1)
                    chunk_pairs(dve, p, 2, C - 2, step)
                    step(C - 1, parity(p, C - 1), 2, has_next(p))
                    for db in range(KD):
                        if has_next(p):
                            split_tokens(p + 1, db)
                        add(p, C - 1, db, cols)
                    if narrow:
                        dve.wait_ge(y_added, (p + 1) * C * KD + A0)
                        dve.tensor_tensor(y_t[:, :, 0:width], y_t[:, :, 0:width], y_t[:, :, width:cols], ALU.add)\
                           .then_inc(y_whole, 1)
                    else:
                        dve.wait_ge(y_added, (p + 1) * C * KD + A0)
                        dve.sem_inc(y_whole, 1)
                    tiles = -(-width // P)
                    for t in range(tiles):
                        dve.wait_ge(y_turned, p * KD + 2 * t + 2 + T0)
                        dve.wait_ge(y_stored[t % 2], (p * (TILES_PASS // 2) + t // 2 + 1) * 16)
                        dve.tensor_copy(y_out[:, t % 2, D // 2:D], y_ps[(2 * t + 1) % 4][:, :])\
                           .then_inc(y_right, TILES_PASS - tiles + 1 if t == tiles - 1 else 1)

                each_width(dve, width_no, at)

            rest_g(0, 0, 0)
            rest_u(0, 0, 0)
            for k in range(KD):
                split_tokens(0, k)

            each_pass(dve, one_pass)


def backbone(nc, a, tables, out):
    F, R, I = mybir.dt.float32, mybir.dt.float32r, mybir.dt.int32
    dram = dict(tables)
    for name, shape, dtype in (("pool_mod", [3, D], F), ("x1", [SEQ, D], F), ("x3", [SEQ, D], F), ("xn", [SEQ, D], F),
                               ("y_dense", [SEQ, D], F), ("y", [SLOT_TILES * P, D], F), ("slot_token", [LISTED_TILES * P, 1], I)):
        dram[name] = nc.dram_tensor(f"scratch_{name}", shape, dtype).ap()
    outer = ExitStack()
    with outer:
        outer.enter_context(nc.allow_non_contiguous_dma(reason="small vectors and tables, one number to a partition"))

        def sb(stack, n, s, d=F):
            return stack.enter_context(nc.sbuf_tensor(n, s, d))

        keep = {
            "ident": sb(outer, "ident", [P, P]),
            "ffn_cols": sb(outer, "ffn_cols", [P, 3, KD]),
            "moe_cols": sb(outer, "moe_cols", [P, 3, KD]),
            "weight": sb(outer, "weight", [P, TOP_K, TX]),
            "slot": sb(outer, "slot", [P, TOP_K, TX], I),
            "token_of": sb(outer, "token_of", [P, LISTED_TILES], I),
            "token_now": sb(outer, "token_now", [P, TILES_PASS], I),
            "table": sb(outer, "table", [1, 2, MAX_PASSES_PAD], I),
        }
        picked = outer.enter_context(nc.semaphore("picked"))
        gathered = outer.enter_context(nc.semaphore("gathered"))

        right, right_short, left, tokens_side = ExitStack(), ExitStack(), ExitStack(), ExitStack()
        with left:
            keep["attn_cols"] = left.enter_context(nc.sbuf_tensor("attn_cols", [P, 4, KD], F))
            keep["gate0"] = left.enter_context(nc.sbuf_tensor("gate0", [P, D], F))
            with right:
                with tokens_side:
                    for name in ("x_hi", "x_lo"):
                        keep[name] = tokens_side.enter_context(nc.sbuf_tensor(name, [P, KD, SEQ + CTX_LEN], R))
                    modulation_phase(nc, a, dram, keep)
                    for name, shape in (("u", [P, TX, D // 2]), ("v_gm", [P, TX, D // 2]), ("v_sums", [P, TX, 2])):
                        keep[name] = right.enter_context(nc.sbuf_tensor(name, shape, F, side="right"))
                    for name, shape in (("q_t", [P, Q_HEADS // 2, SEQ]), ("k_t", [P, SEQ + CTX_LEN]),
                                        ("v", [P, TX + TC, KV_WIDTH])):
                        keep[name] = right_short.enter_context(nc.sbuf_tensor(name, shape, F, side="right"))
                    projection_phase(nc, a["w_in"], dram, keep)
                keep["att"] = left.enter_context(nc.sbuf_tensor("att", [P, TX, D // 2], F))
                with right_short:
                    attention_phase(nc, a["attn_sink"], dram, keep)
                mixer_output_phase(nc, {"x": a["x"], "w_s": a["gm_w_s"], "b_s": a["gm_b_s"], "gain": a["gm_gain"],
                                        "w_out": a["w_out"]}, dram, keep)

        def tile_rows(y):
            return lambda p, t: y[bass.ds((p * TILES_PASS + t) * P, P), :]

        def token_tile(pool, p, t, to):
            return pool.dma_start(to, dram["xn"][(p * TILES_PASS + t) * P:(p * TILES_PASS + t + 1) * P, :])

        expert_mlp_phase(nc, "ffn", (SEQ // TOKENS, FF_DENSE // CHUNK_FF), (a["ffn_w_gate"], a["ffn_w_up"], a["ffn_w_down"]),
                         keep["ffn_cols"], keep["ident"], token_tile, tile_rows(dram["y_dense"]), None)
        pool_phase(nc, a["pool_w"], a["pool_scale"], dram)
        routing_phase(nc, a["router_w"], dram, keep)

        def slot_tile(pool, p, t, to):
            pool.tensor_copy(keep["token_now"][:, t:t + 1], keep["token_of"][:, bass.ds(p * TILES_PASS + t, 1)]).then_inc(picked, 1)
            pool.wait_ge(picked, p * TILES_PASS + t + 1)
            pool.sem_inc(gathered, 1)
            return pool.indirect_dma_start(to, None, dram["xn"], bass.IndirectOffsetOnAxis(ap=keep["token_now"][:, t:t + 1], axis=0))

        experts = tuple(w.rearrange("a e r c -> (a e) r c") for w in (a["moe_w_gate"], a["moe_w_up"], a["moe_w_down"]))
        expert_mlp_phase(nc, "moe", (MAX_PASSES, FF_EXPERT // CHUNK_FF), experts, keep["moe_cols"], keep["ident"], slot_tile,
                         tile_rows(dram["y"]), keep["table"])
        output_phase(nc, a["final_gain"], dram, keep, out)


_INS = ["x", "c", "ctx", "c_ctx", "w_ada", "b_ada", "w_in", "attn_sink", "gm_gain", "gm_w_s", "gm_b_s", "w_out",
        "ffn_w_gate", "ffn_w_up", "ffn_w_down", "pool_w", "pool_scale", "router_w",
        "moe_w_gate", "moe_w_up", "moe_w_down", "final_gain"]


def kernel(**inputs):
    import concourse.bacc as bacc
    from concourse.bass_utils import run_bass_kernel_spmd

    nc = bacc.Bacc("TRN2", target_bir_lowering=False, num_devices=1, dynamic_dma_scratch_size=8192)
    arrays, aps, tables = {}, {}, {}

    def declare(name, a):
        arrays[name] = a
        return nc.dram_tensor(name, a.shape, mybir.dt.from_np(a.dtype), kind="ExternalInput").ap()

    for name in _INS:
        aps[name] = declare(f"in_{name}", np.ascontiguousarray(inputs[name]))
    for name, table in constants().items():
        tables[name] = declare(f"table_{name}", table)
    out = nc.dram_tensor("out", [1, SEQ, D], mybir.dt.float32, kind="ExternalOutput").ap()
    backbone(nc, aps, tables, out)
    r = run_bass_kernel_spmd(nc, [arrays], core_ids=[0])
    return r.results[0]["out"]
```

```python
from contextlib import ExitStack

import numpy as np

import concourse.bass as bass
from concourse import mybir

P = 128
D = 1024
SEQ = 1024
CTX_LEN = 256
DEPTH = 2
GRID_W = 64
EPS = 1e-6
NEG_INF = -1e30
HEAD = 64
Q_HEADS = D // 2 // HEAD
KV_WIDTH = Q_HEADS // 4 * HEAD
Q_END = Q_HEADS * HEAD
KV_END = Q_END + 2 * KV_WIDTH
GM_GROUPS = 8
WINDOW = 128
POOL_SIZES = (2, 4, 8, 16)
ROPE_BASE = 10000.0
FF_DENSE = 2816
FF_EXPERT = 3584
N_EXPERTS = 8
TOP_K = 2

REST_VECTORS = [(0, v) for v in range(2, 6)] + [(1, v) for v in range(6)]

KD = D // P
TX = SEQ // P
TC = CTX_LEN // P
CHUNK_FF = 256
FB = CHUNK_FF // P
TOKENS = 512
TILES_PASS = TOKENS // P
ROUND = 32
WIDTHS = (128, 160) + tuple(range(256, TOKENS + 1, ROUND))
MAX_PASSES = N_EXPERTS + (TOP_K * SEQ - N_EXPERTS) // TOKENS
MAX_PASSES_PAD = 16
SLOT_TILES = MAX_PASSES * TILES_PASS
LISTED_TILES = SLOT_TILES + TILES_PASS


def constants():
    f = np.float32
    out = {"ident": np.eye(P, dtype=f), "ones": np.ones((P, P), f)}
    axis = HEAD // 2
    inv = (f(ROPE_BASE) ** (-np.arange(0, axis, 2, dtype=f) / f(axis))).astype(f)
    t = np.arange(SEQ)
    angle = np.stack([(t // GRID_W).astype(f)[:, None] * inv, (t % GRID_W).astype(f)[:, None] * inv], 1)
    cos, sin = np.cos(angle).astype(f), np.sin(angle).astype(f)
    out["cos"] = np.stack([cos, cos], 2).reshape(SEQ, HEAD)
    out["sin"] = np.stack([-sin, sin], 2).reshape(SEQ, HEAD)
    q, k = np.arange(P)[:, None], np.arange(-P, 2 * P)[None, :]
    out["mask"] = np.where(abs(k - q) <= WINDOW, 0.0, NEG_INF).astype(f)
    full = np.zeros((len(POOL_SIZES), SEQ, SEQ), f)
    for g, w in enumerate(POOL_SIZES):
        for i in range(SEQ):
            lo, hi = max(i - w // 2, 0), min(i + (w - 1 - w // 2), SEQ - 1) + 1
            full[g, lo:hi, i] = f(1.0) / f(hi - lo)
            full[g, i, i] -= f(1.0)
    tile = [slice(i * P, (i + 1) * P) for i in range(TX)]
    out["band"] = np.stack([full[:, tile[i], tile[i]] for i in (0, 1, TX - 1)], 1)
    out["edge"] = np.stack([full[:, tile[0], tile[1]], full[:, tile[1], tile[0]]], 1)
    out["before"] = np.triu(np.ones((P, P), f), 1)
    out["count_up"] = np.arange(MAX_PASSES_PAD, dtype=f)
    out["width_starts"] = np.array((0,) + WIDTHS[:-1], f)
    out["half_starts"] = (np.arange(TOKENS // ROUND) * 2 * ROUND).astype(f)
    out["tokens"] = (np.arange(TX)[None, :] * P + np.arange(P)[:, None]).astype(np.int32)
    return {name: np.ascontiguousarray(a) for name, a in out.items()}


def phase_semaphores(nc, ctx, phase):
    used = []

    def clear():
        nc.clear_and_free_semaphores(used)
        nc.all_engine_barrier(sem_only=True)

    def sem(name):
        used.append(nc.alloc_semaphore(f"{phase}_{name}"))
        return used[-1]

    ctx.callback(clear)
    return sem


def modulation_phase(nc, mod, dram, keep):
    F, R = mybir.dt.float32, mybir.dt.float32r
    ACT, ALU = mybir.ActivationFunctionType, mybir.AluOpType
    ctx = ExitStack()
    with ctx:
        def sb(n, s, d=F):
            return ctx.enter_context(nc.sbuf_tensor(f"mod_{n}", s, d))

        def ps(n, s):
            bank = ctx.enter_context(nc.psum_tensor(f"mod_{n}_ps", [P, 512], F))
            if len(s) == 3:
                return bank[:, 0:s[1] * s[2]].rearrange("p (a b) -> p a b", a=s[1])
            return bank[:, 0:s[1]]

        sem = phase_semaphores(nc, ctx, "mod")

        WBUF = 2
        w_sb = [sb(f"w{i}", [P, KD, 512]) for i in range(WBUF)]
        b_sb = [sb(f"b{i}", [P, 512]) for i in range(WBUF)]
        x_sb = sb("x", [P, TX + TC, D])
        c_col = sb("c", [P, 2, KD])
        c_silu = keep["c_silu"]
        lhs_mixed = sb("lhs_mixed", [P, KD, P])
        wide = [sb(f"wide{i}", [P, 512]) for i in range(2)]
        square = sb("square", [P, D])
        sums = sb("sums", [P, TX + TC])
        mean = sb("mean", [P, TX + TC])
        root = sb("root", [P, TX + TC])
        rstd = sb("rstd", [P, TX + TC])
        x_full = sb("x_full", [P, 2, TOKENS])
        wide_ps = [ps(f"wide{i}", [P, 512]) for i in range(2)]
        col_ps = [ps(f"col{i}", [P, 4, 2]) for i in range(2)]
        turn_ps = [ps(f"turn{i}", [P, TOKENS]) for i in range(3)]

        small_ld, x_ld = sem("small_ld"), [sem(f"x_ld{i}") for i in range(3)]
        w_ld = [sem(f"w_ld{i}") for i in range(WBUF)]
        silu, lhs, wide_mm, wide_out, col_mm, col_out = (
            sem(n) for n in ("silu", "lhs", "wide_mm", "wide_out", "col_mm", "col_out"))
        squared, rooted, dchain, normed = sem("squared"), sem("rooted"), sem("dchain"), sem("normed")
        turned, whole, rounded, split = sem("turned"), sem("whole"), sem("rounded"), sem("split")

        CHUNKS = 2 * D // 512
        GROUPS = [(0, 4, 0), (4, 4, 0), (TX, TC, 2)]

        block = ctx.enter_context(nc.Block())

        @block.sync
        def _(sp):
            sp.dma_start(c_col[:, 0, :], mod["c"].rearrange("a (k p) -> p (a k)", p=P)).then_inc(small_ld, 16)
            sp.dma_start(c_col[:, 1, :], mod["c_ctx"].rearrange("(k p) -> p k", p=P)).then_inc(small_ld, 16)
            sp.dma_start(keep["ident"][:, :], dram["ident"]).then_inc(small_ld, 16)
            for n in range(CHUNKS):
                if n >= WBUF:
                    sp.wait_ge(wide_out, n - WBUF + 1)
                s = slice(n * 512, (n + 1) * 512)
                sp.dma_start(w_sb[n % WBUF][:, :, :], mod["w_ada"][0, :, s].rearrange("(k p) f -> p k f", p=P))\
                  .then_inc(w_ld[n % WBUF], 16)
                sp.dma_start(b_sb[n % WBUF][:, :], mod["b_ada"][0, s].partition_broadcast(P)).then_inc(w_ld[n % WBUF], 16)

        @block.gpsimd
        def _(pool):
            x_tiles = mod["x"].rearrange("a (t p) d -> p (a t) d", p=P)
            pool.dma_start(x_sb[:, 0:4, :], x_tiles[:, 0:4, :]).then_inc(x_ld[0], 16)
            pool.dma_start(x_sb[:, 4:TX, :], x_tiles[:, 4:TX, :]).then_inc(x_ld[1], 16)
            pool.dma_start(x_sb[:, TX:TX + TC, :], mod["ctx"].rearrange("a (t p) d -> p (a t) d", p=P)).then_inc(x_ld[2], 16)

        @block.tensor
        def _(pe):
            def products(n):
                pe.wait_ge(w_ld[n % WBUF], 32 * (n // WBUF + 1))
                if n == 0:
                    pe.wait_ge(lhs, 1)
                if n >= 2:
                    pe.wait_ge(wide_out, n - 1)
                for k in range(KD):
                    last = pe.matmul(wide_ps[n % 2][:, :], lhs_mixed[:, k, :], w_sb[n % WBUF][:, k, :],
                                     start=(k == 0), stop=(k == KD - 1))
                last.then_inc(wide_mm, 1)

            def columns(n):
                pe.wait_ge(wide_out, n + 1)
                if n >= 2:
                    pe.wait_ge(col_out, n - 1)
                for j in range(4):
                    last = pe.matmul(col_ps[n % 2][:, j, :], wide[n % 2][:, j * P:(j + 1) * P],
                                     keep["ident"][:, 0:65:64], start=True, stop=True)
                last.then_inc(col_mm, 1)

            def turn():
                i = 0
                for g, (first, tiles, _) in enumerate(GROUPS):
                    pe.wait_ge(normed, first + tiles)
                    for k in range(KD):
                        if i >= 3:
                            pe.wait_ge(whole, i - 2)
                        for t in range(tiles):
                            last = pe.transpose(turn_ps[i % 3][:, t * P:(t + 1) * P],
                                                x_sb[:, first + t, k * P:(k + 1) * P], keep["ident"][:, :])
                        last.then_inc(turned, 1)
                        i += 1

            pe.wait_ge(small_ld, 48)
            for n in range(CHUNKS):
                products(n)
                if n >= 1:
                    columns(n - 1)
            columns(CHUNKS - 1)
            turn()

        @block.scalar
        def _(act):
            act.wait_ge(small_ld, 48)
            act.activation(c_silu[:, :, :], c_col[:, :, :], ACT.Silu).then_inc(silu, 1)
            for t in range(TX + TC):
                act.wait_ge(x_ld[min(t // 4, 2)], 16)
                if t:
                    act.wait_ge(squared, t)
                act.activation(square[:, :], x_sb[:, t, :], ACT.Square, accum_out=sums[:, t:t + 1]).then_inc(squared, 1)
            act.wait_ge(dchain, 1)
            act.activation(root[:, :], mean[:, :], ACT.Sqrt).then_inc(rooted, 1)
            act.wait_ge(dchain, 2)
            for t in range(TX + TC):
                act.activation(x_sb[:, t, :], x_sb[:, t, :], ACT.Copy, scale=rstd[:, t:t + 1]).then_inc(normed, 1)
            act.wait_ge(col_out, CHUNKS)
            i = 0
            for first, tiles, col in GROUPS:
                w = tiles * P
                for k in range(KD):
                    act.wait_ge(turned, i + 1)
                    if i >= 2:
                        act.wait_ge(split, i - 1)
                    act.activation(x_full[:, i % 2, 0:w], turn_ps[i % 3][:, 0:w], ACT.Identity,
                                   scale=keep["attn_cols"][:, col, k:k + 1], bias=keep["attn_cols"][:, col + 1, k:k + 1])\
                       .then_inc(whole, 1)
                    act.wait_ge(whole, i + 1)
                    act.activation(keep["x_hi"][:, k, first * P:first * P + w], x_full[:, i % 2, 0:w], ACT.Copy)\
                       .then_inc(rounded, 1)
                    i += 1

        @block.vector
        def _(dve):
            dve.wait_ge(silu, 1)
            dve.tensor_copy(lhs_mixed[:, :, 0:P // 2], c_silu[:, 0, :].unsqueeze(2).to_broadcast([P, KD, P // 2]))
            dve.tensor_copy(lhs_mixed[:, :, P // 2:P], c_silu[:, 1, :].unsqueeze(2).to_broadcast([P, KD, P // 2]))\
               .then_inc(lhs, 1)

            def sums_of(n):
                dve.wait_ge(wide_mm, n + 1)
                if n >= 2:
                    dve.wait_ge(col_mm, n - 1)
                dve.tensor_tensor(wide[n % 2][:, :], wide_ps[n % 2][:, :], b_sb[n % WBUF][:, :], ALU.add).then_inc(wide_out, 1)

            def columns_of(n):
                dve.wait_ge(col_mm, n + 1)
                vec, half = n // 2, (n % 2) * 4
                dve.tensor_scalar(keep["attn_cols"][:, 1 - vec, half:half + 4], col_ps[n % 2][:, :, 0], float(vec), None, ALU.add)
                dve.tensor_scalar(keep["attn_cols"][:, 3 - vec, half:half + 4], col_ps[n % 2][:, :, 1], float(vec), None, ALU.add)\
                   .then_inc(col_out, 1)

            def chunk(n):
                sums_of(n)
                if n >= 1:
                    columns_of(n - 1)

            chunk(0)
            dve.wait_ge(squared, TX + TC)
            dve.tensor_scalar(mean[:, :], sums[:, :], 1.0 / D, EPS, ALU.mult, ALU.add).then_inc(dchain, 1)
            dve.wait_ge(rooted, 1)
            dve.reciprocal(rstd[:, :], root[:, :]).then_inc(dchain, 1)
            for n in range(1, CHUNKS):
                chunk(n)
            columns_of(CHUNKS - 1)
            i = 0
            for first, tiles, _ in GROUPS:
                for k in range(KD):
                    dve.wait_ge(rounded, i + 1)
                    here = slice(first * P, (first + tiles) * P)
                    dve.tensor_tensor(keep["x_lo"][:, k, here], x_full[:, i % 2, 0:tiles * P],
                                      keep["x_hi"][:, k, here].bitcast(F), ALU.subtract).then_inc(split, 1)
                    i += 1


def projection_phase(nc, w_in, dram, keep):
    F, R = mybir.dt.float32, mybir.dt.float32r
    ACT, ALU = mybir.ActivationFunctionType, mybir.AluOpType
    ctx = ExitStack()
    with ctx:
        def sb(n, s, d=F):
            return ctx.enter_context(nc.sbuf_tensor(f"proj_{n}", s, d))

        def ps(n, s):
            bank = ctx.enter_context(nc.psum_tensor(f"proj_{n}_ps", [P, 512], F))
            if len(s) == 3:
                return bank[:, 0:s[1] * s[2]].rearrange("p (a b) -> p a b", a=s[1])
            return bank[:, 0:s[1]]

        sem = phase_semaphores(nc, ctx, "proj")

        W = 256
        raw = [sb(f"raw{i}", [P, KD, W]) for i in range(2)]
        w_hi = [sb(f"w_hi{i}", [P, KD, W], R) for i in range(2)]
        w_lo = [sb(f"w_lo{i}", [P, KD, W], R) for i in range(2)]
        cos = sb("cos", [P, TX, HEAD])
        sin = sb("sin", [P, TX, HEAD])
        with_cos = sb("with_cos", [P, W])
        with_sin = sb("with_sin", [P, W])
        roped = [sb(f"roped{i}", [P, W]) for i in range(2)]
        square = sb("square", [P, W])
        out_ps = [ps(f"out{i}", [P, W]) for i in range(4)]
        turn_ps = [ps(f"turn{i}", [P, 2, P]) for i in range(2)]

        tab_ld, raw_ld = sem("tab_ld"), [sem(f"raw_ld{i}") for i in range(2)]
        rounded, split, mm, turned, turned_out, ready, chain, squared = (
            sem(n) for n in ("rounded", "split", "mm", "turned", "turned_out", "ready", "chain", "squared"))
        left = {"dve": sem("left_dve"), "act": sem("left_act")}

        PIECES = ["u0", "q0", "q1", "kv", "u1", "v0", "v1"]
        UNITS = [(i, t) for i, piece in enumerate(PIECES) for t in range(TX + TC if piece == "kv" else TX)]
        who = ["act" if PIECES[i][0] in "uv" else "dve" for i, _ in UNITS]
        nth = [who[:u + 1].count(who[u]) for u in range(len(UNITS))]
        turns = [u for u, w in enumerate(who) if w == "dve"]
        last_unit = [max(u for u, (j, _) in enumerate(UNITS) if j == i) for i in range(len(PIECES))]
        block = ctx.enter_context(nc.Block())

        @block.sync
        def _(sp):
            rows = w_in.rearrange("a (k p) f -> p (a k) f", p=P)
            for i, piece in enumerate(PIECES):
                if i >= 2:
                    sp.wait_ge(split, i - 1)
                to, done = raw[i % 2], raw_ld[i % 2]
                if piece[0] == "q":
                    a = int(piece[1])
                    for side in range(2):
                        for j in range(2):
                            h = side * Q_HEADS // 2 + 2 * a + j
                            at = (2 * j + side) * HEAD
                            sp.dma_start(to[:, :, at:at + HEAD], rows[:, :, h * HEAD:(h + 1) * HEAD]).then_inc(done, 16)
                else:
                    at = {"kv": Q_END, "u0": KV_END, "u1": KV_END + W, "v0": KV_END + 2 * W, "v1": KV_END + 3 * W}[piece]
                    sp.dma_start(to[:, :, :], rows[:, :, at:at + W]).then_inc(done, 16)
                if i == 0:
                    sp.dma_start(cos[:, :, :], dram["cos"].rearrange("(t p) f -> p t f", p=P)).then_inc(tab_ld, 16)
                    sp.dma_start(sin[:, :, :], dram["sin"].rearrange("(t p) f -> p t f", p=P)).then_inc(tab_ld, 16)

        def loads(i):
            return 16 * sum(4 if PIECES[j][0] == "q" else 1 for j in range(i % 2, i + 1, 2))

        @block.tensor
        def _(pe):
            def turn(u):
                if who[u] == "act":
                    return
                i = turns.index(u)
                pe.wait_ge(ready, i + 1)
                if i >= 2:
                    pe.wait_ge(turned_out, i - 1)
                for j in range(2 if PIECES[UNITS[u][0]][0] == "q" else 1):
                    last = pe.transpose(turn_ps[i % 2][:, j, :], roped[i % 2][:, j * P:(j + 1) * P], keep["ident"][:, :])
                last.then_inc(turned, 1)

            for u, (i, t) in enumerate(UNITS):
                pe.wait_ge(split, i + 1)
                if u >= 4:
                    pe.wait_ge(left[who[u - 4]], nth[u - 4])
                bank = out_ps[u % 4]
                here = slice(t * P, (t + 1) * P)
                for k in range(KD):
                    wh, wl = w_hi[i % 2][:, k, :], w_lo[i % 2][:, k, :]
                    pe.matmul(bank[:, :], keep["x_hi"][:, k, here], wh, start=(k == 0), stop=False)
                    pe.matmul(bank[:, :], keep["x_hi"][:, k, here], wl, start=False, stop=False)
                    last = pe.matmul(bank[:, :], keep["x_lo"][:, k, here], wh, start=False, stop=(k == KD - 1))
                last.then_inc(mm, 1)
                if u >= 1:
                    turn(u - 1)
            turn(len(UNITS) - 1)

        @block.scalar
        def _(act):
            def round_piece(i):
                act.wait_ge(raw_ld[i % 2], loads(i))
                if i >= 2:
                    act.wait_ge(mm, last_unit[i - 2] + 1)
                act.activation(w_hi[i % 2][:, :, :], raw[i % 2][:, :, :], ACT.Copy).then_inc(rounded, 1)

            def copy_turned(u):
                i = turns.index(u)
                piece, t = PIECES[UNITS[u][0]], UNITS[u][1]
                act.wait_ge(turned, i + 1)
                if piece[0] == "q":
                    to = keep["q_t"][:, 2 * int(piece[1]):2 * int(piece[1]) + 2, t * P:(t + 1) * P]
                    act.activation(to, turn_ps[i % 2][:, :, :], ACT.Copy, scale=float(HEAD) ** -0.5).then_inc(turned_out, 1)
                else:
                    act.activation(keep["k_t"][:, t * P:(t + 1) * P], turn_ps[i % 2][:, 0, :], ACT.Copy).then_inc(turned_out, 1)

            round_piece(0)
            gelus = 0
            for u, (i, t) in enumerate(UNITS):
                if t == 1 and i + 1 < len(PIECES):
                    round_piece(i + 1)
                if u >= 2 and who[u - 2] == "dve":
                    copy_turned(u - 2)
                if who[u] == "act":
                    act.wait_ge(mm, u + 1)
                    half = int(PIECES[i][1])
                    to = (keep["u"] if PIECES[i][0] == "u" else keep["v_gm"])[:, t, half * W:(half + 1) * W]
                    act.activation(to, out_ps[u % 4][:, :], ACT.Gelu_apprx_tanh).then_inc(left["act"], 1)
                    if PIECES[i][0] == "v":
                        act.wait_ge(left["act"], nth[u])
                        if gelus:
                            act.wait_ge(squared, gelus)
                        gelus += 1
                        act.activation(square[:, :], to, ACT.Square, accum_out=keep["v_sums"][:, t, half:half + 1])\
                           .then_inc(squared, 1)

        @block.vector
        def _(dve):
            chain_n = [0]

            def link(ins):
                chain_n[0] += 1
                ins.then_inc(chain, 1)
                dve.wait_ge(chain, chain_n[0])

            def rest(i):
                dve.wait_ge(rounded, i + 1)
                dve.tensor_tensor(w_lo[i % 2][:, :, :], raw[i % 2][:, :, :], w_hi[i % 2][:, :, :].bitcast(F), ALU.subtract)\
                   .then_inc(split, 1)

            def rotate(u, t, heads, to):
                n = heads * HEAD
                bank = out_ps[u % 4]
                dve.tensor_tensor(with_cos[:, 0:n].rearrange("p (h f) -> p h f", h=heads),
                                  bank[:, 0:n].rearrange("p (h f) -> p h f", h=heads),
                                  cos[:, t:t + 1, :].to_broadcast([P, heads, HEAD]), ALU.mult)
                halves = "p (h a s f) -> p h a s f"
                for s in range(2):
                    o = with_sin[:, 0:n].rearrange(halves, h=heads, a=2, s=2)[:, :, :, s, :]
                    x = bank[:, 0:n].rearrange(halves, h=heads, a=2, s=2)[:, :, :, 1 - s, :]
                    y = sin[:, t:t + 1, :].rearrange("p o (a s f) -> p o a s f", a=2, s=2)[:, :, :, s, :]
                    last = dve.tensor_tensor(o, x, y.to_broadcast([P, heads, 2, HEAD // 4]), ALU.mult)
                link(last)
                return dve.tensor_tensor(to, with_cos[:, 0:n], with_sin[:, 0:n], ALU.add)

            rest(0)
            dve.wait_ge(tab_ld, 32)
            for u, (i, t) in enumerate(UNITS):
                if t == 1 and i + 1 < len(PIECES):
                    rest(i + 1)
                if who[u] != "dve":
                    continue
                n = turns.index(u)
                dve.wait_ge(mm, u + 1)
                if n:
                    dve.wait_ge(ready, n)
                if n >= 2:
                    dve.wait_ge(turned, n - 1)
                to = roped[n % 2]
                if PIECES[i] != "kv":
                    rotate(u, t, 4, to[:, :]).then_inc(ready, 1)
                    dve.wait_ge(ready, n + 1)
                    dve.sem_inc(left["dve"], 1)
                    continue
                if t < TX:
                    rotate(u, t, 2, to[:, 0:P]).then_inc(ready, 1)
                else:
                    dve.tensor_copy(to[:, 0:P], out_ps[u % 4][:, 0:P]).then_inc(ready, 1)
                dve.tensor_copy(keep["v"][:, t, :], out_ps[u % 4][:, P:2 * P]).then_inc(left["dve"], 1)

        @block.gpsimd
        def _(pool):
            pool.wait_ge(turned_out, len(turns))


def attention_phase(nc, sink, w_ada, dram, keep):
    F = mybir.dt.float32
    ACT, ALU, AX = mybir.ActivationFunctionType, mybir.AluOpType, mybir.AxisListType
    ctx = ExitStack()
    with ctx:
        def sb(n, s, d=F):
            return ctx.enter_context(nc.sbuf_tensor(f"att_{n}", s, d))

        def ps(n, s):
            bank = ctx.enter_context(nc.psum_tensor(f"att_{n}_ps", [P, 512], F))
            if len(s) == 3:
                return bank[:, 0:s[1] * s[2]].rearrange("p (a b) -> p a b", a=s[1])
            return bank[:, 0:s[1]]

        sem = phase_semaphores(nc, ctx, "att")

        CTX = TC * P
        GROUP = Q_HEADS // (KV_WIDTH // HEAD)
        mask = sb("mask", [P, 3 * P])
        w_mod = [sb(f"w_mod{i}", [P, KD // 2, D]) for i in range(2)]
        w_mod_ld, summed = [sem(f"w_mod_ld{i}") for i in range(2)], sem("summed")
        zeros = sb("zeros", [P, D])
        zeroed, cleared = sem("zeroed"), sem("cleared")
        sinks = sb("sinks", [P, Q_HEADS])
        top = sb("top", [P, Q_HEADS, 2])
        top1 = sb("top1", [P, Q_HEADS])
        minus = [sb(f"minus{i}", [P, Q_HEADS]) for i in range(2)]
        sink_exp = [sb(f"sink_exp{i}", [P, 1]) for i in range(3)]
        sums = [sb(f"sums{i}", [P, 2]) for i in range(3)]
        total = [sb(f"total{i}", [P, 1]) for i in range(3)]
        inverse = [sb(f"inverse{i}", [P, 1]) for i in range(3)]
        masked = [sb(f"masked{i}", [P, 3 * P]) for i in range(2)]
        prob = [sb(f"prob{i}", [P, 3 * P + CTX]) for i in range(3)]
        prob_t = [sb(f"prob_t{i}", [P, 3 + TC, GROUP, P]) for i in range(2)]
        near_ps = [ps(f"near{i}", [P, 512]) for i in range(2)]
        far_ps = [ps(f"far{i}", [P, 512]) for i in range(2)]
        near_t, far_t = ps("near_t", [P, 512]), ps("far_t", [P, 512])
        out_ps = [ps(f"out{i}", [P, 512]) for i in range(2)]

        ld, scored, masked_ok, far_top, chain, minus_ok, near_exp, far_exp = (
            sem(n) for n in ("ld", "scored", "masked", "far_top", "chain", "minus", "near_exp", "far_exp"))
        near_turned, far_turned, near_copied, far_copied, valued, scaled, inverse_ok, written = (
            sem(n) for n in ("near_t", "far_t", "near_c", "far_c", "valued", "scaled", "inverse_ok", "written"))

        STEPS = [(n, h) for n in range(TX) for h in range(Q_HEADS)]

        def band(n):
            first, last = max(0, n - 1) * P, min(TX, n + 2) * P
            return first, last, first - (n - 1) * P

        def place(h):
            side = h // (Q_HEADS // 2)
            return slice(side * HEAD, (side + 1) * HEAD), h % (Q_HEADS // 2)

        block = ctx.enter_context(nc.Block())

        @block.sync
        def _(sp):
            sp.dma_start(mask[:, :], dram["mask"]).then_inc(ld, 16)
            sp.dma_start(sinks[:, :], sink[0, :].partition_broadcast(P)).then_inc(ld, 16)
            def load_mod(j):
                layer, vec = REST_VECTORS[j // 2]
                if j >= 2:
                    sp.wait_ge(summed, (j - 1) * KD // 2)
                rows = slice(j % 2 * D // 2, (j % 2 + 1) * D // 2)
                sp.dma_start(w_mod[j % 2][:, :, :], w_ada[layer, rows, vec * D:(vec + 1) * D].rearrange("(k p) f -> p k f", p=P))\
                  .then_inc(w_mod_ld[j % 2], 16)

            sp.wait_ge(zeroed, 1)
            rows = dram["y"].rearrange("(a c p) d -> a p c d", p=P, c=TILES_PASS)
            for i in range(max(len(REST_VECTORS), MAX_PASSES)):
                if i < len(REST_VECTORS):
                    load_mod(2 * i)
                    load_mod(2 * i + 1)
                if i < MAX_PASSES:
                    sp.dma_start(rows[i], zeros[:, :].unsqueeze(1).to_broadcast([P, TILES_PASS, D])).then_inc(cleared, 16)
            sp.wait_ge(cleared, 16 * MAX_PASSES)

        @block.gpsimd
        def _(pool):
            pool.memset(zeros[:, :], 0.0).then_inc(zeroed, 1)

        @block.tensor
        def _(pe):
            def score(s):
                n, h = STEPS[s]
                first, last, _ = band(n)
                rows, pair = place(h)
                if s >= 2:
                    pe.wait_ge(masked_ok, s - 1)
                    pe.wait_ge(far_exp, s - 1)
                q = keep["q_t"][rows, pair, n * P:(n + 1) * P]
                pe.matmul(near_ps[s % 2][:, 0:last - first], q, keep["k_t"][rows, first:last], start=True, stop=True)
                pe.matmul(far_ps[s % 2][:, 0:CTX], q, keep["k_t"][rows, TX * P:TX * P + CTX], start=True, stop=True)\
                  .then_inc(scored, 1)

            def turn(s):
                n, h = STEPS[s]
                first, last, _ = band(n)
                keys = last - first
                b = s % 3
                pe.wait_ge(scaled, 2 * s + 2)
                if s:
                    pe.wait_ge(near_copied, s)
                for j in range(keys // P):
                    x = pe.transpose(near_t[:, j * P:(j + 1) * P], prob[b][:, j * P:(j + 1) * P], keep["ident"][:, :])
                x.then_inc(near_turned, 1)
                if s:
                    pe.wait_ge(far_copied, s)
                for j in range(TC):
                    x = pe.transpose(far_t[:, j * P:(j + 1) * P], prob[b][:, (3 + j) * P:(4 + j) * P], keep["ident"][:, :])
                x.then_inc(far_turned, 1)

            def value(g, quarter):
                n, h = STEPS[g * GROUP]
                first, last, _ = band(n)
                side = h // (Q_HEADS // 2)
                cols = slice(side * HEAD, (side + 1) * HEAD)
                if quarter == 0:
                    if g >= 2:
                        pe.wait_ge(written, g - 1)
                    pe.wait_ge(near_copied, (g + 1) * GROUP)
                    pe.wait_ge(far_copied, (g + 1) * GROUP)
                tiles = [(j, first // P + j) for j in range((last - first) // P)] + [(3 + j, TX + j) for j in range(TC)]
                parts = [(odd, m) for odd in range(2) for m in range(len(tiles))]
                for odd, m in parts[quarter * len(parts) // 4:(quarter + 1) * len(parts) // 4]:
                    at, tile = tiles[m]
                    out = out_ps[g % 2][odd * HEAD:(odd + 1) * HEAD, 0:GROUP // 2 * P].rearrange("p (a q) -> p a q", q=P)
                    x = pe.matmul(out, keep["v"][:, tile, cols], prob_t[g % 2][:, at, odd:GROUP:2, :],
                                  start=(m == 0), stop=(m == len(tiles) - 1))
                if quarter == 3:
                    x.then_inc(valued, 1)

            S = len(STEPS)
            for s in range(S + 6):
                if s < S:
                    score(s)
                if 2 <= s < S + 2:
                    turn(s - 2)
                if s >= 6:
                    value(*divmod(s - 6, GROUP))

        @block.vector
        def _(dve):
            chain_n = [0]

            def link(ins):
                chain_n[0] += 1
                ins.then_inc(chain, 1)
                dve.wait_ge(chain, chain_n[0])

            def maxima(s):
                n, h = STEPS[s]
                first, last, at = band(n)
                keys = last - first
                dve.wait_ge(scored, s + 1)
                if s >= 2:
                    dve.wait_ge(near_exp, s - 1)
                dve.tensor_tensor(masked[s % 2][:, 0:keys], near_ps[s % 2][:, 0:keys], mask[:, at:at + keys], ALU.add)\
                   .then_inc(masked_ok, 1)
                dve.reduce_max(top[:, h, 1:2], far_ps[s % 2][:, 0:CTX], AX.X)
                dve.wait_ge(masked_ok, s + 1)
                link(dve.reduce_max(top[:, h, 0:1], masked[s % 2][:, 0:keys], AX.X))
                link(dve.tensor_tensor(top1[:, h:h + 1], top[:, h, 0:1], top[:, h, 1:2], ALU.max))
                dve.tensor_scalar(minus[n % 2][:, h:h + 1], top1[:, h:h + 1], sinks[:, h:h + 1], -1.0, ALU.max, ALU.mult)\
                   .then_inc(minus_ok, 1)

            def inverse_of(s):
                b = s % 3
                dve.wait_ge(far_exp, s + 1)
                link(dve.scalar_tensor_tensor(total[b][:, :], sums[b][:, 0:1], sums[b][:, 1:2], sink_exp[b][:, :], ALU.add, ALU.add))
                dve.reciprocal(inverse[b][:, :], total[b][:, :]).then_inc(inverse_ok, 1)

            def finish(g):
                n, h = STEPS[g * GROUP]
                dve.wait_ge(valued, g + 1)
                dve.tensor_copy(keep["att"][:, h // 2:(h + GROUP) // 2, n * P:(n + 1) * P],
                                out_ps[g % 2][:, 0:GROUP // 2 * P].rearrange("p (a q) -> p a q", q=P)).then_inc(written, 1)

            def add_modulation(m):
                i, k = divmod(m, KD)
                to, c = keep["mod_sum"][:, i, :], keep["c_silu"][:, 0, k:k + 1]
                j = m // (KD // 2)
                w = w_mod[j % 2][:, m % (KD // 2), :]
                dve.wait_ge(w_mod_ld[j % 2], 16 * (j // 2 + 1))
                if k == 0:
                    dve.tensor_scalar(to, w, c, None, ALU.mult).then_inc(summed, 1)
                else:
                    dve.wait_ge(summed, m)
                    dve.scalar_tensor_tensor(to, w, c, to, ALU.mult, ALU.add).then_inc(summed, 1)

            dve.wait_ge(ld, 32)
            S = len(STEPS)
            SHARES = len(REST_VECTORS) * KD
            LEAD = 4
            for s in range(S + 7):
                if s < S:
                    maxima(s)
                if 1 <= s <= S:
                    inverse_of(s - 1)
                for m in range(max(0, s - LEAD) * SHARES // (S - LEAD), max(0, s + 1 - LEAD) * SHARES // (S - LEAD)):
                    if m < SHARES:
                        add_modulation(m)
                if s >= 10 and (s - 10) % GROUP == 0:
                    finish((s - 10) // GROUP)

        @block.scalar
        def _(act):
            def exps(s):
                n, h = STEPS[s]
                first, last, _ = band(n)
                keys = last - first
                b, less = s % 3, minus[n % 2][:, h:h + 1]
                act.wait_ge(minus_ok, s + 1)
                if s >= 3:
                    act.wait_ge(far_turned, s - 2)
                act.activation(sink_exp[b][:, :], sinks[:, h:h + 1], ACT.Exp, bias=less)
                act.activation(prob[b][:, 0:keys], masked[s % 2][:, 0:keys], ACT.Exp, bias=less,
                               accum_out=sums[b][:, 0:1]).then_inc(near_exp, 1)
                act.activation(prob[b][:, 3 * P:3 * P + CTX], far_ps[s % 2][:, 0:CTX], ACT.Exp, bias=less,
                               accum_out=sums[b][:, 1:2]).then_inc(far_exp, 1)

            def divide(s):
                n, h = STEPS[s]
                first, last, _ = band(n)
                b = s % 3
                act.wait_ge(inverse_ok, s + 1)
                act.wait_ge(near_exp, s + 1)
                act.activation(prob[b][:, 0:last - first], prob[b][:, 0:last - first], ACT.Copy, scale=inverse[b][:, :])\
                   .then_inc(scaled, 1)
                act.wait_ge(far_exp, s + 1)
                act.activation(prob[b][:, 3 * P:3 * P + CTX], prob[b][:, 3 * P:3 * P + CTX], ACT.Copy, scale=inverse[b][:, :])\
                   .then_inc(scaled, 1)

            def copy_turned(s):
                n, h = STEPS[s]
                first, last, _ = band(n)
                g, h = s // GROUP, s % GROUP
                act.wait_ge(near_turned, s + 1)
                if g >= 2:
                    act.wait_ge(valued, g - 1)
                act.activation(prob_t[g % 2][:, 0:(last - first) // P, h, :],
                               near_t[:, 0:last - first].rearrange("p (a q) -> p a q", q=P), ACT.Copy).then_inc(near_copied, 1)
                act.wait_ge(far_turned, s + 1)
                act.activation(prob_t[g % 2][:, 3:3 + TC, h, :], far_t[:, 0:CTX].rearrange("p (a q) -> p a q", q=P), ACT.Copy)\
                   .then_inc(far_copied, 1)

            S = len(STEPS)
            for s in range(S + 2):
                if s < S:
                    exps(s)
                if 1 <= s <= S:
                    divide(s - 1)
                if s >= 2:
                    copy_turned(s - 2)


def modulation_rest_phase(nc, b_ada, w_out, dram, keep):
    F = mybir.dt.float32
    ACT, ALU = mybir.ActivationFunctionType, mybir.AluOpType
    ctx = ExitStack()
    with ctx:
        def sb(n, s):
            return ctx.enter_context(nc.sbuf_tensor(f"rest_{n}", s, F))

        sem = phase_semaphores(nc, ctx, "rest")

        rows = [i for i, (layer, vec) in enumerate(REST_VECTORS) if vec < 3]
        columns = [i for i, (layer, vec) in enumerate(REST_VECTORS) if vec >= 3]
        ones = sb("ones", [P, P])
        row_bias = sb("row_bias", [P, len(rows), D])
        row = sb("row", [1, len(rows), D])
        col_bias = sb("col_bias", [P, len(columns), KD])
        row_ps = [ctx.enter_context(nc.psum_tensor(f"rest_row{i}_ps", [P, 512], F)) for i in range(4)]
        col_ps = ctx.enter_context(nc.psum_tensor("rest_col_ps", [P, len(columns), KD], F))
        ld, row_mm, row_out, col_mm, biased, stored = (
            sem(n) for n in ("ld", "row_mm", "row_out", "col_mm", "biased", "stored"))
        KB = 2
        BLOCKS = KD // KB
        raw = [sb(f"raw{i}", [P, KB, D]) for i in range(2)]
        raw_ld, rounded, split = [sem(f"raw_ld{i}") for i in range(2)], sem("rounded"), sem("split")
        block = ctx.enter_context(nc.Block())

        @block.sync
        def _(sp):
            sp.dma_start(ones[:, :], dram["ones"]).then_inc(ld, 16)
            for at, i in enumerate(rows):
                layer, vec = REST_VECTORS[i]
                sp.dma_start(row_bias[:, at, :], b_ada[layer, vec * D:(vec + 1) * D].partition_broadcast(P)).then_inc(ld, 16)
            for at, i in enumerate(columns):
                layer, vec = REST_VECTORS[i]
                sp.dma_start(col_bias[:, at, :], b_ada[layer, vec * D:(vec + 1) * D].rearrange("(k p) -> p k", p=P)).then_inc(ld, 16)
            blocks = w_out.rearrange("a (k p) f -> p (a k) f", p=P)
            for b in range(BLOCKS):
                if b >= 2:
                    sp.wait_ge(split, b - 1)
                sp.dma_start(raw[b % 2][:, :, :], blocks[:, b * KB:(b + 1) * KB, :]).then_inc(raw_ld[b % 2], 16)
            sp.wait_ge(row_out, 2 * len(rows))
            sp.dma_start(dram["pool_mod"].rearrange("(a v) d -> a v d", a=1), row[:, 1:, :]).then_inc(stored, 16)
            sp.wait_ge(stored, 16)

        LOADS = 16 * (1 + len(rows) + len(columns))

        @block.tensor
        def _(pe):
            pe.wait_ge(ld, LOADS)
            for n in range(2 * len(rows)):
                if n >= 4:
                    pe.wait_ge(row_out, n - 3)
                half = slice(n % 2 * 512, (n % 2 + 1) * 512)
                pe.matmul(row_ps[n % 4][:, :], ones[:, :], keep["mod_sum"][:, rows[n // 2], half], start=True, stop=True)\
                  .then_inc(row_mm, 1)
            for at, i in enumerate(columns):
                for k in range(KD):
                    m = pe.matmul(col_ps[:, at, k:k + 1], keep["mod_sum"][:, i, k * P:(k + 1) * P], ones[:, 0:1],
                                  start=True, stop=True)
            m.then_inc(col_mm, 1)

        @block.scalar
        def _(act):
            for b in range(BLOCKS):
                act.wait_ge(raw_ld[b % 2], 16 * (b // 2 + 1))
                act.activation(keep["w_out_hi"][:, b * KB:(b + 1) * KB, :], raw[b % 2][:, :, :], ACT.Copy).then_inc(rounded, 1)

        @block.vector
        def _(dve):
            dve.wait_ge(ld, LOADS)
            for n in range(2 * len(rows)):
                half = slice(n % 2 * 512, (n % 2 + 1) * 512)
                dve.wait_ge(row_mm, n + 1)
                to, bank, bias = keep["gate0"][:, half], row_ps[n % 4][:, :], row_bias[:, n // 2, half]
                if n >= 2:
                    to, bank, bias = row[:, n // 2, half], row_ps[n % 4][0:1, :], row_bias[0:1, n // 2, half]
                dve.tensor_tensor(to, bank, bias, ALU.add).then_inc(row_out, 1)
            for b in range(BLOCKS):
                dve.wait_ge(rounded, b + 1)
                dve.tensor_tensor(keep["w_out_lo"][:, b * KB:(b + 1) * KB, :], raw[b % 2][:, :, :],
                                  keep["w_out_hi"][:, b * KB:(b + 1) * KB, :].bitcast(F), ALU.subtract).then_inc(split, 1)
            dve.wait_ge(col_mm, 1)
            for at, i in enumerate(columns):
                layer, vec = REST_VECTORS[i]
                cols = keep["ffn_cols"] if layer == 0 else keep["moe_cols"]
                slot, added = {3: (1, 0.0), 4: (0, 1.0), 5: (2, 0.0)}[vec]
                dve.scalar_tensor_tensor(cols[:, slot, :], col_ps[:, at, :], added, col_bias[:, at, :], ALU.add, ALU.add)


def mixer_output_phase(nc, gm, dram, keep):
    F, R = mybir.dt.float32, mybir.dt.float32r
    ACT, ALU = mybir.ActivationFunctionType, mybir.AluOpType
    ctx = ExitStack()
    with ctx:
        def sb(n, s, d=F):
            return ctx.enter_context(nc.sbuf_tensor(f"mix_{n}", s, d))

        def ps(n, s):
            bank = ctx.enter_context(nc.psum_tensor(f"mix_{n}_ps", [P, 512], F))
            if len(s) == 3:
                return bank[:, 0:s[1] * s[2]].rearrange("p (a b) -> p a b", a=s[1])
            return bank[:, 0:s[1]]

        sem = phase_semaphores(nc, ctx, "mix")

        GM = D // 2
        w_s = sb("w_s", [P, GM_GROUPS, P])
        w_s_t = sb("w_s_t", [P, GM_GROUPS, P])
        bias = sb("bias", [P, GM_GROUPS])
        gain = sb("gain", [P, GM])
        mean, root, rstd = sb("mean", [P, TX]), sb("root", [P, TX]), sb("rstd", [P, TX])
        v_sum = sb("v_sum", [P, TX])
        w_hi, w_lo = keep["w_out_hi"], keep["w_out_lo"]
        cat_hi = [sb(f"cat_hi{i}", [P, KD, P], R) for i in range(2)]
        cat_lo = [sb(f"cat_lo{i}", [P, KD, P], R) for i in range(2)]
        x_in = [sb(f"x_in{i}", [P, D]) for i in range(2)]
        gated = sb("gated", [P, D])
        x_new = [sb(f"x_new{i}", [P, D]) for i in range(2)]
        x_norm = [sb(f"x_norm{i}", [P, D]) for i in range(2)]
        square = sb("square", [P, D])
        ssum, smean, sroot, srstd = (sb(n, [P, TX]) for n in ("ssum", "smean", "sroot", "srstd"))
        gm_ps = [ps(f"gm{i}", [P, TX, HEAD]) for i in range(2)]
        turn_ps = [ps(f"turn{i}", [P, 4, P]) for i in range(2)]
        y_ps = [ps(f"y{i}", [P, 512]) for i in range(4)]

        ld, x_ld = sem("ld"), [sem(f"x_ld{i}") for i in range(2)]
        w_turned, w_copied, chain, rooted, v_ok, mixed, gm_ok = (
            sem(n) for n in ("w_turned", "w_copied", "chain", "rooted", "v_ok", "mixed", "gm_ok"))
        turned, cat_rounded, cat_split, y_mm, y_read, x_ok, squared, s_mean, s_root, s_rstd, x_normed = (
            sem(n) for n in ("turned", "cat_rounded", "cat_split", "y_mm", "y_read", "x_ok", "squared", "s_mean", "s_root",
                             "s_rstd", "x_normed"))
        x_st = [sem(f"x_st{i}") for i in range(2)]
        mean_ok = sem("mean_ok")
        rstd_ok = sem("rstd_ok")

        def by_feature(t, half):
            return keep["att"][:, :, t * P:(t + 1) * P] if half == 0 else turn_ps[t % 2][:, :, :]

        block = ctx.enter_context(nc.Block())
        x_tiles = gm["x"].rearrange("a (t p) d -> (a t) p d", p=P)

        @block.sync
        def _(sp):
            sp.dma_start(w_s[:, :, :], gm["w_s"].rearrange("a g t s -> t (a g) s")).then_inc(ld, 16)
            sp.dma_start(bias[:, :], gm["b_s"].rearrange("a g t -> t (a g)")).then_inc(ld, 16)
            sp.dma_start(gain[:, :], gm["gain"][0, :].partition_broadcast(P)).then_inc(ld, 16)
            for t in range(TX):
                if t >= 2:
                    sp.wait_ge(x_ok, t - 1)
                sp.dma_start(x_in[t % 2][:, :], x_tiles[t]).then_inc(x_ld[t % 2], 16)

        @block.gpsimd
        def _(pool):
            for t in range(TX):
                pool.wait_ge(x_normed, t + 1)
                pool.dma_start(dram["x1"][t * P:(t + 1) * P, :], x_new[t % 2][:, :]).then_inc(x_st[t % 2], 16)
                pool.dma_start(dram["xn"][t * P:(t + 1) * P, :], x_norm[t % 2][:, :]).then_inc(x_st[t % 2], 16)
            for i in range(2):
                pool.wait_ge(x_st[i], 32 * (TX // 2))

        @block.tensor
        def _(pe):
            pe.wait_ge(ld, 48)
            for g in range(GM_GROUPS):
                x = pe.transpose(turn_ps[g // 4][:, g % 4, :], w_s[:, g, :], keep["ident"][:, :])
                if g % 4 == 3:
                    x.then_inc(w_turned, 1)
            pe.wait_ge(w_copied, 2)

            pe.wait_ge(v_ok, TX)
            for g in range(GM_GROUPS):
                if g >= 2:
                    pe.wait_ge(gm_ok, g - 1)
                pe.matmul(gm_ps[g % 2][:, :, :], w_s_t[:, g, :], keep["v_gm"][:, :, g * HEAD:(g + 1) * HEAD],
                          start=True, stop=True).then_inc(mixed, 1)

            def turn(t):
                if t == 0:
                    pe.wait_ge(gm_ok, GM_GROUPS)
                if t >= 2:
                    pe.wait_ge(cat_split, 2 * (t - 1))
                for j in range(4):
                    x = pe.transpose(turn_ps[t % 2][:, j, :], keep["u"][:, t, j * P:(j + 1) * P], keep["ident"][:, :])
                x.then_inc(turned, 1)

            def project(t):
                pe.wait_ge(cat_split, 2 * t + 2)
                if t >= 2:
                    pe.wait_ge(y_read, t - 1)
                for half in range(2):
                    bank = y_ps[2 * (t % 2) + half]
                    cols = slice(half * 512, (half + 1) * 512)
                    for k in range(KD):
                        pe.matmul(bank[:, :], cat_hi[t % 2][:, k, :], w_hi[:, k, cols], start=(k == 0), stop=False)
                        pe.matmul(bank[:, :], cat_hi[t % 2][:, k, :], w_lo[:, k, cols], start=False, stop=False)
                        x = pe.matmul(bank[:, :], cat_lo[t % 2][:, k, :], w_hi[:, k, cols], start=False, stop=(k == KD - 1))
                x.then_inc(y_mm, 1)

            turn(0)
            for t in range(TX):
                if t + 1 < TX:
                    turn(t + 1)
                project(t)

        @block.scalar
        def _(act):
            for i in range(2):
                act.wait_ge(w_turned, i + 1)
                act.activation(w_s_t[:, 4 * i:4 * i + 4, :], turn_ps[i][:, :, :], ACT.Copy).then_inc(w_copied, 1)
            act.wait_ge(mean_ok, 1)
            act.activation(root[:, :], mean[:, :], ACT.Sqrt).then_inc(rooted, 1)

            def round_cat(t):
                for half in range(2):
                    if half:
                        act.wait_ge(turned, t + 1)
                    if t >= 2 and half == 0:
                        act.wait_ge(y_mm, t - 1)
                    act.activation(cat_hi[t % 2][:, 4 * half:4 * half + 4, :], by_feature(t, half), ACT.Copy)\
                       .then_inc(cat_rounded, 1)

            def norm(t):
                act.wait_ge(x_ok, t + 1)
                if t:
                    act.wait_ge(squared, t)
                act.activation(square[:, :], x_new[t % 2][:, :], ACT.Square, accum_out=ssum[:, t:t + 1]).then_inc(squared, 1)
                act.wait_ge(s_mean, t + 1)
                act.activation(sroot[:, t:t + 1], smean[:, t:t + 1], ACT.Sqrt).then_inc(s_root, 1)
                act.wait_ge(s_rstd, t + 1)
                if t >= 2:
                    act.wait_ge(x_st[t % 2], 32 * (t // 2))
                act.activation(x_norm[t % 2][:, :], x_new[t % 2][:, :], ACT.Copy, scale=srstd[:, t:t + 1]).then_inc(x_normed, 1)

            round_cat(0)
            for t in range(TX):
                if t + 1 < TX:
                    round_cat(t + 1)
                norm(t)

        @block.vector
        def _(dve):
            chain_n = [0]

            def link(ins):
                chain_n[0] += 1
                ins.then_inc(chain, 1)
                dve.wait_ge(chain, chain_n[0])

            link(dve.tensor_tensor(v_sum[:, :], keep["v_sums"][:, :, 0], keep["v_sums"][:, :, 1], ALU.add))
            dve.tensor_scalar(mean[:, :], v_sum[:, :], 1.0 / GM, EPS, ALU.mult, ALU.add).then_inc(mean_ok, 1)
            dve.wait_ge(rooted, 1)
            dve.reciprocal(rstd[:, :], root[:, :]).then_inc(rstd_ok, 1)
            dve.wait_ge(rstd_ok, 1)
            dve.wait_ge(ld, 48)

            def scale_v(t):
                dve.scalar_tensor_tensor(keep["v_gm"][:, t, :], keep["v_gm"][:, t, :], rstd[:, t:t + 1], gain[:, :],
                                         ALU.mult, ALU.mult).then_inc(v_ok, 1)

            def gate(g):
                cols = slice(g * HEAD, (g + 1) * HEAD)
                dve.wait_ge(mixed, g + 1)
                dve.scalar_tensor_tensor(keep["u"][:, :, cols], gm_ps[g % 2][:, :, :], bias[:, g:g + 1], keep["u"][:, :, cols],
                                         ALU.add, ALU.mult).then_inc(gm_ok, 1)

            def rest_cat(t):
                for half in range(2):
                    dve.wait_ge(cat_rounded, 2 * t + half + 1)
                    dve.tensor_tensor(cat_lo[t % 2][:, 4 * half:4 * half + 4, :], by_feature(t, half),
                                      cat_hi[t % 2][:, 4 * half:4 * half + 4, :].bitcast(F), ALU.subtract).then_inc(cat_split, 1)

            def add(t):
                dve.wait_ge(y_mm, t + 1)
                if t:
                    dve.wait_ge(x_ok, t)
                for half in range(2):
                    x = dve.tensor_tensor(gated[:, half * 512:(half + 1) * 512], y_ps[2 * (t % 2) + half][:, :],
                                          keep["gate0"][:, half * 512:(half + 1) * 512], ALU.mult)
                x.then_inc(y_read, 1)
                dve.wait_ge(y_read, t + 1)
                dve.wait_ge(x_ld[t % 2], 16 * (t // 2 + 1))
                if t >= 2:
                    dve.wait_ge(x_st[t % 2], 32 * (t // 2))
                    dve.wait_ge(x_normed, t - 1)
                dve.tensor_tensor(x_new[t % 2][:, :], gated[:, :], x_in[t % 2][:, :], ALU.add).then_inc(x_ok, 1)

            def norm(t):
                dve.wait_ge(squared, t + 1)
                dve.tensor_scalar(smean[:, t:t + 1], ssum[:, t:t + 1], 1.0 / D, EPS, ALU.mult, ALU.add).then_inc(s_mean, 1)
                dve.wait_ge(s_root, t + 1)
                dve.reciprocal(srstd[:, t:t + 1], sroot[:, t:t + 1]).then_inc(s_rstd, 1)

            for t in range(TX):
                scale_v(t)
            for g in range(GM_GROUPS):
                gate(g)
            rest_cat(0)
            for t in range(TX):
                if t + 1 < TX:
                    rest_cat(t + 1)
                add(t)
                norm(t)


def pool_phase(nc, pool_w, pool_scale, ident, dram):
    F = mybir.dt.float32
    ACT, ALU = mybir.ActivationFunctionType, mybir.AluOpType
    ctx = ExitStack()
    with ctx:
        def sb(n, s, d=F):
            return ctx.enter_context(nc.sbuf_tensor(f"pool_{n}", s, d))

        def ps(n, s):
            bank = ctx.enter_context(nc.psum_tensor(f"pool_{n}_ps", [P, 512], F))
            if len(s) == 3:
                return bank[:, 0:s[1] * s[2]].rearrange("p (a b) -> p a b", a=s[1])
            return bank[:, 0:s[1]]

        sem = phase_semaphores(nc, ctx, "pool")

        G = len(POOL_SIZES)
        GD = D // G
        band = sb("band", [P, G, 3, P])
        edge = sb("edge", [P, G, 2, P])
        weights = sb("weights", [P, G, GD // P, GD])
        shift, scale, gate, scales = (sb(n, [P, D]) for n in ("shift", "scale", "gate", "scales"))
        y_in = sb("y_in", [P, TX, D])
        x = sb("x", [P, TX, D])
        h = sb("h", [P, TX, D])
        scaled = sb("scaled", [P, D])
        square = sb("square", [P, D])
        diff = [sb(f"diff{i}", [P, D]) for i in range(2)]
        diff_t = [sb(f"diff_t{i}", [P, KD, P]) for i in range(2)]
        gated = sb("gated", [P, D])
        x_norm = [sb(f"x_norm{i}", [P, D]) for i in range(2)]
        sums, mean, root, rstd = (sb(n, [P, 2 * TX]) for n in ("sums", "mean", "root", "rstd"))
        diff_ps = [ps(f"diff{i}", [P, 512]) for i in range(2)]
        turn_ps = [ps(f"turn{i}", [P, 4, P]) for i in range(2)]
        y_ps = [ps(f"y{i}", [P, 512]) for i in range(4)]

        turned, turned_out = sem("turned"), sem("turned_out")
        ld, mod_ld, out_ld, y_ld, x_st = sem("ld"), sem("mod_ld"), sem("out_ld"), [sem(f"y_ld{t}") for t in range(TX)], [sem(f"x_st{i}") for i in range(2)]
        chain, x_sum, squared, rooted, ready, scaled_ok, h_ok = (
            sem(n) for n in ("chain", "x_sum", "squared", "rooted", "ready", "scaled_ok", "h_ok"))
        mean_ok, diffed, copied, y_mm, y_read, x_ok, normed = (
            sem(n) for n in ("mean_ok", "diffed", "copied", "y_mm", "y_read", "x_ok", "normed"))
        block = ctx.enter_context(nc.Block())

        @block.sync
        def _(sp):
            for t in range(TX):
                sp.dma_start(x[:, t, :], dram["x1"][t * P:(t + 1) * P, :]).then_inc(y_ld[t], 16)
                sp.dma_start(y_in[:, t, :], dram["y_dense"][t * P:(t + 1) * P, :]).then_inc(y_ld[t], 16)
                if t == 0:
                    for i, to in enumerate((shift, scale)):
                        sp.dma_start(to[:, :], dram["pool_mod"][i, :].partition_broadcast(P)).then_inc(mod_ld, 16)
                if t == 1:
                    sp.dma_start(band[:, :, :, :], dram["band"].rearrange("g e s t -> s g e t")).then_inc(ld, 16)
                    sp.dma_start(edge[:, :, :, :], dram["edge"].rearrange("g e s t -> s g e t")).then_inc(ld, 16)
                    sp.dma_start(weights[:, :, :, :], pool_w.rearrange("a g (c p) d -> p (a g) c d", p=P)).then_inc(ld, 16)
            sp.dma_start(gate[:, :], dram["pool_mod"][2, :].partition_broadcast(P)).then_inc(out_ld, 16)
            sp.dma_start(scales[:, :], pool_scale[0, :].partition_broadcast(P)).then_inc(out_ld, 16)

        @block.gpsimd
        def _(pool):
            for t in range(TX):
                pool.wait_ge(y_ld[t], 32)
                pool.tensor_tensor(x[:, t, :], x[:, t, :], y_in[:, t, :], ALU.add).then_inc(x_sum, 1)
            for t in range(TX):
                pool.wait_ge(normed, t + 1)
                pool.dma_start(dram["x3"][t * P:(t + 1) * P, :], x[:, t, :]).then_inc(x_st[t % 2], 16)
                pool.dma_start(dram["xn"][t * P:(t + 1) * P, :], x_norm[t % 2][:, :]).then_inc(x_st[t % 2], 16)
            for i in range(2):
                pool.wait_ge(x_st[i], 32 * (TX // 2))

        @block.tensor
        def _(pe):
            def difference(t):
                pe.wait_ge(h_ok, min(t + 2, TX))
                if t:
                    pe.wait_ge(copied, 2 * t)
                which = 0 if t == 0 else 2 if t == TX - 1 else 1
                for g in range(G):
                    cols = slice(g * GD, (g + 1) * GD)
                    at = g * GD % 512
                    parts = [(band[:, g, which, :], t)] + [(edge[:, g, 0, :], t - 1)] * (t > 0) + [(edge[:, g, 1, :], t + 1)] * (t < TX - 1)
                    for i, (matrix, tile) in enumerate(parts):
                        m = pe.matmul(diff_ps[g * GD // 512][:, at:at + GD], matrix, h[:, tile, cols], start=(i == 0),
                                      stop=(i == len(parts) - 1))
                    if g % 2:
                        m.then_inc(diffed, 1)

            def turn(t):
                for half in range(2):
                    pe.wait_ge(copied, 2 * t + half + 1)
                    if t:
                        pe.wait_ge(turned_out, 2 * t + half - 1)
                    for j in range(4):
                        k = 4 * half + j
                        m = pe.transpose(turn_ps[half][:, j, :], diff[t % 2][:, k * P:(k + 1) * P], ident[:, :])
                    m.then_inc(turned, 1)

            def project(t):
                pe.wait_ge(turned_out, 2 * t + 2)
                if t >= 2:
                    pe.wait_ge(y_read, t - 1)
                for g in range(G):
                    bank = y_ps[2 * (t % 2) + g * GD // 512]
                    at = g * GD % 512
                    for c in range(GD // P):
                        m = pe.matmul(bank[:, at:at + GD], diff_t[t % 2][:, g * GD // P + c, :], weights[:, g, c, :],
                                      start=(c == 0), stop=(c == GD // P - 1))
                m.then_inc(y_mm, 1)

            pe.wait_ge(ld, 48)
            difference(0)
            for t in range(TX):
                if t + 1 < TX:
                    difference(t + 1)
                turn(t)
                if t:
                    project(t - 1)
            project(TX - 1)

        @block.scalar
        def _(act):
            def sum_squares(i, source):
                if i:
                    act.wait_ge(squared, i)
                act.activation(square[:, :], source, ACT.Square, accum_out=sums[:, i:i + 1]).then_inc(squared, 1)
                act.wait_ge(mean_ok, i + 1)
                act.activation(root[:, i:i + 1], mean[:, i:i + 1], ACT.Sqrt).then_inc(rooted, 1)

            def copy(t):
                for half in range(2):
                    act.wait_ge(diffed, 2 * t + half + 1)
                    if t >= 2:
                        act.wait_ge(turned, 2 * (t - 1))
                    act.activation(diff[t % 2][:, half * 512:(half + 1) * 512], diff_ps[half][:, :], ACT.Copy)\
                       .then_inc(copied, 1)

            def copy_turned(t):
                for half in range(2):
                    act.wait_ge(turned, 2 * t + half + 1)
                    if t >= 2:
                        act.wait_ge(y_mm, t - 1)
                    act.activation(diff_t[t % 2][:, 4 * half:4 * half + 4, :], turn_ps[half][:, :, :], ACT.Copy)\
                       .then_inc(turned_out, 1)

            def norm(t):
                act.wait_ge(x_ok, t + 1)
                sum_squares(TX + t, x[:, t, :])
                act.wait_ge(ready, TX + t + 1)
                if t >= 2:
                    act.wait_ge(x_st[t % 2], 32 * (t // 2))
                act.activation(x_norm[t % 2][:, :], x[:, t, :], ACT.Copy, scale=rstd[:, TX + t:TX + t + 1]).then_inc(normed, 1)

            for t in range(TX):
                act.wait_ge(x_sum, t + 1)
                sum_squares(t, x[:, t, :])
            copy(0)
            for t in range(TX):
                if t + 1 < TX:
                    copy(t + 1)
                copy_turned(t)
                if t:
                    norm(t - 1)
            norm(TX - 1)

        @block.vector
        def _(dve):
            chain_n = [0]

            def link(ins):
                chain_n[0] += 1
                ins.then_inc(chain, 1)
                dve.wait_ge(chain, chain_n[0])

            def norm(i):
                dve.wait_ge(squared, i + 1)
                dve.tensor_scalar(mean[:, i:i + 1], sums[:, i:i + 1], 1.0 / D, EPS, ALU.mult, ALU.add).then_inc(mean_ok, 1)
                dve.wait_ge(rooted, i + 1)
                dve.reciprocal(rstd[:, i:i + 1], root[:, i:i + 1]).then_inc(ready, 1)
                dve.wait_ge(ready, i + 1)

            def modulate(t):
                norm(t)
                if t:
                    dve.wait_ge(h_ok, t)
                link(dve.scalar_tensor_tensor(scaled[:, :], x[:, t, :], rstd[:, t:t + 1], scale[:, :], ALU.mult, ALU.mult))
                dve.tensor_tensor(h[:, t, :], scaled[:, :], shift[:, :], ALU.add).then_inc(h_ok, 1)

            dve.wait_ge(mod_ld, 32)
            link(dve.tensor_scalar(scale[:, :], scale[:, :], 1.0, None, ALU.add))
            for t in range(TX):
                modulate(t)
            dve.wait_ge(out_ld, 32)
            for t in range(TX):
                dve.wait_ge(y_mm, t + 1)
                if t:
                    dve.wait_ge(x_ok, t)
                for half in range(2):
                    cols = slice(half * 512, (half + 1) * 512)
                    m = dve.tensor_tensor(gated[:, cols], y_ps[2 * (t % 2) + half][:, :], scales[:, cols], ALU.mult)
                m.then_inc(y_read, 1)
                dve.wait_ge(y_read, t + 1)
                link(dve.tensor_tensor(gated[:, :], gated[:, :], gate[:, :], ALU.mult))
                dve.tensor_tensor(x[:, t, :], x[:, t, :], gated[:, :], ALU.add).then_inc(x_ok, 1)
                norm(TX + t)


def routing_phase(nc, router_w, dram, keep):
    F, I = mybir.dt.float32, mybir.dt.int32
    ACT, ALU, AX = mybir.ActivationFunctionType, mybir.AluOpType, mybir.AxisListType
    ctx = ExitStack()
    with ctx:
        def sb(n, s, d=F):
            return ctx.enter_context(nc.sbuf_tensor(f"route_{n}", s, d))

        def ps(n, s):
            bank = ctx.enter_context(nc.psum_tensor(f"route_{n}_ps", [P, 512], F))
            if len(s) == 3:
                return bank[:, 0:s[1] * s[2]].rearrange("p (a b) -> p a b", a=s[1])
            return bank[:, 0:s[1]]

        sem = phase_semaphores(nc, ctx, "route")

        E = N_EXPERTS
        router = sb("router", [P, KD, E])
        before = sb("before", [P, P])
        ones = sb("ones", [P, P])
        expert_of = sb("expert_of", [P, E])
        pass_of = sb("pass_of", [P, MAX_PASSES_PAD])
        logits_t = sb("logits_t", [E, SEQ])
        x = sb("x", [P, TX, D])
        h = [sb(f"h{i}", [P, TOKENS]) for i in range(2 * KD)]
        logits = sb("logits", [P, TX, E])
        best = sb("best", [P, TX, E])
        best_at = sb("best_at", [P, TX, E], mybir.dt.uint32)
        best_f = sb("best_f", [P, TX, E])
        chosen = [sb(f"chosen{i}", [P, TX, E]) for i in range(TOP_K)]
        either = sb("either", [P, TX, E])
        ranks = sb("ranks", [P, TX, E])
        totals = sb("totals", [P, TX, E])
        running = sb("running", [P, TX + 1, E])
        small = {n: sb(n, [P, E]) for n in ("over", "passes", "any", "half", "room", "gap2")}
        ends = sb("ends", [P, E])
        starts = sb("starts", [P, E])
        slots = sb("slots", [P, TX, E])
        picked = sb("picked", [P, TX, E])
        slot_f = sb("slot_f", [P, TOP_K, TX])
        gap = sb("gap", [P, TX])
        gap_exp = sb("gap_exp", [P, TX])
        gap_1 = sb("gap_1", [P, TX])
        M = MAX_PASSES_PAD
        started, ended, here, part, counts = (sb(n, [P, M, E]) for n in ("started", "ended", "here", "part", "counts"))
        count, above, table_f = sb("count", [P, M]), sb("above", [P, M, len(WIDTHS)]), sb("table_f", [P, 2, M])
        width_of = sb("width_of", [P, len(WIDTHS)])
        half_of, halves = sb("half_of", [P, TOKENS // ROUND]), sb("halves", [P, E, TOKENS // ROUND])
        zeros = sb("zeros", [P, LISTED_TILES], I)
        turn_ps = [ps(f"turn{i}", [P, TOKENS]) for i in range(3)]
        logit_t_ps = [ps(f"logit_t{g}", [P, TOKENS]) for g in range(2)]
        logit_ps = ps("logit", [P, TX, E])
        rank_ps = ps("rank", [P, TX * E])
        total_ps = ps("total", [P, TX * E])

        x_ld = [sem(f"x_ld{g}") for g in range(2)]
        ld, turned, h_ok, logit_mm, chain, exp_ok, either_ok, ranked, slots_ok, zeroed, cleared = (
            sem(n) for n in ("ld", "turned", "h_ok", "logit_mm", "chain", "exp_ok", "either_ok", "ranked",
                             "slots_ok", "zeroed", "cleared"))
        gap_ok, logit_t_mm, logit_t_out = sem("gap_ok"), sem("logit_t_mm"), sem("logit_t_out")
        block = ctx.enter_context(nc.Block())

        @block.sync
        def _(sp):
            for g in range(2):
                sp.dma_start(x[:, 4 * g:4 * g + 4, :], dram["xn"][g * TOKENS:(g + 1) * TOKENS, :].rearrange("(t p) d -> p t d", p=P))\
                  .then_inc(x_ld[g], 16)
            for to, name in ((before[:, :], "before"), (ones[:, :], "ones"), (keep["tokens"][:, :], "tokens")):
                sp.dma_start(to, dram[name]).then_inc(ld, 16)
            sp.dma_start(expert_of[:, :], dram["count_up"][0:E].partition_broadcast(P)).then_inc(ld, 16)
            sp.dma_start(pass_of[:, :], dram["count_up"][0:M].partition_broadcast(P)).then_inc(ld, 16)
            sp.dma_start(width_of[:, :], dram["width_starts"].partition_broadcast(P)).then_inc(ld, 16)
            sp.dma_start(half_of[:, :], dram["half_starts"].partition_broadcast(P)).then_inc(ld, 16)
            sp.dma_start(router[:, :, :], router_w.rearrange("a (k p) e -> p (a k) e", p=P)).then_inc(ld, 16)
            sp.wait_ge(zeroed, 1)
            sp.dma_start(dram["slot_token"].rearrange("(p c) o -> p (c o)", p=P), zeros[:, :]).then_inc(cleared, 16)
            sp.wait_ge(cleared, 16)

        @block.gpsimd
        def _(pool):
            pool.memset(zeros[:, :], 0).then_inc(zeroed, 1)

        @block.tensor
        def _(pe):
            def logits_of(i):
                g, k = divmod(i, KD)
                if i == 0:
                    pe.wait_ge(ld, 16 * 8)
                pe.wait_ge(h_ok, i + 1)
                m = pe.matmul(logit_t_ps[g][0:E, :], router[:, k, :], h[i][:, :], start=(k == 0), stop=(k == KD - 1))
                if k == KD - 1:
                    m.then_inc(logit_t_mm, 1)

            for g in range(2):
                pe.wait_ge(x_ld[g], 16)
                for k in range(KD):
                    i = g * KD + k
                    if i >= 3:
                        pe.wait_ge(h_ok, i - 2)
                    for t in range(4):
                        m = pe.transpose(turn_ps[i % 3][:, t * P:(t + 1) * P], x[:, 4 * g + t, k * P:(k + 1) * P],
                                         keep["ident"][:, :])
                    m.then_inc(turned, 1)
                    if i >= 1:
                        logits_of(i - 1)
            logits_of(2 * KD - 1)
            for t in range(TX):
                pe.wait_ge(logit_t_out, t // 4 + 1)
                m = pe.transpose(logit_ps[:, t, :], logits_t[:, t * P:(t + 1) * P], keep["ident"][0:E, 0:E])
            m.then_inc(logit_mm, 1)
            pe.wait_ge(either_ok, 1)
            flat = either[:, :, :].rearrange("p t e -> p (t e)")
            pe.matmul(rank_ps[:, :], before[:, :], flat, start=True, stop=True)
            pe.matmul(total_ps[:, :], ones[:, :], flat, start=True, stop=True).then_inc(ranked, 1)

        @block.scalar
        def _(act):
            for i in range(2 * KD):
                k = i % KD
                act.wait_ge(turned, i + 1)
                act.activation(h[i][:, :], turn_ps[i % 3][:, :], ACT.Identity, scale=keep["moe_cols"][:, 0, k:k + 1],
                               bias=keep["moe_cols"][:, 1, k:k + 1]).then_inc(h_ok, 1)
            act.wait_ge(gap_ok, 1)
            act.activation(gap_exp[:, :], gap[:, :], ACT.Exp).then_inc(exp_ok, 1)

        @block.vector
        def _(dve):
            chain_n = [0]

            def link(ins):
                chain_n[0] += 1
                ins.then_inc(chain, 1)
                dve.wait_ge(chain, chain_n[0])

            def over_tiles(ap):
                return ap.unsqueeze(1).to_broadcast([P, TX, E])

            for g in range(2):
                dve.wait_ge(logit_t_mm, g + 1)
                dve.tensor_copy(logits_t[:, g * TOKENS:(g + 1) * TOKENS], logit_t_ps[g][0:E, :]).then_inc(logit_t_out, 1)
            dve.wait_ge(logit_mm, 1)
            dve.wait_ge(ld, 16 * 8)
            link(dve.tensor_copy(logits[:, :, :], logit_ps[:, :, :]))
            for t in range(TX):
                m = dve.max(best[:, t, :], logits[:, t, :])
            link(m)
            for t in range(TX):
                m = dve.max_index(best_at[:, t, :], best[:, t, :], logits[:, t, :])
            link(m)
            link(dve.tensor_copy(best_f[:, :, :], best_at[:, :, :]))
            for i in range(TOP_K):
                m = dve.tensor_tensor(chosen[i][:, :, :], best_f[:, :, i:i + 1].to_broadcast([P, TX, E]),
                                      over_tiles(expert_of[:, :]), ALU.is_equal)
            link(m)
            dve.tensor_tensor(either[:, :, :], chosen[0][:, :, :], chosen[1][:, :, :], ALU.add).then_inc(either_ok, 1)
            dve.tensor_tensor(gap[:, :], best[:, :, 1], best[:, :, 0], ALU.subtract).then_inc(gap_ok, 1)
            dve.wait_ge(exp_ok, 1)
            link(dve.tensor_scalar(gap_1[:, :], gap_exp[:, :], 1.0, None, ALU.add))
            link(dve.reciprocal(keep["weight"][:, 0, :], gap_1[:, :]))
            dve.tensor_tensor(keep["weight"][:, 1, :], gap_exp[:, :], keep["weight"][:, 0, :], ALU.mult)
            dve.wait_ge(ranked, 1)
            dve.tensor_copy(totals[:, :, :].rearrange("p t e -> p (t e)"), total_ps[:, :])
            link(dve.memset(running[:, 0, :], 0.0))
            for t in range(TX):
                link(dve.tensor_tensor(running[:, t + 1, :], running[:, t, :], totals[:, t, :], ALU.add))
            link(dve.tensor_tensor(ranks[:, :, :].rearrange("p t e -> p (t e)"), rank_ps[:, :],
                                   running[:, 0:TX, :].rearrange("p t e -> p (t e)"), ALU.add))
            chose = running[:, TX, :]
            dve.tensor_scalar(small["over"][:, :], chose, float(TOKENS), None, ALU.is_gt)
            dve.tensor_tensor(halves[:, :, :], chose.unsqueeze(2).to_broadcast([P, E, TOKENS // ROUND]),
                              half_of[:, :].unsqueeze(1).to_broadcast([P, E, TOKENS // ROUND]), ALU.is_gt)
            link(dve.tensor_scalar(small["any"][:, :], chose, 0.0, None, ALU.is_gt))
            dve.reduce_sum(small["half"][:, :], halves[:, :, :], AX.X)
            link(dve.tensor_tensor(small["passes"][:, :], small["over"][:, :], small["any"][:, :], ALU.add))
            link(dve.tensor_scalar(small["gap2"][:, :], small["half"][:, :], float(-ROUND), float(TOKENS), ALU.mult, ALU.add))
            link(dve.tensor_tensor(small["gap2"][:, :], small["gap2"][:, :], small["over"][:, :], ALU.mult))
            link(dve.tensor_scalar(small["room"][:, :], small["gap2"][:, :], -1.0, float(TOKENS), ALU.mult, ALU.add))
            link(dve.tensor_copy(ends[:, 0:1], small["passes"][:, 0:1]))
            for e in range(1, E):
                link(dve.tensor_tensor(ends[:, e:e + 1], ends[:, e - 1:e], small["passes"][:, e:e + 1], ALU.add))
            link(dve.tensor_tensor(starts[:, :], ends[:, :], small["passes"][:, :], ALU.subtract))
            link(dve.tensor_tensor(picked[:, :, :], ranks[:, :, :], over_tiles(small["room"][:, :]), ALU.is_ge))
            link(dve.tensor_tensor(picked[:, :, :], picked[:, :, :], over_tiles(small["gap2"][:, :]), ALU.mult))
            link(dve.tensor_tensor(ranks[:, :, :], ranks[:, :, :], picked[:, :, :], ALU.add))
            link(dve.scalar_tensor_tensor(slots[:, :, :], over_tiles(starts[:, :]), float(TOKENS), ranks[:, :, :],
                                          ALU.mult, ALU.add))
            for i in range(TOP_K):
                link(dve.tensor_tensor(picked[:, :, :], slots[:, :, :], chosen[i][:, :, :], ALU.mult))
                link(dve.reduce_sum(slot_f[:, i, :], picked[:, :, :], AX.X))
            dve.tensor_copy(keep["slot"][:, :, :], slot_f[:, :, :]).then_inc(slots_ok, 1)
            by_pass = pass_of[:, :].unsqueeze(2).to_broadcast([P, M, E])

            def by_expert(ap):
                return ap.unsqueeze(1).to_broadcast([P, M, E])

            dve.tensor_tensor(started[:, :, :], by_pass, by_expert(starts[:, :]), ALU.is_ge)
            dve.tensor_tensor(ended[:, :, :], by_pass, by_expert(ends[:, :]), ALU.is_lt)
            link(dve.tensor_tensor(part[:, :, :], by_expert(starts[:, :]), by_pass, ALU.subtract))
            dve.tensor_tensor(here[:, :, :], started[:, :, :], ended[:, :, :], ALU.mult)
            link(dve.tensor_tensor(counts[:, :, :], part[:, :, :], by_expert(small["room"][:, :]), ALU.mult))
            link(dve.tensor_tensor(counts[:, :, :], counts[:, :, :], by_expert(chose), ALU.add))
            link(dve.tensor_tensor(counts[:, :, :], counts[:, :, :], by_expert(small["room"][:, :]), ALU.min))
            link(dve.tensor_tensor(counts[:, :, :], counts[:, :, :], here[:, :, :], ALU.mult))
            dve.reduce_sum(count[:, :], counts[:, :, :], AX.X)
            link(dve.tensor_tensor(part[:, :, :], here[:, :, :], by_expert(expert_of[:, :]), ALU.mult))
            dve.reduce_sum(table_f[:, 0, :], part[:, :, :], AX.X)
            link(dve.tensor_tensor(above[:, :, :], count[:, :].unsqueeze(2).to_broadcast([P, M, len(WIDTHS)]),
                                   width_of[:, :].unsqueeze(1).to_broadcast([P, M, len(WIDTHS)]), ALU.is_gt))
            link(dve.reduce_sum(table_f[:, 1, :], above[:, :, :], AX.X))
            link(dve.tensor_copy(table_f[:, 0, M - 1:M], ends[:, E - 1:E]))
            dve.tensor_copy(keep["table"][:, :, :], table_f[0:1, :, :])


def output_phase(nc, final_gain, dram, keep, out):
    F = mybir.dt.float32
    ACT, ALU = mybir.ActivationFunctionType, mybir.AluOpType
    ctx = ExitStack()
    with ctx:
        def sb(n, s, d=F):
            return ctx.enter_context(nc.sbuf_tensor(f"out_{n}", s, d))

        sem = phase_semaphores(nc, ctx, "out")

        gain = sb("gain", [P, D])
        x = sb("x", [P, TX, D])
        y = sb("y", [P, TX, TOP_K, D])
        square = sb("square", [P, D])
        result = [sb(f"result{i}", [P, D]) for i in range(2)]
        sums, mean, root, rstd = (sb(n, [P, TX]) for n in ("sums", "mean", "root", "rstd"))
        ld, x_ok, squared, mean_ok, rooted, ready, done, chain = (
            sem(n) for n in ("ld", "x_ok", "squared", "mean_ok", "rooted", "ready", "done", "chain"))
        x_ld = [sem(f"x_ld{t}") for t in range(TX)]
        y_ld = [sem(f"y_ld{t}") for t in range(TX)]
        stored = [sem(f"stored{i}") for i in range(2)]
        block = ctx.enter_context(nc.Block())

        @block.sync
        def _(sp):
            sp.dma_start(gain[:, :], final_gain.partition_broadcast(P)).then_inc(ld, 16)
            for t in range(TX):
                sp.dma_start(x[:, t, :], dram["x3"][t * P:(t + 1) * P, :]).then_inc(x_ld[t], 16)
            rows = out.rearrange("a (t p) d -> (a t) p d", p=P)
            for t in range(TX):
                sp.wait_ge(done, t + 1)
                sp.dma_start(rows[t], result[t % 2][:, :]).then_inc(stored[t % 2], 16)
            for i in range(2):
                sp.wait_ge(stored[i], 16 * (TX // 2))

        @block.gpsimd
        def _(pool):
            for t in range(TX):
                for i in range(TOP_K):
                    pool.indirect_dma_start(y[:, t, i, :], None, dram["y"],
                                            bass.IndirectOffsetOnAxis(ap=keep["slot"][:, i, t:t + 1], axis=0)).then_inc(y_ld[t], 16)

        @block.scalar
        def _(act):
            for t in range(TX):
                act.wait_ge(x_ok, t + 1)
                if t:
                    act.wait_ge(squared, t)
                act.activation(square[:, :], x[:, t, :], ACT.Square, accum_out=sums[:, t:t + 1]).then_inc(squared, 1)
                act.wait_ge(mean_ok, t + 1)
                act.activation(root[:, t:t + 1], mean[:, t:t + 1], ACT.Sqrt).then_inc(rooted, 1)

        @block.vector
        def _(dve):
            def add(t):
                dve.wait_ge(x_ld[t], 16)
                dve.wait_ge(y_ld[t], 16 * TOP_K)
                for i in range(TOP_K):
                    dve.scalar_tensor_tensor(x[:, t, :], y[:, t, i, :], keep["weight"][:, i, t:t + 1], x[:, t, :],
                                             ALU.mult, ALU.add).then_inc(chain if i == 0 else x_ok, 1)
                    if i == 0:
                        dve.wait_ge(chain, t + 1)

            def norm(t):
                dve.wait_ge(squared, t + 1)
                dve.tensor_scalar(mean[:, t:t + 1], sums[:, t:t + 1], 1.0 / D, EPS, ALU.mult, ALU.add).then_inc(mean_ok, 1)
                dve.wait_ge(rooted, t + 1)
                dve.reciprocal(rstd[:, t:t + 1], root[:, t:t + 1]).then_inc(ready, 1)
                dve.wait_ge(ready, t + 1)
                if t >= 2:
                    dve.wait_ge(stored[t % 2], 16 * (t // 2))
                dve.scalar_tensor_tensor(result[t % 2][:, :], x[:, t, :], rstd[:, t:t + 1], gain[:, :], ALU.mult, ALU.mult)\
                   .then_inc(done, 1)

            add(0)
            dve.wait_ge(ld, 16)
            for t in range(TX):
                if t + 1 < TX:
                    add(t + 1)
                norm(t)


def expert_mlp_phase(nc, name, shape, weights, columns, ident, rows_of, y_rows, table, prepare=None):
    F, R = mybir.dt.float32, mybir.dt.float32r
    ACT, ALU, AX = mybir.ActivationFunctionType, mybir.AluOpType, mybir.AxisListType
    passes, C = shape
    gate_w, up_w, down_w = weights
    ctx = ExitStack()
    with ctx:
        def sb(n, s, d=F):
            return ctx.enter_context(nc.sbuf_tensor(f"{name}_{n}", s, d))

        def ps(n):
            return ctx.enter_context(nc.psum_tensor(f"{name}_{n}", [P, TOKENS], F))

        sem = phase_semaphores(nc, ctx, name)

        raw_g = sb("raw_g", [P, KD, CHUNK_FF])
        raw_u = sb("raw_u", [P, KD, CHUNK_FF])
        raw_d = sb("raw_d", [P, FB, D])
        g_hi = [sb(f"g_hi{i}", [P, KD, CHUNK_FF], R) for i in range(2)]
        g_lo = [sb(f"g_lo{i}", [P, KD, CHUNK_FF], R) for i in range(2)]
        u_hi = [sb(f"u_hi{i}", [P, KD, CHUNK_FF], R) for i in range(2)]
        u_lo = [sb(f"u_lo{i}", [P, KD, CHUNK_FF], R) for i in range(2)]
        d_hi = [sb(f"d_hi{i}", [P, FB, D], R) for i in range(2)]
        d_lo = [sb(f"d_lo{i}", [P, FB, D], R) for i in range(2)]
        x_rows = sb("x_rows", [P, TILES_PASS, D])
        x = sb("x", [P, KD, 2, TOKENS], R)
        h_full = sb("h_full", [P, FB, TOKENS])
        x_full = h_full
        h = [sb(f"h{i}", [P, FB, 2, TOKENS], R) for i in range(2)]
        y_t = sb("y_t", [P, KD, TOKENS])
        y_out = sb("y_out", [P, 2, D])
        g_ps = [ps(f"g{f}") for f in range(FB)]
        u_ps = [ps(f"u{f}") for f in range(FB)]
        y_ps = [ps(f"y{i}") for i in range(4)]
        x_ps = [g_ps[0], u_ps[0], g_ps[1], u_ps[1]]

        g_loaded, u_loaded, d_loaded, x_loaded, all_stored = (sem(n) for n in ("g_ld", "u_ld", "d_ld", "x_ld", "all_st"))
        y_stored = [sem(f"y_st{i}") for i in range(2)]
        g_rounded, u_rounded, d_rounded = (sem(n) for n in ("g_rnd", "u_rnd", "d_rnd"))
        g_split, u_split, d_split = (sem(n) for n in ("g_spl", "u_spl", "d_spl"))
        x_turned, x_rounded, x_whole, x_split = (sem(n) for n in ("x_t", "x_rnd", "x_wh", "x_spl"))
        g_done, u_done, silu_done, h_whole, h_rounded, h_split = (sem(n) for n in ("g_mm", "u_mm", "silu", "h_wh", "h_rnd", "h_spl"))
        halves_added, y_whole = sem("halves"), sem("y_wh")
        y_done, y_added, y_turned, y_left, y_right = (sem(n) for n in ("y_mm", "y_add", "y_t2", "y_l", "y_r"))
        W0, U0, X0, H0, Y0, A0, T0, O0 = 1, 2 * FB, KD, FB, 2 * KD, 4, KD, TILES_PASS

        block = ctx.enter_context(nc.Block())

        def each_pass(eng, body):
            if table is None:
                for p in range(passes):
                    body(p, None)
                return
            with eng.Fori(0, passes) as p:
                width_no = eng.value_load(table[0:1, 1, bass.ds(p, 1)], min_val=0, max_val=len(WIDTHS))
                with eng.If(width_no > 0):
                    body(p, width_no)
                    eng.nop()

        def each_width(eng, width_no, body):
            if width_no is None:
                body(TOKENS, False)
                return

            def among(first, last):
                if first == last:
                    width = WIDTHS[first - 1]
                    body(width, 2 * width < TOKENS - 2 * ROUND)
                    return
                middle = (first + last) // 2
                with eng.If(width_no <= middle):
                    among(first, middle)
                    eng.nop()
                with eng.If(width_no > middle):
                    among(middle + 1, last)
                    eng.nop()

            among(1, len(WIDTHS))
            eng.nop()

        def has_next(p):
            return table is not None or p + 1 < passes

        def parity(p, c):
            return (c if table is not None else p * C + c) % 2

        def chunk_pairs(eng, p, first, last, body):
            pairs = (last - first + 1) // 2
            with eng.Fori(0, pairs) as i:
                body(2 * i + first, parity(p, first))
                body(2 * i + first + 1, parity(p, first + 1))
            for c in range(first + 2 * pairs, last + 1):
                body(c, parity(p, c))

        @block.sync
        def _(sp):
            def pick(w, expert, lo_row, rows, lo_col, cols):
                if table is None:
                    return w[0, bass.ds(lo_row, rows), bass.ds(lo_col, cols)]
                return w[bass.ds(expert, 1), bass.ds(lo_row, rows), bass.ds(lo_col, cols)].rearrange("a r c -> (a r) c")

            def load_in(p, c, expert):
                n = p * C + c
                sp.wait_ge(g_split, n + W0)
                sp.dma_start(raw_g[:, :, :], pick(gate_w, expert, 0, D, c * CHUNK_FF, CHUNK_FF)
                             .rearrange("(k p) f -> p k f", p=P)).then_inc(g_loaded, 16)
                sp.wait_ge(u_split, n + W0)
                sp.dma_start(raw_u[:, :, :], pick(up_w, expert, 0, D, c * CHUNK_FF, CHUNK_FF)
                             .rearrange("(k p) f -> p k f", p=P)).then_inc(u_loaded, 16)

            def load_down(p, c, expert):
                sp.wait_ge(d_split, p * C + c + W0)
                sp.dma_start(raw_d[:, :, :], pick(down_w, expert, c * CHUNK_FF, CHUNK_FF, 0, D)
                             .rearrange("(b p) d -> p b d", p=P)).then_inc(d_loaded, 16)

            def expert_of(p):
                if table is None:
                    return 0
                return sp.value_load(table[0:1, 0, bass.ds(p, 1)], min_val=0, max_val=gate_w.shape[0] - 1)

            def one_pass(p, _):
                expert = expert_of(p)
                with sp.Fori(1, C) as c:
                    load_in(p, c, expert)
                    load_down(p, c - 1, expert)
                if has_next(p):
                    load_in(p + 1, 0, expert_of(p + 1))
                load_down(p, C - 1, expert)

            if table is None:
                sp.wait_ge(x_loaded, TILES_PASS * 16)
            load_in(0, 0, expert_of(0))
            each_pass(sp, one_pass)

        @block.gpsimd
        def _(pool):
            pool.sem_inc(x_turned, X0)

            def rest_d(p, c, par):
                n = p * C + c
                pool.wait_ge(d_rounded, n + 1)
                pool.tensor_tensor(d_lo[par][:, :, :], raw_d[:, :, :], d_hi[par][:, :, :].bitcast(F), ALU.subtract)\
                    .then_inc(d_split, 1)

            def fetch(p):
                pool.wait_ge(x_turned, p * KD + X0)
                for t in range(TILES_PASS):
                    rows_of(pool, p, t, x_rows[:, t, :]).then_inc(x_loaded, 16)

            def one_pass(p, _):
                if has_next(p):
                    fetch(p + 1)
                chunk_pairs(pool, p, 0, C - 1, lambda c, par: rest_d(p, c, par))

            pool.sem_inc(d_split, W0)
            if prepare:
                prepare(pool)
            fetch(0)
            each_pass(pool, one_pass)

        @block.tensor
        def _(pe):
            pe.sem_inc(u_done, U0)
            pe.sem_inc(y_done, Y0)

            def turn_rows(p, k):
                if k == 0:
                    pe.wait_ge(x_loaded, (p + 1) * TILES_PASS * 16)
                    pe.wait_ge(silu_done, p * C * FB + H0)
                    pe.wait_ge(h_whole, p * C * FB + H0)
                if k >= 4:
                    pe.wait_ge(x_whole, p * KD + k - 3)
                for t in range(TILES_PASS):
                    last = pe.transpose(x_ps[k % 4][:, t * P:(t + 1) * P], x_rows[:, t, k * P:(k + 1) * P],
                                        ident[:, :])
                last.then_inc(x_turned, 1)

            def product(bank, wh, wl, moving, width, narrow, start, stop):
                if narrow:
                    out = bank[:, 0:2 * width].rearrange("p (s w) -> p s w", s=2)
                    pe.matmul(out, wh, moving[:, :, 0:width], start=start, stop=False)
                    return pe.matmul(out, wl, moving[:, :, 0:width], start=False, stop=stop)
                pe.matmul(bank[:, 0:width], wh, moving[:, 0, 0:width], start=start, stop=False)
                pe.matmul(bank[:, 0:width], wh, moving[:, 1, 0:width], start=False, stop=False)
                return pe.matmul(bank[:, 0:width], wl, moving[:, 0, 0:width], start=False, stop=stop)

            def hidden(p, c, par, width, narrow):
                n = p * C + c
                if type(c) is int and c == 0:
                    pe.wait_ge(x_split, (p + 1) * KD + 2)
                for f in range(FB):
                    for bank, w_hi, w_lo, split, freed, done in (
                            (g_ps[f], g_hi[par], g_lo[par], g_split, silu_done, g_done),
                            (u_ps[f], u_hi[par], u_lo[par], u_split, h_whole, u_done)):
                        if f == 0:
                            pe.wait_ge(split, n + W0 + 1)
                        pe.wait_ge(freed, n * FB + f - FB + 1 + H0)
                        for k in range(KD):
                            wh, wl = (w[:, k, f * P:(f + 1) * P] for w in (w_hi, w_lo))
                            last = product(bank, wh, wl, x[:, k, :, :], width, narrow, k == 0, k == KD - 1)
                        last.then_inc(done, 1)

            def down(p, c, par, width, narrow, ready_next=False):
                n = p * C + c
                pe.wait_ge(y_left, p * TILES_PASS + O0)
                pe.wait_ge(y_right, p * TILES_PASS + O0)
                if ready_next:
                    for k in range(4):
                        turn_rows(p + 1, k)
                pe.wait_ge(d_split, n + W0 + 1)
                pe.wait_ge(h_split, (n + 1) * FB + H0)
                for db in range(KD):
                    if ready_next and db < KD - 4:
                        turn_rows(p + 1, db + 4)
                    pe.wait_ge(y_added, n * KD + db - 3 + A0)
                    for f in range(FB):
                        wh, wl = (w[:, f, db * P:(db + 1) * P] for w in (d_hi[par], d_lo[par]))
                        last = product(y_ps[db % 4], wh, wl, h[par][:, f, :, :], width, narrow, f == 0, f == FB - 1)
                    last.then_inc(y_done, 1)

            def turn_result(p, width):
                tiles = -(-width // P)
                pe.wait_ge(y_whole, p + 1)
                for t in range(tiles):
                    if t >= 2:
                        pe.wait_ge(y_left, p * TILES_PASS + t - 1 + O0)
                        pe.wait_ge(y_right, p * TILES_PASS + t - 1 + O0)
                    for half in range(2):
                        bank = y_ps[(2 * t + half) % 4]
                        for j in range(4):
                            last = pe.transpose(bank[:, j * P:(j + 1) * P], y_t[:, 4 * half + j, t * P:(t + 1) * P],
                                                ident[:, :])
                        final = t == tiles - 1 and half == 1
                        last.then_inc(y_turned, KD - (2 * tiles - 1) if final else 1)

            def one_pass(p, width_no):
                def at(width, narrow):
                    hidden(p, 0, parity(p, 0), width, narrow)

                    def step(c, par):
                        hidden(p, c, par, width, narrow)
                        down(p, c - 1, 1 - par, width, narrow)

                    chunk_pairs(pe, p, 1, C - 1, step)
                    down(p, C - 1, parity(p, C - 1), width, narrow, has_next(p))
                    turn_result(p, width)

                each_width(pe, width_no, at)

            for k in range(KD):
                turn_rows(0, k)
            each_pass(pe, one_pass)

        @block.scalar
        def _(act):
            act.sem_inc(silu_done, H0)
            act.sem_inc(y_left, O0)
            for i in range(2):
                act.sem_inc(y_stored[i], 16)

            def round_up(n, par, raw, hi, loaded, rounded, freed, count):
                act.wait_ge(freed, count)
                act.wait_ge(loaded, (n + 1) * 16)
                act.activation(hi[par][:, :, :], raw[:, :, :], ACT.Copy).then_inc(rounded, 1)

            def round_g(p, c, par):
                n = p * C + c
                round_up(n, par, raw_g, g_hi, g_loaded, g_rounded, u_done, (n - 1) * FB + U0)

            def round_u(p, c, par):
                n = p * C + c
                round_up(n, par, raw_u, u_hi, u_loaded, u_rounded, u_done, (n - 1) * FB + U0)

            def round_d(p, c, par):
                n = p * C + c
                round_up(n, par, raw_d, d_hi, d_loaded, d_rounded, y_done, (n - 1) * KD + Y0)

            def silu(p, c, f, width, narrow):
                n = p * C + c
                if narrow:
                    act.wait_ge(halves_added, 2 * (n * FB + f) + 1)
                    gate = h_full[:, f, 0:width]
                else:
                    act.wait_ge(g_done, n * FB + f + 1)
                    act.wait_ge(h_split, n * FB + f - FB + 1 + H0)
                    gate = g_ps[f][:, 0:width]
                act.activation(h_full[:, f, 0:width], gate, ACT.Silu).then_inc(silu_done, 1)

            def round_hidden(p, c, par, f, width):
                n = p * C + c
                act.wait_ge(h_whole, n * FB + f + 1 + H0)
                act.wait_ge(y_done, (n - 1) * KD + Y0)
                act.activation(h[par][:, f, 0, 0:width], h_full[:, f, 0:width], ACT.Copy).then_inc(h_rounded, 1)

            def ready_tokens(p):
                act.wait_ge(u_done, p * C * FB + U0)
                act.wait_ge(h_split, p * C * FB + H0)
                for k in range(KD):
                    act.wait_ge(x_turned, p * KD + k + 1 + X0)
                    act.wait_ge(x_split, p * KD + k - 1 + 2)
                    act.activation(x_full[:, k % 2, :], x_ps[k % 4][:, :], ACT.Identity,
                                   scale=columns[:, 0, k:k + 1], bias=columns[:, 1, k:k + 1]).then_inc(x_whole, 1)
                    act.wait_ge(x_whole, p * KD + k + 1)
                    act.activation(x[:, k, 0, :], x_full[:, k % 2, :], ACT.Copy).then_inc(x_rounded, 1)

            def one_pass(p, width_no):
                def at(width, narrow):
                    def step(c, par, round_next=True):
                        if round_next:
                            round_g(p, c + 1, 1 - par)
                        silu(p, c, 0, width, narrow)
                        if round_next:
                            round_u(p, c + 1, 1 - par)
                        round_hidden(p, c, par, 0, width)
                        silu(p, c, 1, width, narrow)
                        round_hidden(p, c, par, 1, width)
                        round_d(p, c, par)

                    chunk_pairs(act, p, 0, C - 2, step)
                    step(C - 1, parity(p, C - 1), has_next(p))
                    if has_next(p):
                        ready_tokens(p + 1)
                    tiles = -(-width // P)
                    for t in range(TILES_PASS):
                        if t < tiles:
                            act.wait_ge(y_turned, p * KD + 2 * t + 1 + T0)
                            act.wait_ge(y_stored[t % 2], (p * (TILES_PASS // 2) + t // 2 + 1) * 16)
                            act.activation(y_out[:, t % 2, 0:D // 2], y_ps[2 * t % 4][:, :], ACT.Copy)\
                               .then_inc(y_left, TILES_PASS - tiles + 1 if t == tiles - 1 else 1)
                            act.wait_ge(y_left, p * TILES_PASS + t + 1 + O0)
                            act.wait_ge(y_right, p * TILES_PASS + t + 1 + O0)
                            act.dma_start(y_rows(p, t), y_out[:, t % 2, :]).then_inc(y_stored[t % 2], 16)
                        else:
                            act.wait_ge(y_stored[t % 2], (p * (TILES_PASS // 2) + t // 2 + 1) * 16)
                            act.sem_inc(y_stored[t % 2], 16)

                each_width(act, width_no, at)

            if table is None:
                ready_tokens(0)
            round_g(0, 0, 0)
            round_u(0, 0, 0)
            if table is not None:
                ready_tokens(0)

            each_pass(act, one_pass)
            ran = passes if table is None else act.value_load(table[0:1, 0, 15:16], min_val=1, max_val=passes)
            for i in range(2):
                act.wait_ge(y_stored[i], (ran * (TILES_PASS // 2) + 1) * 16)
            act.sem_inc(all_stored, 1)

        @block.vector
        def _(dve):
            if table is not None:
                dve.memset(y_t[:, :, :], 0.0).then_inc(y_added, A0)
                dve.wait_ge(y_added, A0)
            else:
                dve.sem_inc(y_added, A0)
            dve.sem_inc(g_split, W0)
            dve.sem_inc(u_split, W0)
            dve.sem_inc(h_whole, H0)
            dve.sem_inc(h_split, H0)
            dve.sem_inc(x_split, 2)
            dve.sem_inc(y_right, O0)
            dve.sem_inc(y_turned, T0)

            def rest(n, par, raw, hi, lo, rounded, split):
                dve.wait_ge(rounded, n + 1)
                dve.tensor_tensor(lo[par][:, :, :], raw[:, :, :], hi[par][:, :, :].bitcast(F), ALU.subtract).then_inc(split, 1)

            def rest_g(p, c, par):
                rest(p * C + c, par, raw_g, g_hi, g_lo, g_rounded, g_split)

            def rest_u(p, c, par):
                rest(p * C + c, par, raw_u, u_hi, u_lo, u_rounded, u_split)

            def add_halves(to, bank, width):
                dve.reduce_sum(to, bank[:, 0:2 * width].rearrange("p (s w) -> p w s", s=2), AX.X).then_inc(halves_added, 1)

            def add_gate(p, c, f, width):
                n = p * C + c
                dve.wait_ge(g_done, n * FB + f + 1)
                dve.wait_ge(h_split, n * FB + f - FB + 1 + H0)
                add_halves(h_full[:, f, 0:width], g_ps[f], width)

            def add_up(p, c, f, width):
                dve.wait_ge(u_done, (p * C + c) * FB + f + 1 + U0)
                add_halves(h_full[:, f, TOKENS // 2:TOKENS // 2 + width], u_ps[f], width)

            def whole(p, c, f, width, narrow):
                n = p * C + c
                up = u_ps[f][:, 0:width]
                if narrow:
                    up = h_full[:, f, TOKENS // 2:TOKENS // 2 + width]
                    dve.wait_ge(halves_added, 2 * (n * FB + f) + 2)
                dve.wait_ge(silu_done, n * FB + f + 1 + H0)
                dve.wait_ge(u_done, n * FB + f + 1 + U0)
                dve.tensor_tensor(h_full[:, f, 0:width], h_full[:, f, 0:width], up, ALU.mult)\
                   .then_inc(h_whole, 1)

            def rest_hidden(p, c, par, f, width):
                n = p * C + c
                dve.wait_ge(h_rounded, n * FB + f + 1)
                dve.tensor_tensor(h[par][:, f, 1, 0:width], h_full[:, f, 0:width], h[par][:, f, 0, 0:width].bitcast(F),
                                  ALU.subtract).then_inc(h_split, 1)

            def add(p, c, db, cols, first=False):
                n = p * C + c
                dve.wait_ge(y_done, n * KD + db + 1 + Y0)
                gate = columns[:, 2, db:db + 1]
                if first:
                    dve.tensor_scalar(y_t[:, db, 0:cols], y_ps[db % 4][:, 0:cols], gate, None, ALU.mult)\
                       .then_inc(y_added, 1)
                else:
                    dve.wait_ge(y_added, (n - 1) * KD + db + 1 + A0)
                    dve.scalar_tensor_tensor(y_t[:, db, 0:cols], y_ps[db % 4][:, 0:cols], gate,
                                             y_t[:, db, 0:cols], ALU.mult, ALU.add).then_inc(y_added, 1)

            def split_tokens(p, k):
                dve.wait_ge(x_rounded, p * KD + k + 1)
                dve.tensor_tensor(x[:, k, 1, :], x_full[:, k % 2, :], x[:, k, 0, :].bitcast(F),
                                  ALU.subtract).then_inc(x_split, 1)

            def one_pass(p, width_no):
                def at(width, narrow):
                    cols = 2 * width if narrow else width
                    if not narrow and table is not None:
                        dve.sem_inc(halves_added, 2 * C * FB)

                    def step(c, par, share=2, rest_next=True):
                        if narrow:
                            add_gate(p, c, 0, width)
                        if rest_next:
                            rest_g(p, c + 1, 1 - par)
                        if narrow:
                            add_up(p, c, 0, width)
                        whole(p, c, 0, width, narrow)
                        if narrow:
                            add_gate(p, c, 1, width)
                            rest_hidden(p, c, par, 0, width)
                        if rest_next:
                            rest_u(p, c + 1, 1 - par)
                        if narrow:
                            add_up(p, c, 1, width)
                        else:
                            rest_hidden(p, c, par, 0, width)
                        whole(p, c, 1, width, narrow)
                        if share == 1:
                            dve.wait_ge(y_turned, p * KD + T0)
                        if share:
                            for db in range(2):
                                add(p, c - 1, db, cols, share == 1)
                        rest_hidden(p, c, par, 1, width)
                        if share:
                            for db in range(2, KD):
                                add(p, c - 1, db, cols, share == 1)

                    step(0, parity(p, 0), 0)
                    step(1, parity(p, 1), 1)
                    chunk_pairs(dve, p, 2, C - 2, step)
                    step(C - 1, parity(p, C - 1), 2, has_next(p))
                    if has_next(p):
                        split_tokens(p + 1, 0)
                        split_tokens(p + 1, 1)
                    for db in range(KD):
                        if has_next(p) and db + 2 < KD:
                            split_tokens(p + 1, db + 2)
                        add(p, C - 1, db, cols)
                    if narrow:
                        dve.wait_ge(y_added, (p + 1) * C * KD + A0)
                        dve.tensor_tensor(y_t[:, :, 0:width], y_t[:, :, 0:width], y_t[:, :, width:cols], ALU.add)\
                           .then_inc(y_whole, 1)
                    else:
                        dve.wait_ge(y_added, (p + 1) * C * KD + A0)
                        dve.sem_inc(y_whole, 1)
                    tiles = -(-width // P)
                    for t in range(tiles):
                        dve.wait_ge(y_turned, p * KD + 2 * t + 2 + T0)
                        dve.wait_ge(y_stored[t % 2], (p * (TILES_PASS // 2) + t // 2 + 1) * 16)
                        dve.tensor_copy(y_out[:, t % 2, D // 2:D], y_ps[(2 * t + 1) % 4][:, :])\
                           .then_inc(y_right, TILES_PASS - tiles + 1 if t == tiles - 1 else 1)

                each_width(dve, width_no, at)

            if table is not None:
                rest_g(0, 0, 0)
                rest_u(0, 0, 0)
            for k in range(KD):
                split_tokens(0, k)
            if table is None:
                rest_g(0, 0, 0)
                rest_u(0, 0, 0)

            each_pass(dve, one_pass)


def backbone(nc, a, tables, out):
    F, R, I = mybir.dt.float32, mybir.dt.float32r, mybir.dt.int32
    dram = dict(tables)
    for name, shape, dtype in (("pool_mod", [3, D], F), ("x1", [SEQ, D], F), ("x3", [SEQ, D], F), ("xn", [SEQ, D], F),
                               ("y_dense", [SEQ, D], F), ("y", [SLOT_TILES * P, D], F), ("slot_token", [LISTED_TILES * P, 1], I)):
        dram[name] = nc.dram_tensor(f"scratch_{name}", shape, dtype).ap()
    outer = ExitStack()
    with outer:
        outer.enter_context(nc.allow_non_contiguous_dma(reason="small vectors and tables, one number to a partition"))

        def sb(stack, n, s, d=F):
            return stack.enter_context(nc.sbuf_tensor(n, s, d))

        keep = {
            "ident": sb(outer, "ident", [P, P]),
            "ffn_cols": sb(outer, "ffn_cols", [P, 3, KD]),
            "moe_cols": sb(outer, "moe_cols", [P, 3, KD]),
            "weight": sb(outer, "weight", [P, TOP_K, TX]),
            "slot": sb(outer, "slot", [P, TOP_K, TX], I),
            "token_of": sb(outer, "token_of", [P, LISTED_TILES], I),
            "token_now": sb(outer, "token_now", [P, TILES_PASS], I),
            "tokens": sb(outer, "tokens", [P, TX], I),
            "table": sb(outer, "table", [1, 2, MAX_PASSES_PAD], I),
        }
        picked = outer.enter_context(nc.semaphore("picked"))
        scattered = outer.enter_context(nc.semaphore("scattered"))
        listed = outer.enter_context(nc.semaphore("listed"))
        gathered = outer.enter_context(nc.semaphore("gathered"))

        right, right_short, left, tokens_side = ExitStack(), ExitStack(), ExitStack(), ExitStack()
        with left:
            keep["attn_cols"] = left.enter_context(nc.sbuf_tensor("attn_cols", [P, 4, KD], F))
            keep["gate0"] = left.enter_context(nc.sbuf_tensor("gate0", [P, D], F))
            keep["c_silu"] = left.enter_context(nc.sbuf_tensor("c_silu", [P, 2, KD], F))
            with right:
                with tokens_side:
                    for name in ("x_hi", "x_lo"):
                        keep[name] = tokens_side.enter_context(nc.sbuf_tensor(name, [P, KD, SEQ + CTX_LEN], R))
                    modulation_phase(nc, a, dram, keep)
                    for name, shape in (("u", [P, TX, D // 2]), ("v_gm", [P, TX, D // 2]), ("v_sums", [P, TX, 2])):
                        keep[name] = right.enter_context(nc.sbuf_tensor(name, shape, F, side="right"))
                    for name, shape in (("q_t", [P, Q_HEADS // 2, SEQ]), ("k_t", [P, SEQ + CTX_LEN]),
                                        ("v", [P, TX + TC, KV_WIDTH])):
                        keep[name] = right_short.enter_context(nc.sbuf_tensor(name, shape, F, side="right"))
                    projection_phase(nc, a["w_in"], dram, keep)
                keep["att"] = left.enter_context(nc.sbuf_tensor("att", [P, Q_HEADS // 2, SEQ], F))
                with nc.sbuf_tensor("mod_sum", [P, len(REST_VECTORS), D], F) as keep["mod_sum"]:
                    with right_short:
                        attention_phase(nc, a["attn_sink"], a["w_ada"], dram, keep)
                    for name in ("w_out_hi", "w_out_lo"):
                        keep[name] = right.enter_context(nc.sbuf_tensor(name, [P, KD, D], R, side="right"))
                    modulation_rest_phase(nc, a["b_ada"], a["w_out"], dram, keep)
                mixer_output_phase(nc, {"x": a["x"], "w_s": a["gm_w_s"], "b_s": a["gm_b_s"], "gain": a["gm_gain"]}, dram, keep)

        def tile_rows(y):
            return lambda p, t: y[bass.ds((p * TILES_PASS + t) * P, P), :]

        def token_tile(pool, p, t, to):
            return pool.dma_start(to, dram["xn"][(p * TILES_PASS + t) * P:(p * TILES_PASS + t + 1) * P, :])

        expert_mlp_phase(nc, "ffn", (SEQ // TOKENS, FF_DENSE // CHUNK_FF), (a["ffn_w_gate"], a["ffn_w_up"], a["ffn_w_down"]),
                         keep["ffn_cols"], keep["ident"], token_tile, tile_rows(dram["y_dense"]), None)
        pool_phase(nc, a["pool_w"], a["pool_scale"], keep["ident"], dram)
        routing_phase(nc, a["router_w"], dram, keep)

        def list_slots(pool):
            for i in range(TOP_K):
                for t in range(TX):
                    pool.indirect_dma_start(dram["slot_token"], bass.IndirectOffsetOnAxis(ap=keep["slot"][:, i, t:t + 1], axis=0),
                                            keep["tokens"][:, t:t + 1], None).then_inc(scattered, 16)
            pool.wait_ge(scattered, 16 * TOP_K * TX)
            pool.dma_start(keep["token_of"][:, :], dram["slot_token"].rearrange("(c p) o -> p (c o)", p=P)).then_inc(listed, 16)
            pool.wait_ge(listed, 16)

        def slot_tile(pool, p, t, to):
            pool.tensor_copy(keep["token_now"][:, t:t + 1], keep["token_of"][:, bass.ds(p * TILES_PASS + t, 1)]).then_inc(picked, 1)
            pool.wait_ge(picked, p * TILES_PASS + t + 1)
            pool.sem_inc(gathered, 1)
            return pool.indirect_dma_start(to, None, dram["xn"], bass.IndirectOffsetOnAxis(ap=keep["token_now"][:, t:t + 1], axis=0))

        experts = tuple(w.rearrange("a e r c -> (a e) r c") for w in (a["moe_w_gate"], a["moe_w_up"], a["moe_w_down"]))
        expert_mlp_phase(nc, "moe", (MAX_PASSES, FF_EXPERT // CHUNK_FF), experts, keep["moe_cols"], keep["ident"], slot_tile,
                         tile_rows(dram["y"]), keep["table"], list_slots)
        output_phase(nc, a["final_gain"], dram, keep, out)


_INS = ["x", "c", "ctx", "c_ctx", "w_ada", "b_ada", "w_in", "attn_sink", "gm_gain", "gm_w_s", "gm_b_s", "w_out",
        "ffn_w_gate", "ffn_w_up", "ffn_w_down", "pool_w", "pool_scale", "router_w",
        "moe_w_gate", "moe_w_up", "moe_w_down", "final_gain"]


def kernel(**inputs):
    import concourse.bacc as bacc
    from concourse.bass_utils import run_bass_kernel_spmd

    nc = bacc.Bacc("TRN2", target_bir_lowering=False, num_devices=1, dynamic_dma_scratch_size=8192)
    arrays, aps, tables = {}, {}, {}

    def declare(name, a):
        arrays[name] = a
        return nc.dram_tensor(name, a.shape, mybir.dt.from_np(a.dtype), kind="ExternalInput").ap()

    for name in _INS:
        aps[name] = declare(f"in_{name}", np.ascontiguousarray(inputs[name]))
    for name, table in constants().items():
        tables[name] = declare(f"table_{name}", table)
    out = nc.dram_tensor("out", [1, SEQ, D], mybir.dt.float32, kind="ExternalOutput").ap()
    backbone(nc, aps, tables, out)
    r = run_bass_kernel_spmd(nc, [arrays], core_ids=[0])
    return r.results[0]["out"]
```
